# Optimizing a Trainium2 kernel written in Bass

```python
import jax, jax.numpy as jnp
from jax import lax
import numpy as np

D_MODEL = 1024
BATCH = 1
SEQ = 1024
DEPTH = 1

CONV_CH = D_MODEL // 2
CONV_K = 3
N_HEADS = 8
HEAD_DIM = (D_MODEL // 2) // N_HEADS
N_KV_HEADS = 2
GQA = N_HEADS // N_KV_HEADS
N_BRANCH = 3
CMP_BLOCK = 32
CMP_STRIDE = 16
CMP_HIDDEN = 256
SEL_BLOCK = 64
SEL_TOP = 16
WINDOW = 512
Q_BLOCK = 128
D_FF = ((8 * D_MODEL // 3 + 255) // 256) * 256
NORM_EPS = 1e-6

kernel_name = "hymba_conv_nsa_alibi_block"

def _proj_sizes():
    kv = N_KV_HEADS * HEAD_DIM
    return [CONV_CH, CONV_CH, CONV_CH, N_HEADS * HEAD_DIM, kv, kv, kv, kv, kv, kv, N_HEADS * N_BRANCH]

def _split_points():
    return [int(v) for v in np.cumsum(_proj_sizes())[:-1]]

def _rmsnorm(x, g):
    xf = x.astype(jnp.float32)
    y = xf * lax.rsqrt(jnp.mean(xf * xf, axis=-1, keepdims=True) + NORM_EPS)
    return (y * g.astype(jnp.float32)).astype(x.dtype)

def _masked_softmax(s, mask):
    s = jnp.where(mask, s, -jnp.inf)
    m = jnp.max(s, axis=-1, keepdims=True)
    m = jnp.where(jnp.isfinite(m), m, 0.0)
    e = jnp.where(mask, jnp.exp(s - m), 0.0)
    return e / jnp.maximum(jnp.sum(e, axis=-1, keepdims=True), 1e-30)

def _alibi_slopes():
    h = jnp.arange(1, N_HEADS + 1, dtype=jnp.float32)
    return jnp.exp2(-8.0 * h / N_HEADS)

def _short_conv(b_gate, c_gate, h, conv_w):
    u = c_gate * h
    up = jnp.pad(u, ((0, 0), (CONV_K - 1, 0), (0, 0)))
    S = u.shape[1]
    conv = sum(conv_w[i] * up[:, i:i + S] for i in range(CONV_K))
    return b_gate * conv

def _compress(k, pos, w1, w2):
    B, S = k.shape[:2]
    nc = (S - CMP_BLOCK) // CMP_STRIDE + 1
    idx = CMP_STRIDE * jnp.arange(nc)[:, None] + jnp.arange(CMP_BLOCK)[None, :]
    blk = k[:, idx] + pos[None, None, :, None, :]
    blk = blk.transpose(0, 1, 3, 2, 4).reshape(B, nc, N_KV_HEADS, CMP_BLOCK * HEAD_DIM)
    return jax.nn.gelu(blk @ w1) @ w2

def _nsa(q, k_cmp, v_cmp, k_sel, v_sel, k_win, v_win, gates,
         k_cmp_pos, k_cmp_w1, k_cmp_w2, v_cmp_pos, v_cmp_w1, v_cmp_w2):
    B, S = q.shape[:2]
    f32 = jnp.float32
    scale = HEAD_DIM ** -0.5
    slopes = _alibi_slopes().reshape(N_KV_HEADS, GQA)[None, :, :, None, None]

    kc = _compress(k_cmp, k_cmp_pos, k_cmp_w1, k_cmp_w2)
    vc = _compress(v_cmp, v_cmp_pos, v_cmp_w1, v_cmp_w2)
    nc = kc.shape[1]
    c_start = CMP_STRIDE * jnp.arange(nc)
    c_end = c_start + CMP_BLOCK - 1

    n_sel = S // SEL_BLOCK
    n_top = min(SEL_TOP, n_sel)
    s_start = SEL_BLOCK * jnp.arange(n_sel)
    ov = jnp.minimum(c_end[:, None] + 1, s_start[None, :] + SEL_BLOCK) - jnp.maximum(c_start[:, None], s_start[None, :])
    overlap = jnp.clip(ov, 0).astype(f32) / CMP_BLOCK
    ks_blk = k_sel.reshape(B, n_sel, SEL_BLOCK, N_KV_HEADS, HEAD_DIM).transpose(0, 3, 1, 2, 4)
    vs_blk = v_sel.reshape(B, n_sel, SEL_BLOCK, N_KV_HEADS, HEAD_DIM).transpose(0, 3, 1, 2, 4)
    bi = jnp.arange(B)[:, None, None, None]
    ki = jnp.arange(N_KV_HEADS)[None, :, None, None]

    kw_pad = jnp.pad(k_win, ((0, 0), (WINDOW, 0), (0, 0), (0, 0)))
    vw_pad = jnp.pad(v_win, ((0, 0), (WINDOW, 0), (0, 0), (0, 0)))

    nq = S // Q_BLOCK
    qb = q.reshape(B, nq, Q_BLOCK, N_KV_HEADS, GQA, HEAD_DIM).transpose(1, 0, 2, 3, 4, 5)
    gb = gates.reshape(B, nq, Q_BLOCK, N_KV_HEADS, GQA, N_BRANCH).transpose(1, 0, 2, 3, 4, 5)
    starts = jnp.arange(nq, dtype=jnp.int32) * Q_BLOCK

    def block(args):
        qi, gi, q0 = args
        t = q0 + jnp.arange(Q_BLOCK, dtype=jnp.int32)

        dist_c = (t[:, None] - c_end[None, :]).astype(f32)
        s_c = jnp.einsum('bqkgd,bnkd->bkgqn', qi, kc).astype(f32) * scale - slopes * dist_c
        p_c = _masked_softmax(s_c, dist_c >= 0)
        o_c = jnp.einsum('bkgqn,bnkd->bqkgd', p_c.astype(vc.dtype), vc)

        imp = jnp.einsum('bkgqn,nj->bkqj', p_c, overlap)
        jblk = jnp.arange(n_sel)[None, :]
        imp = jnp.where(s_start[None, :] > t[:, None], -jnp.inf, imp)
        forced = (jblk == 0) | (jblk == (t[:, None] // SEL_BLOCK))
        imp = jnp.where(forced, jnp.inf, imp)
        _, idx = lax.top_k(imp, n_top)
        k_g = ks_blk[bi, ki, idx].reshape(B, N_KV_HEADS, Q_BLOCK, n_top * SEL_BLOCK, HEAD_DIM)
        v_g = vs_blk[bi, ki, idx].reshape(B, N_KV_HEADS, Q_BLOCK, n_top * SEL_BLOCK, HEAD_DIM)
        pos = (idx[..., None] * SEL_BLOCK + jnp.arange(SEL_BLOCK)).reshape(B, N_KV_HEADS, Q_BLOCK, n_top * SEL_BLOCK)
        dist_s = (t[None, None, :, None] - pos).astype(f32)[:, :, None]
        s_s = jnp.einsum('bqkgd,bkqmd->bkgqm', qi, k_g).astype(f32) * scale - slopes * dist_s
        p_s = _masked_softmax(s_s, dist_s >= 0)
        o_s = jnp.einsum('bkgqm,bkqmd->bqkgd', p_s.astype(v_g.dtype), v_g)

        kwi = lax.dynamic_slice_in_dim(kw_pad, q0, Q_BLOCK + WINDOW, axis=1)
        vwi = lax.dynamic_slice_in_dim(vw_pad, q0, Q_BLOCK + WINDOW, axis=1)
        kpos = q0 - WINDOW + jnp.arange(Q_BLOCK + WINDOW, dtype=jnp.int32)
        dist_w = t[:, None] - kpos[None, :]
        mask_w = (dist_w >= 0) & (dist_w < WINDOW) & (kpos[None, :] >= 0)
        s_w = jnp.einsum('bqkgd,bskd->bkgqs', qi, kwi).astype(f32) * scale - slopes * dist_w.astype(f32)
        p_w = _masked_softmax(s_w, mask_w)
        o_w = jnp.einsum('bkgqs,bskd->bqkgd', p_w.astype(vwi.dtype), vwi)

        return gi[..., 0:1] * o_c + gi[..., 1:2] * o_s + gi[..., 2:3] * o_w

    out = lax.map(block, (qb, gb, starts))
    return out.transpose(1, 0, 2, 3, 4, 5).reshape(B, S, N_HEADS * HEAD_DIM)

def setup_inputs(seed: int = 0) -> dict:
    key = jax.random.key(seed)
    ks = jax.random.split(key, 20)
    nrm = jax.random.normal
    d_in = sum(_proj_sizes())
    f = jnp.float32
    return {
        "x": nrm(ks[0], (BATCH, SEQ, D_MODEL), f),
        "norm1_g": 1.0 + 0.1 * nrm(ks[1], (DEPTH, D_MODEL), f),
        "w_in": nrm(ks[2], (DEPTH, D_MODEL, d_in), f) * D_MODEL ** -0.5,
        "conv_w": nrm(ks[3], (DEPTH, CONV_K, CONV_CH), f) * CONV_K ** -0.5,
        "k_cmp_pos": 0.1 * nrm(ks[4], (DEPTH, CMP_BLOCK, HEAD_DIM), f),
        "k_cmp_w1": nrm(ks[5], (DEPTH, CMP_BLOCK * HEAD_DIM, CMP_HIDDEN), f) * (CMP_BLOCK * HEAD_DIM) ** -0.5,
        "k_cmp_w2": nrm(ks[6], (DEPTH, CMP_HIDDEN, HEAD_DIM), f) * CMP_HIDDEN ** -0.5,
        "v_cmp_pos": 0.1 * nrm(ks[7], (DEPTH, CMP_BLOCK, HEAD_DIM), f),
        "v_cmp_w1": nrm(ks[8], (DEPTH, CMP_BLOCK * HEAD_DIM, CMP_HIDDEN), f) * (CMP_BLOCK * HEAD_DIM) ** -0.5,
        "v_cmp_w2": nrm(ks[9], (DEPTH, CMP_HIDDEN, HEAD_DIM), f) * CMP_HIDDEN ** -0.5,
        "gn_conv_g": 1.0 + 0.1 * nrm(ks[10], (DEPTH, CONV_CH), f),
        "gn_nsa_g": 1.0 + 0.1 * nrm(ks[11], (DEPTH, N_HEADS * HEAD_DIM), f),
        "w_out": nrm(ks[12], (DEPTH, CONV_CH + N_HEADS * HEAD_DIM, D_MODEL), f) * (CONV_CH + N_HEADS * HEAD_DIM) ** -0.5,
        "norm2_g": 1.0 + 0.1 * nrm(ks[13], (DEPTH, D_MODEL), f),
        "w_gate": nrm(ks[14], (DEPTH, D_MODEL, D_FF), f) * D_MODEL ** -0.5,
        "w_up": nrm(ks[15], (DEPTH, D_MODEL, D_FF), f) * D_MODEL ** -0.5,
        "w_down": nrm(ks[16], (DEPTH, D_FF, D_MODEL), f) * D_FF ** -0.5,
        "norm_f_g": 1.0 + 0.1 * nrm(ks[17], (D_MODEL,), f),
    }

def reference(x, norm1_g, w_in, conv_w, k_cmp_pos, k_cmp_w1, k_cmp_w2, v_cmp_pos, v_cmp_w1, v_cmp_w2,
              gn_conv_g, gn_nsa_g, w_out, norm2_g, w_gate, w_up, w_down, norm_f_g):
    h = x
    B, S, _ = x.shape
    for l in range(DEPTH):
        u = _rmsnorm(h, norm1_g[l])
        proj = u @ w_in[l]
        cb, cc, ch, q, kc, vc, ksl, vsl, kw, vw, g = jnp.split(proj, _split_points(), axis=-1)

        conv_out = _short_conv(cb, cc, ch, conv_w[l])

        kvs = lambda t_: t_.reshape(B, S, N_KV_HEADS, HEAD_DIM)
        qh = q.reshape(B, S, N_KV_HEADS, GQA, HEAD_DIM)
        gates = jax.nn.sigmoid(g.reshape(B, S, N_KV_HEADS, GQA, N_BRANCH))
        nsa_out = _nsa(qh, kvs(kc), kvs(vc), kvs(ksl), kvs(vsl), kvs(kw), kvs(vw), gates,
                       k_cmp_pos[l], k_cmp_w1[l], k_cmp_w2[l], v_cmp_pos[l], v_cmp_w1[l], v_cmp_w2[l])

        mixed = jnp.concatenate([_rmsnorm(conv_out, gn_conv_g[l]), _rmsnorm(nsa_out, gn_nsa_g[l])], axis=-1)
        h = h + mixed @ w_out[l]

        u2 = _rmsnorm(h, norm2_g[l])
        h = h + (jax.nn.silu(u2 @ w_gate[l]) * (u2 @ w_up[l])) @ w_down[l]
    return _rmsnorm(h, norm_f_g)


_drawn_inputs = setup_inputs


def setup_inputs(seed=0):
    import zlib

    import numpy as np

    out = dict(_drawn_inputs(seed))
    spreads = {}
    factors = {'k_cmp_pos': 8.0}
    for name, (base, spread) in spreads.items():
        noise = np.random.default_rng([zlib.crc32(name.encode()), seed]).standard_normal(out[name].shape)
        drawn = base * np.exp(spread * noise) if base else spread * noise
        out[name] = __import__('jax').numpy.asarray(drawn.astype(out[name].dtype))
    for name, factor in factors.items():
        out[name] = (out[name] * factor).astype(out[name].dtype)
    return out
```

```python
from contextlib import ExitStack

import concourse.bass as bass
from concourse import mybir

P = 128
SEQ, DM = 1024, 1024
NT = SEQ // P
KD = DM // P
HALVES, HT = 2, NT // 2
HN = HT * P
CONV = 512
CT = CONV // P
NH, HD, NKV, GQA = 8, 64, 2, 4
CMP_BLOCK, CMP_STRIDE, CMP_HID = 32, 16, 256
NC = (SEQ - CMP_BLOCK) // CMP_STRIDE + 1
NB = NKV * NC
LP = CMP_BLOCK // 2
SEL_BLOCK, SEL_TOP = 64, 16
assert SEQ // SEL_BLOCK <= SEL_TOP
WIN_T = 4
WINDOW = WIN_T * P
DFF = 2816
FT = DFF // P
EPS = 1e-6
NBR = 3
NGATE = NH * NBR

D_IN = 3 * CONV + NH * HD + 6 * NKV * HD + NGATE
Q0 = 3 * CONV
KC0, VC0, KS0, VS0, KW0, VW0 = (Q0 + NH * HD + P * n for n in range(6))
QT = NH * HD // P
FIRST_COLS = [Q0 + P * t for t in range(QT)] + [KS0, KW0, VS0, VW0, KC0, VC0]
N_FIRST = len(FIRST_COLS)
N_IN = N_FIRST + 3 * CT + 1
GATE0 = P - NGATE
ACT_EV = N_FIRST + CT + 1
DVE_EV = N_FIRST + 2 * CT
PIECES = [(0, 8), (8, 8), (16, FT - 16)]
NPC = len(PIECES)
CMP_PC = 4

W_CMP = HALVES * N_IN
W_BACK = W_CMP + 2 * CMP_PC
N_BACK = KD + 2 * FT + NPC * KD

MASKED = -1.0e38
CMP, SEL, WIN = range(NBR)
FLOOR = -1.0e30
SLOTS = 8
UNITS = NT * NKV
CMP_AT = SEQ + WINDOW + P

KiB = 1024


def key_tiles(i):
    j0 = max(0, i - WIN_T)
    sel = [(0, j, P * j) for j in range(i + 1)]
    win = [(1, j, P * (i + 1) + P * (j - j0)) for j in range(j0, i + 1)]
    return sel + win + [(2, 0, P * (i + 1) + P * (i + 1 - j0))]


KTS = [key_tiles(u // NKV) for u in range(UNITS)]
KT_BASE = [sum(len(k) for k in KTS[:u]) for u in range(UNITS + 1)]


ITEMS = 2 * GQA
N_ITEMS = ITEMS * UNITS
BEATS = ITEMS + 2
N_KT = KT_BASE[UNITS]
GROUP_END = [KT_BASE[u] + max(q for q, (b, _, _) in enumerate(KTS[u]) if b == br)
             for u in range(UNITS) for br in range(NBR)]
GROUP_START = [0] + [e + 1 for e in GROUP_END[:-1]]


def beat_tiles(u, b):
    n = len(KTS[u])
    return range(KT_BASE[u] + n * b // BEATS, KT_BASE[u] + n * (b + 1) // BEATS)


def unit_of(kt):
    return max(u for u in range(UNITS) if KT_BASE[u] <= kt)


def rows_of(kt):
    u = unit_of(kt)
    return NC if KTS[u][kt - KT_BASE[u]][0] == 2 else P


def groups_ending(kt):
    return [g for g in range(NBR * UNITS) if GROUP_END[g] == kt]


def hymba_block(nc, x, norm1_g, w_in, conv_w, k_cmp_pos, k_cmp_w1, k_cmp_w2, v_cmp_pos, v_cmp_w1,
                v_cmp_w2, gn_conv_g, gn_nsa_g, w_out, norm2_g, w_gate, w_up, w_down, norm_f_g, out):
    f32, f32r = mybir.dt.float32, mybir.dt.float32r
    ALU = mybir.AluOpType
    ACT = mybir.ActivationFunctionType
    ds = bass.ds

    x, out = x[0], out[0]
    w_in, w_out, w_gate, w_up, w_down = w_in[0], w_out[0], w_gate[0], w_up[0], w_down[0]
    x_t = x.rearrange("(t p) d -> p t d", p=P)
    out_t = out.rearrange("(t p) d -> p t d", p=P)
    w_in_k = w_in.rearrange("(k p) m -> p k m", p=P)
    w_out_k = w_out.rearrange("(k p) m -> p k m", p=P)
    w_gate_k = w_gate.rearrange("(k p) m -> p k m", p=P)
    w_up_k = w_up.rearrange("(k p) m -> p k m", p=P)
    w_down_k = w_down.rearrange("(k p) m -> p k m", p=P)
    w1_k = [w[0].rearrange("(c p) m -> p c m", p=P) for w in (k_cmp_w1, v_cmp_w1)]
    w2_k = [w[0].rearrange("(c p) m -> p c m", p=P) for w in (k_cmp_w2, v_cmp_w2)]
    pos_k = [w[0].rearrange("(c l) d -> (l d) c", l=2) for w in (k_cmp_pos, v_cmp_pos)]

    ctx = ExitStack()
    with ctx:
        origin = (nc.sbuf_base + 31) // 32 * 32
        limit = nc.sbuf_usable_end

        def at(name, offset, shape, dt=f32):
            size = 4
            for n in shape[1:]:
                size *= n
            assert origin + offset + size <= limit, (name, origin + offset + size - limit)
            return nc.alloc_sbuf_tensor_at(name, shape, dt, offset=origin + int(offset))

        def sem(name):
            return ctx.enter_context(nc.semaphore(name))

        place = [0]

        def small(name, shape, dt=f32):
            size = 4
            for n in shape[1:]:
                size *= n
            t = at(name, place[0], shape, dt)
            place[0] += (size + 31) // 32 * 32
            assert place[0] <= 8 * KiB, place[0]
            return t

        ident = small("ident", [P, P])
        fold = small("fold", [P, HD])
        ones = small("ones", [P, P])
        ssq = small("ssq", [P, NT])
        rms = small("rms", [P, NT])
        inv = small("inv", [P, NT])
        gconv = small("gconv", [P, CT])
        taps = small("taps", [P, 3, CT])
        gates = small("gates", [P, NT, NGATE])
        pos = small("pos", [P, 2, LP])
        w2d = small("w2d", [P, 2, 2, 2 * HD])
        qscale = small("qscale", [P, QT])
        kcc = small("kcc", [P, 2, NKV, NC + 1], f32r)
        vcc = small("vcc", [P, NKV, 2 * HD], f32r)
        nmax = small("nmax", [P, SLOTS, NBR])
        rsum = small("rsum", [P, SLOTS, NBR])
        rsafe = small("rsafe", [P, SLOTS, NBR])
        rinv = small("rinv", [P, SLOTS, NBR])
        wgt = small("wgt", [P, SLOTS, NBR])

        convT = at("convT", 8 * KiB, [P, CT, SEQ])
        wraw = at("wraw", 104 * KiB, [P, 2, 1024])
        whi = at("whi", 112 * KiB, [P, 2, 1024], f32r)
        wlo = at("wlo", 120 * KiB, [P, 2, 1024], f32r)
        qs = at("qs", 24 * KiB, [P, NH, SEQ], f32r)
        vs = at("vs", 56 * KiB, [P, 2, NT, NKV, 2 * HD], f32r)
        kT = at("kT", 72 * KiB, [P, 2, 2, SEQ], f32r)
        kcs = at("kcs", 88 * KiB, [P, 2, NKV, SEQ])
        uhi = at("uhi", 128 * KiB, [P, KD, HN], f32r)
        ulo = at("ulo", 144 * KiB, [P, KD, HN], f32r)
        xin = at("xin", 160 * KiB, [P, 2, DM])
        g1b = at("g1b", 168 * KiB, [P, DM])
        qstage = at("qstage", 172 * KiB, [P, 2, 2, HN], f32r)
        vraw = at("vraw", 180 * KiB, [P, 2, HN])
        kcraw = at("kcraw", 184 * KiB, [P, 2, HN])
        graw = at("graw", 188 * KiB, [P, HN])
        ccs = at("ccs", 190 * KiB, [P, HN])
        cacc = at("cacc", 192 * KiB, [P, HN])
        useq = at("useq", 194 * KiB, [P, CT, HN + 2])
        junk1 = at("junk1", 203 * KiB, [P, DM])
        csq = at("csq", 198 * KiB, [P, 2, HN])
        crms = at("crms", 202 * KiB, [P, SEQ])
        ks = at("ks", 128 * KiB, [P, 2, 2, NKV, SEQ], f32r)
        blk = at("blk", 160 * KiB, [P, LP, NB])
        bhi = at("bhi", 168 * KiB, [P, LP, NB], f32r)
        blo = at("blo", 176 * KiB, [P, LP, NB], f32r)
        hid = at("hid", 184 * KiB, [P, 4, CMP_HID])
        hidT = at("hidT", 188 * KiB, [P, 2, NB])
        dsel = at("dsel", 189 * KiB, [P, SEQ])
        dwin = at("dwin", 193 * KiB, [P, WINDOW + P])
        dcmp = at("dcmp", 195.5 * KiB, [P, NT, NC])
        probs = at("probs", 72 * KiB, [P, SLOTS, CMP_AT + HD])
        pthi = at("pthi", 160 * KiB, [P, 2, GQA * P], f32r)
        ptlo = at("ptlo", 164 * KiB, [P, 2, GQA * P], f32r)
        osb = at("osb", 168 * KiB, [P, 2, GQA * P])
        parts = at("parts", 198 * KiB, [P, 2, NBR, GQA * HD])
        nsa = at("nsa", 172 * KiB, [P, NT, NH * HD])
        hhi = at("hhi", 24 * KiB, [P, FT, HN], f32r)
        hlo = at("hlo", 128 * KiB, [P, FT, HN], f32r)
        vhi = at("vhi", 68 * KiB, [P, KD, HN], f32r)
        vlo = at("vlo", 84 * KiB, [P, KD, HN], f32r)
        yT = at("yT", 100 * KiB, [P, 2, HN])
        res = at("res", 188 * KiB, [P, HT, DM])
        mhi = at("mhi", 24 * KiB, [P, KD, HN], f32r)
        gvec = at("gvec", 40 * KiB, [P, DM])
        nrm = at("nrm", 44 * KiB, [P, 2, DM])
        junk2 = at("junk2", 52 * KiB, [P, DM])
        mlo = at("mlo", 128 * KiB, [P, KD, HN], f32r)
        silu = yT
        psum = ctx.enter_context(nc.psum_tensor("psum", [P, 8, 512], f32))

        w_in_sem = [sem("w_arrived0"), sem("w_arrived1")]
        w_hi = sem("w_hi")
        w_lo = sem("w_lo")
        w_used = sem("w_used")
        consts = sem("consts")
        vecs = sem("vecs")
        x_in = [sem("x_in0"), sem("x_in1")]
        x_sq = sem("x_sq")
        x_ms = sem("x_ms")
        x_n = sem("x_n")
        tr = sem("tr")
        tr_hi = sem("tr_hi")
        tr_lo = sem("tr_lo")
        act_ev = sem("act_ev")
        dve_ev = sem("dve_ev")
        q_out = [sem("q_out0"), sem("q_out1")]
        kc_out = [sem("kc_out0"), sem("kc_out1")]
        ks_out = sem("ks_out")
        vt = sem("vt")
        vt_hi = sem("vt_hi")
        vt_lo = sem("vt_lo")
        gexp = sem("gexp")
        own = sem("own")
        pool_own = sem("pool_own")
        c_sq = sem("c_sq")
        c_ss = sem("c_ss")
        c_ms = sem("c_ms")
        c_rt = sem("c_rt")
        c_done = sem("c_done")
        b_raw = sem("b_raw")
        b_hi = sem("b_hi")
        b_lo = sem("b_lo")
        h0 = sem("h0")
        h1 = sem("h1")
        h2 = sem("h2")
        h3 = sem("h3")
        h4 = sem("h4")
        h5 = sem("h5")
        m2 = sem("m2")
        cc_hi = sem("cc_hi")
        cc_lo = sem("cc_lo")
        qk_sel = sem("qk_sel")
        qk_wc = sem("qk_wc")
        sel_read = sem("sel_read")
        wc_read = sem("wc_read")
        exped = sem("exped")
        pt = sem("pt")
        pt_hi = sem("pt_hi")
        pt_lo = sem("pt_lo")
        pv = sem("pv")
        o_sb = sem("o_sb")
        o_tok = sem("o_tok")
        o_part = sem("o_part")
        o_done = sem("o_done")
        res_in = sem("res_in")
        gv_in = sem("gv_in")
        s_sq = sem("s_sq")
        s_ms = sem("s_ms")
        s_n = sem("s_n")
        cm_hi = sem("cm_hi")
        cm_lo = sem("cm_lo")
        y_sb = sem("y_sb")
        y_tr = sem("y_tr")
        y_add = sem("y_add")
        sil = sem("sil")
        glu = sem("glu")
        g_hi = sem("g_hi")
        g_lo = sem("g_lo")
        fin = sem("fin")
        stored = sem("stored")

        block = ctx.enter_context(nc.Block())

        def raw(ap):
            return ap.bitcast(f32)

        def slot(w):
            return w % 2

        def w_of(hf, stage):
            return W_BACK + N_BACK * hf + {"out": 0, "glu": KD, "down": KD + 2 * FT}[stage]

        @block.sync
        def _(sp):
            def load_w(w, par, src, cols=1024):
                sp.wait_ge(w_lo, w - 1)
                sp.dma_start(wraw[:, par, 0:cols].rearrange("p (k m) -> p k m", m=src.shape[2]), src)\
                    .then_inc(w_in_sem[par], 16)

            def cols_of(k):
                if k < N_FIRST:
                    return FIRST_COLS[k]
                if k == N_IN - 1:
                    return D_IN - P
                c, n = divmod(k - N_FIRST, 3)
                return P * c + (CONV, 2 * CONV, 0)[n]

            sp.dma_start(xin[:, 0, :], x_t[:, 0, :]).then_inc(x_in[0], 16)
            sp.dma_start(xin[:, 1, :], x_t[:, 1, :]).then_inc(x_in[1], 16)
            sp.dma_start(g1b[:, :], norm1_g[0].partition_broadcast(P)).then_inc(vecs, 16)
            for w in range(2):
                sp.dma_start(wraw[:, w, :].rearrange("p (k m) -> p k m", m=P),
                             w_in_k[:, :, cols_of(w):cols_of(w) + P]).then_inc(w_in_sem[w], 16)
            for t in range(2, HT):
                sp.wait_ge(x_n, t - 1)
                sp.wait_ge(tr, 2 * (t - 1))
                sp.dma_start(xin[:, t % 2, :], x_t[:, t, :]).then_inc(x_in[t % 2], 16)
            with nc.allow_non_contiguous_dma(reason="small parameters, once"):
                sp.dma_start(gconv[:, :], gn_conv_g[0].rearrange("(c p) -> p c", p=P)).then_inc(vecs, 16)
                for n in range(3):
                    sp.dma_start(taps[:, n, :], conv_w[0, n].rearrange("(c p) -> p c", p=P)).then_inc(vecs, 16)
                for n in range(2):
                    sp.dma_start(pos[:, n, :], pos_k[n]).then_inc(vecs, 16)
                    for d in range(2):
                        sp.dma_start(w2d[:, n, :, d * HD:(d + 1) * HD], w2_k[n]).then_inc(vecs, 16)

            def stage_out(hf, k):
                w = N_IN * hf + k
                tok = HN * hf
                if k < QT:
                    sp.wait_ge(act_ev, ACT_EV * hf + k + 1)
                    sp.wait_ge(dve_ev, DVE_EV * hf + k + 1)
                    for r in range(2):
                        for part in range(2):
                            sp.dma_start(raw(qs[HD * part:HD * (part + 1), 2 * k + r, tok:tok + HN]),
                                         raw(qstage[HD * r:HD * (r + 1), k % 2, part, :])).then_inc(q_out[k % 2], 16)
                elif k in (8, 9):
                    n = k - 8
                    sp.wait_ge(act_ev, ACT_EV * hf + k + 1)
                    sp.wait_ge(dve_ev, DVE_EV * hf + k + 1)
                    for g in range(NKV):
                        src = kcraw[HD * g:HD * (g + 1), n, :]
                        sp.dma_start(kcs[0:HD, n, g, tok:tok + HN], src).then_inc(kc_out[n], 16)
                        skip = 1 - hf
                        sp.dma_start(kcs[HD:P, n, g, tok - 1 + skip:tok - 1 + HN], src[:, skip:HN])\
                            .then_inc(kc_out[n], 16)

            for hf in range(HALVES):
                for k in range(N_IN):
                    w = N_IN * hf + k
                    if w >= 2:
                        load_w(w, slot(w), w_in_k[:, :, cols_of(k):cols_of(k) + P])
                    if (hf, k) in ((0, 18), (0, 19), (1, 1), (1, 2)):
                        t = HT + k - 18 if hf == 0 else HT + 1 + k
                        sp.wait_ge(tr, 2 * (t - 1))
                        sp.dma_start(xin[:, t % 2, :], x_t[:, t, :]).then_inc(x_in[t % 2], 16)
                    if k >= 2:
                        stage_out(hf, k - 2)

            sp.wait_ge(w_used, HALVES * N_IN)
            sp.wait_ge(act_ev, ACT_EV * HALVES - 1)
            sp.wait_ge(dve_ev, DVE_EV * HALVES)
            for br in range(2):
                for part in range(2):
                    for g in range(NKV):
                        for d in range(2):
                            sp.dma_start(raw(ks[HD * d:HD * (d + 1), br, part, g, :]),
                                         raw(kT[HD * g:HD * (g + 1), br, part, :])).then_inc(ks_out, 16)

            for n in range(2):
                for pc in range(CMP_PC):
                    w = W_CMP + CMP_PC * n + pc
                    load_w(w, slot(w), w1_k[n][:, 4 * pc:4 * pc + 4, :])

            sp.wait_ge(pt, KT_BASE[UNITS])
            for hf in range(HALVES):
                if hf:
                    sp.wait_ge(stored, 16 * HT * hf)
                else:
                    sp.wait_ge(o_done, UNITS)
                    sp.wait_ge(sel_read, UNITS * GQA)
                    sp.wait_ge(wc_read, UNITS * GQA)
                sp.dma_start(res[:, :, :], x_t[:, HT * hf:HT * (hf + 1), :]).then_inc(res_in, 16)
                sp.dma_start(gvec[:, 0:NH * HD], gn_nsa_g[0].partition_broadcast(P)).then_inc(gv_in, 16)
                w0 = w_of(hf, "out")
                for m in range(2):
                    load_w(w0 + m, slot(w0 + m), w_out_k[:, :, P * m:P * (m + 1)])
                with sp.Fori(1, KD // 2) as mm:
                    for d in range(2):
                        load_w(mm * 2 + (w0 + d), slot(w0 + d), w_out_k[:, :, ds(mm * (2 * P) + P * d, P)])
                w0 = w_of(hf, "glu")
                for d, src in enumerate((w_gate_k, w_up_k)):
                    load_w(w0 + d, slot(w0 + d), src[:, :, 0:P])
                sp.wait_ge(s_n, 2 * HT * hf + HT)
                sp.dma_start(gvec[:, :], norm2_g[0].partition_broadcast(P)).then_inc(gv_in, 16)
                with sp.Fori(1, FT) as f:
                    for d, src in enumerate((w_gate_k, w_up_k)):
                        load_w(f * 2 + (w0 + d), slot(w0 + d), src[:, :, ds(f * P, P)])
                w0 = w_of(hf, "down")
                with sp.Fori(0, KD // 2) as mm:
                    for e in range(2):
                        for n, (k0, nk) in enumerate(PIECES):
                            d = NPC * e + n
                            load_w(mm * (2 * NPC) + (w0 + d), slot(w0 + d),
                                   w_down_k[:, k0:k0 + nk, ds(mm * (2 * P) + P * e, P)], nk * P)
                sp.wait_ge(w_used, w0 + NPC * KD)
                sp.dma_start(gvec[:, :], norm_f_g.partition_broadcast(P)).then_inc(gv_in, 16)
                for t in range(HT):
                    sp.wait_ge(fin, HT * hf + t + 1)
                    sp.dma_start(out_t[:, HT * hf + t, :], res[:, t, :]).then_inc(stored, 16)
            sp.wait_ge(stored, 16 * NT)

        @block.gpsimd
        def _(pool):
            def w_lo_of(w, par, cols=1024):
                pool.wait_ge(w_hi, w + 1)
                pool.tensor_tensor(wlo[:, par, 0:cols], wraw[:, par, 0:cols], raw(whi[:, par, 0:cols]),
                                   ALU.subtract).then_inc(w_lo, 1)

            pool.memset(ident[:, :], 0.0).then_inc(pool_own, 1)
            pool.memset(fold[:, :], 0.0).then_inc(pool_own, 1)
            pool.memset(ones[:, :], 1.0).then_inc(consts, 1)
            pool.memset(raw(kcc[:, :, :, :]), 0.0).then_inc(consts, 1)
            for c in range(CT):
                pool.memset(useq[:, c, 0:2], 0.0).then_inc(consts, 1)
            pool.wait_ge(pool_own, 2)
            pool.affine_select(out=ident[:, :], in_=ident[:, :], compare_op=ALU.not_equal, fill=1.0, base=0,
                               pattern=[[-1, P]], channel_multiplier=1).then_inc(consts, 1)
            pool.affine_select(out=fold[:, :], in_=fold[:, :], compare_op=ALU.not_equal, fill=1.0, base=0,
                               pattern=[[-1, HD]], channel_multiplier=1).then_inc(pool_own, 1)
            pool.wait_ge(pool_own, 3)
            pool.affine_select(out=fold[:, :], in_=fold[:, :], compare_op=ALU.not_equal, fill=1.0, base=-HD,
                               pattern=[[-1, HD]], channel_multiplier=1).then_inc(consts, 1)

            assert HALVES * N_IN % 2 == 0
            with pool.Fori(0, HALVES * N_IN, 2) as w:
                for d in range(2):
                    w_lo_of(w + d, d)

            pool.wait_ge(act_ev, ACT_EV * HALVES)
            pool.wait_ge(dve_ev, DVE_EV * HALVES)
            pool.wait_ge(vt, 3 * HALVES)
            pool.wait_ge(kc_out[0], 64 * HALVES)
            pool.wait_ge(kc_out[1], 64 * HALVES)
            pool.iota(dsel[:, :], pattern=[[1, SEQ]], base=P - SEQ, channel_multiplier=-1,
                      allow_small_or_imprecise_dtypes=True).then_inc(pool_own, 1)
            pool.iota(dwin[:, :], pattern=[[1, WINDOW + P]], base=-WINDOW, channel_multiplier=-1,
                      allow_small_or_imprecise_dtypes=True).then_inc(pool_own, 1)
            pool.iota(dcmp[:, :, :], pattern=[[-P, NT], [CMP_STRIDE, NC]], base=CMP_BLOCK - 1,
                      channel_multiplier=-1, allow_small_or_imprecise_dtypes=True).then_inc(pool_own, 1)
            pool.wait_ge(pool_own, 6)
            pool.affine_select(out=dsel[:, :], in_=dsel[:, :], compare_op=ALU.is_ge, fill=MASKED,
                               base=SEQ - P, pattern=[[-1, SEQ]], channel_multiplier=1).then_inc(consts, 1)
            pool.affine_select(out=dwin[:, :], in_=dwin[:, :], compare_op=ALU.is_ge, fill=MASKED,
                               base=WINDOW, pattern=[[-1, WINDOW + P]], channel_multiplier=1).then_inc(pool_own, 1)
            pool.affine_select(out=dcmp[:, :, :], in_=dcmp[:, :, :], compare_op=ALU.is_ge, fill=MASKED,
                               base=1 - CMP_BLOCK, pattern=[[P, NT], [-CMP_STRIDE, NC]],
                               channel_multiplier=1).then_inc(consts, 1)
            pool.wait_ge(pool_own, 7)
            pool.affine_select(out=dwin[:, :], in_=dwin[:, :], compare_op=ALU.is_ge, fill=MASKED,
                               base=-1, pattern=[[1, WINDOW + P]], channel_multiplier=-1).then_inc(consts, 1)

            for w in range(W_CMP, W_BACK):
                w_lo_of(w, slot(w))

            for u in range(UNITS):
                i, g = divmod(u, NKV)
                o = nsa[:, i, GQA * HD * g:GQA * HD * (g + 1)]
                pool.wait_ge(o_part, NBR * (u + 1))
                pool.tensor_tensor(o, parts[:, u % 2, 2, :], parts[:, u % 2, 0, :], ALU.add).then_inc(pool_own, 1)
                pool.wait_ge(pool_own, 8 + u)
                pool.tensor_tensor(o, o, parts[:, u % 2, 1, :], ALU.add).then_inc(o_done, 1)

            for hf in range(HALVES):
                w0 = w_of(hf, "out")
                for c in range(CT):
                    pool.wait_ge(cm_hi, CT * hf + c + 1)
                    pool.tensor_tensor(mlo[:, c, :], convT[:, c, HN * hf:HN * (hf + 1)], raw(mhi[:, c, :]),
                                       ALU.subtract).then_inc(cm_lo, 1)
                with pool.Fori(0, KD + 2 * FT, 2) as k:
                    for d in range(2):
                        w_lo_of(k + (w0 + d), slot(w0 + d))
                w0 = w_of(hf, "down")
                with pool.Fori(0, KD // 2) as mm:
                    for e in range(2):
                        for n, (_, nk) in enumerate(PIECES):
                            d = NPC * e + n
                            w_lo_of(mm * (2 * NPC) + (w0 + d), slot(w0 + d), nk * P)

        @block.scalar
        def _(act):
            def w_hi_of(w, par, pairs, cols=1024):
                act.wait_ge(w_in_sem[par], pairs * 16)
                act.activation(whi[:, par, 0:cols], wraw[:, par, 0:cols], ACT.Copy).then_inc(w_hi, 1)

            def next_w(w, pairs, cols=1024, par=None):
                act.wait_ge(w_used, w - 1)
                w_hi_of(w, slot(w) if par is None else par, pairs, cols)

            def norm_tile(hf, t, n):
                act.wait_ge(x_in[n % 2], 16 * (n // 2 + 1))
                act.activation(junk1[:, :], xin[:, n % 2, :], ACT.Square, accum_out=ssq[:, n:n + 1])\
                    .then_inc(x_sq, 1)
                act.wait_ge(x_ms, 2 * n + 1)
                act.activation(rms[:, n:n + 1], ssq[:, n:n + 1], ACT.Sqrt).then_inc(x_sq, 1)

            def norm_hi(t, n):
                for b in range(2):
                    act.wait_ge(tr, 2 * n + b + 1)
                    act.activation(uhi[:, 4 * b:4 * b + 4, P * t:P * (t + 1)],
                                   psum[:, 2 * (n % 2) + b, :].rearrange("p (k m) -> p k m", m=P),
                                   ACT.Copy).then_inc(tr_hi, 1)

            w_hi_of(0, 0, 1)
            act.wait_ge(own, NH)
            for hf in range(HALVES):
                if hf:
                    act.wait_ge(w_used, N_IN * hf)
                for t in range(HT):
                    n = HT * hf + t
                    if n:
                        act.wait_ge(x_sq, 2 * n)
                    norm_tile(hf, t, n)
                    if t:
                        norm_hi(t - 1, n - 1)
                norm_hi(HT - 1, HT * hf + HT - 1)

                w0, e0, tok = N_IN * hf, ACT_EV * hf, HN * hf
                for k in range(QT):
                    w = w0 + k
                    next_w(w + 1, (w + 1) // 2 + 1)
                    act.wait_ge(w_used, w + 1)
                    uses = 2 * hf + k // 2
                    if uses:
                        act.wait_ge(q_out[k % 2], 64 * uses)
                    act.activation(qstage[:, k % 2, 0, :], psum[:, 4 + slot(w), :], ACT.Copy,
                                   scale=qscale[:, k:k + 1]).then_inc(act_ev, 1)
                for k in range(QT, QT + 2):
                    w = w0 + k
                    next_w(w + 1, (w + 1) // 2 + 1)
                    act.wait_ge(w_used, w + 1)
                    act.activation(kT[:, k - QT, 0, tok:tok + HN], psum[:, 4 + slot(w), :],
                                   ACT.Copy).then_inc(act_ev, 1)
                for k in range(QT + 2, N_FIRST):
                    w = w0 + k
                    next_w(w + 1, (w + 1) // 2 + 1)
                    act.wait_ge(w_used, w + 1)
                    dst = vraw if k < QT + 4 else kcraw
                    if hf and k >= QT + 4:
                        act.wait_ge(kc_out[k % 2], 64)
                    act.activation(dst[0:HD, k % 2, :], psum[0:HD, 4 + slot(w), :],
                                   ACT.Copy).then_inc(act_ev, 1)
                for c in range(CT):
                    for n in range(3):
                        w = w0 + N_FIRST + 3 * c + n
                        next_w(w + 1, (w + 1) // 2 + 1)
                        if n == 0:
                            act.wait_ge(w_used, w + 1)
                            act.wait_ge(dve_ev, DVE_EV * hf + N_FIRST + 2 * c)
                            act.activation(ccs[:, :], psum[:, 4 + slot(w), :], ACT.Copy).then_inc(act_ev, 1)
                w = w0 + N_IN - 1
                if w + 1 < W_BACK:
                    next_w(w + 1, (w + 1) // 2 + 1)
                act.wait_ge(w_used, w + 1)
                act.activation(graw[:, :], psum[:, 4 + slot(w), :], ACT.Copy).then_inc(act_ev, 1)

                for br in range(2):
                    act.wait_ge(vt, 3 * hf + br + 1)
                    act.activation(vs[:, br, HT * hf:HT * (hf + 1), :, 0:HD],
                                   psum[:, 6 + br, :].rearrange("p (t g d) -> p t g d", t=HT, g=NKV),
                                   ACT.Copy).then_inc(vt_hi, 1)
                act.wait_ge(vt, 3 * hf + 3)
                act.activation(gates[:, HT * hf:HT * (hf + 1), :],
                               psum[:, 6, :].rearrange("p (t m) -> p t m", m=P)[:, :, GATE0:P],
                               ACT.Exp, scale=-1.0).then_inc(gexp, 1)

            act.wait_ge(dve_ev, DVE_EV * HALVES)
            for n in range(HALVES * CT):
                hf, c = divmod(n, CT)
                if n >= 2:
                    act.wait_ge(c_ss, n - 1)
                act.activation(csq[:, n % 2, :], convT[:, c, HN * hf:HN * (hf + 1)], ACT.Square)\
                    .then_inc(c_sq, 1)
            for hf in range(HALVES):
                act.wait_ge(c_ms, hf + 1)
                act.activation(crms[:, HN * hf:HN * (hf + 1)], crms[:, HN * hf:HN * (hf + 1)], ACT.Sqrt)\
                    .then_inc(c_rt, 1)

            for n in range(2):
                act.wait_ge(b_raw, n + 1)
                if n:
                    act.wait_ge(w_used, W_CMP + CMP_PC)
                act.activation(bhi[:, :, :], blk[:, :, :], ACT.Copy).then_inc(b_hi, 1)
                for pc in range(CMP_PC):
                    w = W_CMP + CMP_PC * n + pc
                    if w + 1 < W_BACK:
                        next_w(w + 1, (w + 1) // 2 + 1)
                act.wait_ge(w_used, W_CMP + CMP_PC * (n + 1))
                act.activation(hid[0:NB, 0, :], psum[0:NB, n, 0:CMP_HID], ACT.Copy).then_inc(h0, 1)
                act.wait_ge(h1, n + 1)
                act.activation(hid[0:NB, 2, :], hid[0:NB, 1, :], ACT.Tanh, scale=(2 / 3.141592653589793) ** 0.5)\
                    .then_inc(h2, 1)
                act.wait_ge(h4, n + 1)
                act.activation(hidT[:, :, :], psum[:, 2, 0:2 * NB].rearrange("p (t m) -> p t m", t=2),
                               ACT.Copy, scale=0.5).then_inc(h5, 1)
                act.wait_ge(m2, n + 1)
                if n == 0:
                    act.activation(kcc[:, 0, :, 0:NC], psum[:, 3, 0:NB].rearrange("p (g m) -> p g m", g=NKV),
                                   ACT.Copy).then_inc(cc_hi, 1)
                else:
                    act.activation(vcc[0:NC, :, 0:HD],
                                   psum[0:NC, 3, 0:P].rearrange("p (g d) -> p g d", g=NKV),
                                   ACT.Copy).then_inc(cc_hi, 1)

            def exp_item(m):
                n, wc = divmod(m, 2)
                i, s = n // GQA // NKV, n % SLOTS
                n_sel, n_win = P * (i + 1), P * min(i + 1, WIN_T + 1)
                act.wait_ge(wc_read if wc else sel_read, n + 1)
                cols = ((WIN, n_sel, n_win), (CMP, n_sel + n_win, NC)) if wc else ((SEL, 0, n_sel),)
                for br, c0, cn in cols:
                    ins = act.activation(probs[:, s, c0:c0 + cn], probs[:, s, c0:c0 + cn], ACT.Exp, scale=-1.0,
                                         bias=nmax[:, s, br:br + 1], accum_out=rsum[:, s, br:br + 1])
                ins.then_inc(exped, 1)

            def outputs(g):
                act.wait_ge(pv, GROUP_END[g] + 1)
                act.activation(osb[:, g % 2, :], psum[:, 6 + g % 2, :], ACT.Copy).then_inc(o_sb, 1)

            def hi_tile(kt):
                rows = rows_of(kt)
                act.wait_ge(pt, kt + 1)
                if kt >= 2:
                    act.wait_ge(pv, kt - 1)
                act.activation(pthi[0:rows, kt % 2, :], psum[0:rows, 4 + kt % 2, :], ACT.Copy)\
                    .then_inc(pt_hi, 1)
                for g in groups_ending(kt - 1):
                    outputs(g)

            for m in range(ITEMS):
                exp_item(m)
            for u in range(UNITS):
                for b in range(BEATS):
                    for kt in beat_tiles(u, b):
                        hi_tile(kt)
                    if b < ITEMS and u + 1 < UNITS:
                        exp_item(ITEMS * (u + 1) + b)
            for g in groups_ending(N_KT - 1):
                outputs(g)

            def half_rms(n, src, width):
                for t in range(HT):
                    if n or t:
                        act.wait_ge(s_sq, (HT + 1) * n + t)
                    act.activation(junk2[:, 0:width], src(t), ACT.Square, accum_out=ssq[:, t:t + 1])\
                        .then_inc(s_sq, 1)
                act.wait_ge(s_ms, 2 * n + 1)
                act.activation(rms[:, 0:HT], ssq[:, 0:HT], ACT.Sqrt).then_inc(s_sq, 1)

            for hf in range(HALVES):
                act.wait_ge(o_done, UNITS)
                half_rms(3 * hf, lambda t: nsa[:, HT * hf + t, :], NH * HD)
                w0 = w_of(hf, "out")
                next_w(w0, w0 // 2 + 1)
                for c in range(CT):
                    act.activation(mhi[:, c, :], convT[:, c, HN * hf:HN * (hf + 1)], ACT.Copy)\
                        .then_inc(cm_hi, 1)
                for t in range(HT):
                    n = TR_BASE(hf) + t
                    act.wait_ge(tr, n + 1)
                    act.activation(mhi[:, CT:KD, P * t:P * (t + 1)],
                                   psum[:, t % 2, :].rearrange("p (k m) -> p k m", m=P),
                                   ACT.Copy).then_inc(tr_hi, 1)

                def copy_y(n, par, bank):
                    act.wait_ge(y_tr, n - 1)
                    act.activation(yT[:, par, :], psum[:, bank, :], ACT.Copy).then_inc(y_sb, 1)

                y0 = 2 * KD * hf
                for m in range(2):
                    next_w(w0 + m + 1, (w0 + m + 1) // 2 + 1)
                    act.wait_ge(w_used, w0 + m + 1)
                    if y0 + m >= 2:
                        act.wait_ge(y_tr, y0 + m - 1)
                    act.activation(yT[:, m, :], psum[:, 4 + m, :], ACT.Copy).then_inc(y_sb, 1)
                with act.Fori(1, KD // 2) as mm:
                    for d in range(2):
                        nw = w0 + d + 1
                        act.wait_ge(w_used, mm * 2 + (nw - 1))
                        w_hi_of(mm * 2 + nw, slot(nw), mm + (nw // 2 + 1))
                        act.wait_ge(w_used, mm * 2 + (w0 + d + 1))
                        copy_y(mm * 2 + (y0 + d), d, 4 + d)

                act.wait_ge(y_add, y0 + KD)
                half_rms(3 * hf + 1, lambda t: res[:, t, :], DM)
                for t in range(HT):
                    for b in range(2):
                        n = TR_BASE(hf) + HT + 2 * t + b
                        act.wait_ge(tr, n + 1)
                        act.activation(vhi[:, 4 * b:4 * b + 4, P * t:P * (t + 1)],
                                       psum[:, 2 * (t % 2) + b, :].rearrange("p (k m) -> p k m", m=P),
                                       ACT.Copy).then_inc(tr_hi, 1)

                w0, f0 = w_of(hf, "glu"), FT * hf

                def silu_of(f, par):
                    act.activation(silu[:, par, :], psum[:, 2 * par, :], ACT.Silu).then_inc(sil, 1)

                def glu_step(f, par, first):
                    a = w0 + 1
                    act.wait_ge(w_used, f * 2 + (a - 1))
                    w_hi_of(f * 2 + a, slot(a), f + (a // 2 + 1))
                    if not first:
                        silu_of(f - 1, 1 - par)
                    b = w0 + 2
                    act.wait_ge(w_used, f * 2 + (b - 1))
                    w_hi_of(f * 2 + b, slot(b), f + (b // 2 + 1))
                    if not first:
                        act.wait_ge(glu, f + f0)
                        act.activation(hhi[:, ds(f - 1, 1), :],
                                       silu[:, 1 - par:2 - par, :], ACT.Copy).then_inc(g_hi, 1)

                glu_step(0, 0, True)
                glu_step(1, 1, False)
                with act.Fori(2, FT, 2) as f:
                    for d in range(2):
                        act.wait_ge(g_lo, f + (f0 + d - 2))
                        glu_step(f + d, d, False)
                act.wait_ge(w_used, w0 + 2 * FT)
                act.wait_ge(g_lo, f0 + FT - 2)
                silu_of(FT - 1, 1)
                act.wait_ge(glu, f0 + FT)
                act.activation(hhi[:, FT - 1, :], silu[:, 1, :], ACT.Copy).then_inc(g_hi, 1)

                w0, y0 = w_of(hf, "down"), KD * (2 * hf + 1)
                act.wait_ge(g_lo, f0 + FT)
                last_w = w0 + NPC * KD - 1
                with act.Fori(0, KD // 2 - 1) as mm:
                    for e in range(2):
                        for n in range(NPC):
                            d = NPC * e + n + 1
                            nk = PIECES[(n + 1) % NPC][1]
                            act.wait_ge(w_used, mm * (2 * NPC) + (w0 + d - 1))
                            w_hi_of(mm * (2 * NPC) + (w0 + d), slot(w0 + d), mm * NPC + ((w0 + d) // 2 + 1), nk * P)
                        act.wait_ge(w_used, mm * (2 * NPC) + (w0 + NPC * (e + 1)))
                        copy_y(mm * 2 + (y0 + e), e, 4 + e)
                for e in range(2):
                    for n in range(NPC):
                        w = w0 + NPC * (KD - 2 + e) + n + 1
                        if w <= last_w:
                            next_w(w, w // 2 + 1, PIECES[(n + 1) % NPC][1] * P)
                    act.wait_ge(w_used, w0 + NPC * (KD - 2 + e + 1))
                    copy_y(y0 + KD - 2 + e, e, 4 + e)
                act.wait_ge(y_add, y0 + KD)
                half_rms(3 * hf + 2, lambda t: res[:, t, :], DM)

        @block.tensor
        def _(pe):
            def mm3(bank_ap, w_ap_hi, w_ap_lo, x_hi, x_lo, first, last):
                pe.matmul(bank_ap, w_ap_hi, x_hi, start=first, stop=False)
                pe.matmul(bank_ap, w_ap_hi, x_lo, start=False, stop=False)
                return pe.matmul(bank_ap, w_ap_lo, x_hi, start=False, stop=last)

            def dense(par, bank, xh, xl, k0=0, nk=KD, first=True, last=True):
                for k in range(nk):
                    c = slice(P * k, P * (k + 1))
                    ins = mm3(psum[:, bank, :], whi[:, par, c], wlo[:, par, c], xh[:, k0 + k, :], xl[:, k0 + k, :],
                              first and k == 0, last and k == nk - 1)
                return ins

            pe.wait_ge(consts, CONSTS_FIRST)
            for hf in range(HALVES):
                for t in range(HT):
                    n = HT * hf + t
                    pe.wait_ge(x_n, n + 1)
                    for b in range(2):
                        if n >= 2:
                            pe.wait_ge(tr_lo, 2 * (n - 2) + b + 1)
                        for k in range(4):
                            ins = pe.transpose(psum[:, 2 * (n % 2) + b, P * k:P * (k + 1)],
                                               xin[:, n % 2, P * (4 * b + k):P * (4 * b + k + 1)], ident[:, :])
                        ins.then_inc(tr, 1)
                pe.wait_ge(tr_hi, 2 * HT * (hf + 1))
                pe.wait_ge(tr_lo, 2 * HT * (hf + 1))
                w0 = N_IN * hf
                A0, D0 = ACT_EV * hf, DVE_EV * hf
                if hf:
                    pe.wait_ge(act_ev, A0)
                    pe.wait_ge(dve_ev, D0)
                for k in range(2):
                    pe.wait_ge(w_lo, w0 + k + 1)
                    dense(slot(w0 + k), 4 + slot(w0 + k), uhi, ulo).then_inc(w_used, 1)
                with pe.Fori(2, N_FIRST, 2) as k:
                    for d in range(2):
                        pe.wait_ge(w_lo, k + (w0 + d + 1))
                        pe.wait_ge(act_ev, k + (A0 + d - 1))
                        pe.wait_ge(dve_ev, k + (D0 + d - 1))
                        dense(slot(w0 + d), 4 + slot(w0 + d), uhi, ulo).then_inc(w_used, 1)
                pe.wait_ge(act_ev, A0 + N_FIRST)
                with pe.Fori(0, CT, 2) as c:
                    for e in range(2):
                        for n in range(3):
                            d = 3 * e + n
                            wd = w0 + N_FIRST + d
                            pe.wait_ge(w_lo, c * 3 + (wd + 1))
                            if n == 0:
                                pe.wait_ge(dve_ev, c * 2 + (D0 + N_FIRST + 2 * e - 1))
                            elif n == 1:
                                pe.wait_ge(dve_ev, c * 2 + (D0 + N_FIRST + 2 * e))
                            else:
                                pe.wait_ge(act_ev, c + (A0 + N_FIRST + e + 1))
                            dense(slot(wd), 4 + slot(wd), uhi, ulo).then_inc(w_used, 1)
                w = w0 + N_IN - 1
                pe.wait_ge(w_lo, w + 1)
                pe.wait_ge(dve_ev, D0 + DVE_EV - 1)
                dense(slot(w), 4 + slot(w), uhi, ulo).then_inc(w_used, 1)

                pe.wait_ge(dve_ev, D0 + N_FIRST)
                for n in range(3):
                    if n == 0 and hf:
                        pe.wait_ge(gexp, hf)
                    if n == 1 and hf:
                        pe.wait_ge(vt_hi, 2 * hf)
                        pe.wait_ge(vt_lo, 2 * hf)
                    if n == 2:
                        pe.wait_ge(act_ev, A0 + ACT_EV)
                        pe.wait_ge(vt_hi, 2 * hf + 1)
                        pe.wait_ge(vt_lo, 2 * hf + 1)
                    for t in range(HT):
                        src = (vraw[:, 0, :], vraw[:, 1, :], graw[:, :])[n]
                        ins = pe.transpose(psum[:, (6, 7, 6)[n], P * t:P * (t + 1)], src[:, P * t:P * (t + 1)],
                                           ident[:, :])
                    ins.then_inc(vt, 1)

            for n in range(HALVES * CT):
                hf, c = divmod(n, CT)
                pe.wait_ge(c_sq, n + 1)
                pe.matmul(psum[:, hf, :], ones[:, :], csq[:, n % 2, :], start=c == 0, stop=c == CT - 1)\
                    .then_inc(c_ss, 1)

            for n in range(2):
                pe.wait_ge(b_lo, n + 1)
                if n == 0:
                    pe.wait_ge(c_ms, HALVES)
                for pc in range(CMP_PC):
                    w = W_CMP + CMP_PC * n + pc
                    pe.wait_ge(w_lo, w + 1)
                    for q in range(LP // CMP_PC):
                        lp = LP // CMP_PC * pc + q
                        c = slice(CMP_HID * q, CMP_HID * (q + 1))
                        o = psum[0:NB, n, 0:CMP_HID]
                        pe.matmul(o, bhi[:, lp, :], whi[:, slot(w), c], start=lp == 0, stop=False)
                        pe.matmul(o, blo[:, lp, :], whi[:, slot(w), c], start=False, stop=False)
                        ins = pe.matmul(o, bhi[:, lp, :], wlo[:, slot(w), c], start=False, stop=lp == LP - 1)
                    ins.then_inc(w_used, 1)
                pe.wait_ge(h3, n + 1)
                if n:
                    pe.wait_ge(h5, n)
                for t in range(2):
                    ins = pe.transpose(psum[:, 2, NB * t:NB * (t + 1)], hid[0:NB, 3, P * t:P * (t + 1)],
                                       ident[0:NB, 0:NB])
                ins.then_inc(h4, 1)
                pe.wait_ge(h5, n + 1)
                if n:
                    pe.wait_ge(cc_lo, n)
                if n == 0:
                    for t in range(2):
                        ins = pe.matmul(psum[:, 3, 0:NB], w2d[:, 0, t, :], hidT[:, t, :], start=t == 0, stop=t == 1)
                else:
                    for g in range(NKV):
                        for t in range(2):
                            ins = pe.matmul(psum[0:NC, 3, HD * g:HD * (g + 1)], hidT[:, t, NC * g:NC * (g + 1)],
                                            w2d[:, 1, t, 0:HD], start=t == 0, stop=t == 1)
                ins.then_inc(m2, 1)

            def scores(m):
                n, wc = divmod(m, 2)
                u, j = divmod(n, GQA)
                i, g = divmod(u, NKV)
                q = qs[:, GQA * g + j, P * i:P * (i + 1)]
                n_sel, n_win = P * (i + 1), P * min(i + 1, WIN_T + 1)

                def against(br, bank, start_key, keys):
                    for c in range(0, keys, 512):
                        cn = min(512, keys - c)
                        o = psum[:, bank + c // 512, 0:cn]
                        for part in range(2):
                            ins = pe.matmul(o, q, ks[:, br, part, g, start_key + c:start_key + c + cn],
                                            start=part == 0, stop=part == 1)
                    return ins

                if n:
                    pe.wait_ge(wc_read if wc else sel_read, n)
                if wc:
                    against(1, 2, n_sel - n_win, n_win)
                    for part in range(2):
                        ins = pe.matmul(psum[:, 3, P:P + NC + 1], q, kcc[:, part, g, :],
                                        start=part == 0, stop=part == 1)
                    ins.then_inc(qk_wc, 1)
                else:
                    against(0, 0, 0, n_sel).then_inc(qk_sel, 1)

            def transposes(kt):
                u = unit_of(kt)
                col, rows = KTS[u][kt - KT_BASE[u]][2], rows_of(kt)
                if kt == KT_BASE[u]:
                    pe.wait_ge(exped, ITEMS * (u + 1))
                if kt >= 2:
                    pe.wait_ge(pt_lo, kt - 1)
                for j in range(GQA):
                    s = (GQA * u + j) % SLOTS
                    ins = pe.transpose(psum[0:rows, 4 + kt % 2, P * j:P * (j + 1)], probs[:, s, col:col + rows],
                                       ident[:, :])
                ins.then_inc(pt, 1)

            def values(kt):
                u = unit_of(kt)
                br, t, _ = KTS[u][kt - KT_BASE[u]]
                g, rows, group = u % NKV, rows_of(kt), NBR * u + br
                v = vcc[0:rows, g, :] if br == 2 else vs[:, br, t, g, :]
                pe.wait_ge(pt_lo, kt + 1)
                first, last = kt == GROUP_START[group], kt == GROUP_END[group]
                if first and group >= 2:
                    pe.wait_ge(o_part, group - 1)
                o = psum[:, 6 + group % 2, :]
                pe.matmul(o, v, pthi[0:rows, kt % 2, :], start=first, stop=False)
                pe.matmul(o, v, ptlo[0:rows, kt % 2, :], start=False, stop=last).then_inc(pv, 1)
                for e in groups_ending(kt - 1):
                    folded(e)

            def folded(g):
                pe.wait_ge(o_sb, g + 1)
                for j in range(GQA):
                    ins = pe.matmul(psum[:, 6 + g % 2, HD * j:HD * (j + 1)], osb[:, g % 2, P * j:P * (j + 1)],
                                    fold[:, :], start=True, stop=True)
                ins.then_inc(o_tok, 1)

            pe.wait_ge(consts, CONSTS_ALL)
            pe.wait_ge(ks_out, 16 * 16)
            for k in range(2):
                pe.wait_ge(q_out[k], 64 * HALVES * QT // 2)
            pe.wait_ge(cc_lo, 2)
            pe.wait_ge(vt_lo, 2 * HALVES)
            pe.wait_ge(vt_hi, 2 * HALVES)
            for m in range(ITEMS + 1):
                scores(m)
            for u in range(UNITS):
                for b in range(BEATS):
                    m = ITEMS * (u + 1) + b + 1
                    if b < ITEMS and m < N_ITEMS:
                        scores(m)
                    for kt in beat_tiles(u, b):
                        transposes(kt)
                        if kt:
                            values(kt - 1)
            values(N_KT - 1)
            for g in groups_ending(N_KT - 1):
                folded(g)

            for hf in range(HALVES):
                for t in range(HT):
                    n = TR_BASE(hf) + t
                    pe.wait_ge(s_n, 2 * HT * hf + t + 1)
                    if n >= 2:
                        pe.wait_ge(tr_lo, n - 1)
                    for k in range(CT):
                        ins = pe.transpose(psum[:, t % 2, P * k:P * (k + 1)], nrm[:, t % 2, P * k:P * (k + 1)],
                                           ident[:, :])
                    ins.then_inc(tr, 1)
                pe.wait_ge(tr_lo, TR_BASE(hf) + HT)
                pe.wait_ge(cm_lo, CT * (hf + 1))

                def turn(n, par, again=True):
                    if again:
                        pe.wait_ge(y_add, n - 1)
                    pe.wait_ge(y_sb, n + 1)
                    for t in range(HT):
                        ins = pe.transpose(psum[:, 6 + par, P * t:P * (t + 1)], yT[:, par, P * t:P * (t + 1)],
                                           ident[:, :])
                    ins.then_inc(y_tr, 1)

                w0, y0 = w_of(hf, "out"), 2 * KD * hf
                for m in range(2):
                    pe.wait_ge(w_lo, w0 + m + 1)
                    if hf:
                        pe.wait_ge(y_sb, y0 + m - 1)
                    dense(slot(w0 + m), 4 + m, mhi, mlo).then_inc(w_used, 1)

                def project(m, d):
                    pe.wait_ge(w_lo, m + (w0 + d + 1))
                    pe.wait_ge(y_sb, m + (y0 + d - 1))
                    dense(slot(w0 + d), 4 + d, mhi, mlo).then_inc(w_used, 1)

                for d in range(2):
                    project(2, d)
                    turn(y0 + d, d, hf > 0)
                with pe.Fori(4, KD, 2) as m:
                    for d in range(2):
                        project(m, d)
                        turn(m + (y0 + d - 2), d)
                for m in range(2):
                    turn(y0 + KD - 2 + m, m)

                for t in range(HT):
                    pe.wait_ge(s_n, 2 * HT * hf + HT + t + 1)
                    for b in range(2):
                        n = TR_BASE(hf) + HT + 2 * t + b
                        if t >= 2:
                            pe.wait_ge(tr_lo, n - 3)
                        for k in range(4):
                            ins = pe.transpose(psum[:, 2 * (t % 2) + b, P * k:P * (k + 1)],
                                               nrm[:, t % 2, P * (4 * b + k):P * (4 * b + k + 1)], ident[:, :])
                        ins.then_inc(tr, 1)
                pe.wait_ge(tr_lo, TR_BASE(hf) + 3 * HT)

                w0, f0 = w_of(hf, "glu"), FT * hf
                for f in range(2):
                    for d in range(2):
                        pe.wait_ge(w_lo, w0 + 2 * f + d + 1)
                        dense(slot(w0 + d), 2 * f + d, vhi, vlo).then_inc(w_used, 1)
                with pe.Fori(2, FT, 2) as f:
                    for e in range(2):
                        pe.wait_ge(glu, f + (f0 + e - 1))
                        for d in range(2):
                            pe.wait_ge(w_lo, f * 2 + (w0 + 2 * e + d + 1))
                            dense(slot(w0 + d), 2 * e + d, vhi, vlo).then_inc(w_used, 1)
                pe.wait_ge(g_lo, f0 + FT)
                pe.wait_ge(g_hi, f0 + FT)

                w0, y0 = w_of(hf, "down"), KD * (2 * hf + 1)

                def down(m, e):
                    pe.wait_ge(y_sb, m + (y0 + e - 1))
                    for n, (k0, nk) in enumerate(PIECES):
                        d = NPC * e + n
                        pe.wait_ge(w_lo, m * NPC + (w0 + d + 1))
                        dense(slot(w0 + d), 4 + e, hhi, hlo, k0, nk, n == 0, n == NPC - 1).then_inc(w_used, 1)

                for e in range(2):
                    down(0, e)
                with pe.Fori(2, KD, 2) as m:
                    for e in range(2):
                        down(m, e)
                        turn(m + (y0 + e - 2), e)
                for e in range(2):
                    turn(y0 + KD - 2 + e, e)

        @block.vector
        def _(dve):
            class Own:
                n = 0

            def did(ins):
                ins.then_inc(own, 1)
                Own.n += 1

            def settle():
                dve.wait_ge(own, Own.n)

            for h in range(NH):
                did(dve.memset(qscale[HD * (h % 2):HD * (h % 2 + 1), h // 2:h // 2 + 1],
                               HD ** -0.5 * 2.0 ** (h + 1)))
            dve.wait_ge(consts, CONSTS_FIRST)
            for hf in range(HALVES):
                def norm_tile(t):
                    n = HT * hf + t
                    dve.wait_ge(x_sq, 2 * n + 1)
                    dve.tensor_scalar(ssq[:, n:n + 1], ssq[:, n:n + 1], 1.0 / DM, EPS, ALU.mult, ALU.add)\
                        .then_inc(x_ms, 1)
                    dve.wait_ge(x_sq, 2 * n + 2)
                    dve.reciprocal(inv[:, n:n + 1], rms[:, n:n + 1]).then_inc(x_ms, 1)
                    dve.wait_ge(x_ms, 2 * n + 2)
                    if n == 0:
                        dve.wait_ge(vecs, 16)
                    dve.scalar_tensor_tensor(xin[:, n % 2, :], xin[:, n % 2, :], inv[:, n:n + 1], g1b[:, :],
                                             ALU.mult, ALU.mult).then_inc(x_n, 1)

                def norm_lo(t):
                    n = HT * hf + t
                    for b in range(2):
                        dve.wait_ge(tr_hi, 2 * n + b + 1)
                        sl = (slice(None), slice(4 * b, 4 * b + 4), slice(P * t, P * (t + 1)))
                        dve.tensor_tensor(ulo[sl], psum[:, 2 * (n % 2) + b, :].rearrange("p (k m) -> p k m", m=P),
                                          raw(uhi[sl]), ALU.subtract).then_inc(tr_lo, 1)

                if hf:
                    dve.wait_ge(w_used, N_IN * hf)
                for t in range(HT):
                    norm_tile(t)
                    if t:
                        norm_lo(t - 1)
                norm_lo(HT - 1)

                w0, tok = N_IN * hf, HN * hf
                for k in range(QT):
                    w = w0 + k
                    dve.wait_ge(act_ev, ACT_EV * hf + k + 1)
                    dve.scalar_tensor_tensor(qstage[:, k % 2, 1, :], psum[:, 4 + slot(w), :], qscale[:, k:k + 1],
                                             raw(qstage[:, k % 2, 0, :]), ALU.mult, ALU.subtract).then_inc(dve_ev, 1)
                for k in range(QT, QT + 2):
                    w = w0 + k
                    dve.wait_ge(act_ev, ACT_EV * hf + k + 1)
                    dve.tensor_tensor(kT[:, k - QT, 1, tok:tok + HN], psum[:, 4 + slot(w), :],
                                      raw(kT[:, k - QT, 0, tok:tok + HN]), ALU.subtract).then_inc(dve_ev, 1)
                for k in range(QT + 2, N_FIRST):
                    w = w0 + k
                    dve.wait_ge(w_used, w + 1)
                    dst = vraw if k < QT + 4 else kcraw
                    if hf and k >= QT + 4:
                        dve.wait_ge(kc_out[k % 2], 64)
                    dve.tensor_copy(dst[HD:P, k % 2, :], psum[HD:P, 4 + slot(w), :]).then_inc(dve_ev, 1)
                if hf == 0:
                    dve.wait_ge(vecs, VECS)
                for c in range(CT):
                    w = w0 + N_FIRST + 3 * c
                    dve.wait_ge(act_ev, ACT_EV * hf + N_FIRST + c + 1)
                    dve.wait_ge(w_used, w + 2)
                    dve.tensor_tensor(useq[:, c, 2:HN + 2], psum[:, 4 + slot(w + 1), :], ccs[:, :], ALU.mult)\
                        .then_inc(dve_ev, 1)
                    dve.wait_ge(dve_ev, DVE_EV * hf + N_FIRST + 2 * c + 1)
                    did(dve.tensor_scalar(cacc[:, :], useq[:, c, 0:HN], taps[:, 0, c:c + 1], None, ALU.mult))
                    for n in (1, 2):
                        settle()
                        did(dve.scalar_tensor_tensor(cacc[:, :], useq[:, c, n:n + HN], taps[:, n, c:c + 1],
                                                     cacc[:, :], ALU.mult, ALU.add))
                    if hf == 0:
                        settle()
                        did(dve.tensor_copy(useq[:, c, 0:2], useq[:, c, HN:HN + 2]))
                    dve.wait_ge(w_used, w + 3)
                    settle()
                    dve.tensor_tensor(convT[:, c, tok:tok + HN], cacc[:, :], psum[:, 4 + slot(w + 2), :],
                                      ALU.mult).then_inc(dve_ev, 1)
                    dve.wait_ge(dve_ev, DVE_EV * hf + N_FIRST + 2 * c + 2)

                for br in range(2):
                    dve.wait_ge(vt_hi, 2 * hf + br + 1)
                    tt = slice(HT * hf, HT * (hf + 1))
                    dve.tensor_tensor(vs[:, br, tt, :, HD:2 * HD],
                                      psum[:, 6 + br, :].rearrange("p (t g d) -> p t g d", t=HT, g=NKV),
                                      raw(vs[:, br, tt, :, 0:HD]), ALU.subtract).then_inc(vt_lo, 1)
                dve.wait_ge(gexp, hf + 1)
                g_ap = gates[:, HT * hf:HT * (hf + 1), :]
                did(dve.tensor_scalar(g_ap, g_ap, 1.0, None, ALU.add))
                settle()
                did(dve.reciprocal(g_ap, g_ap))

            for hf in range(HALVES):
                dve.wait_ge(c_ss, CT * (hf + 1))
                dve.tensor_scalar(crms[:, HN * hf:HN * (hf + 1)], psum[:, hf, :], 1.0 / CONV, EPS,
                                  ALU.mult, ALU.add).then_inc(c_ms, 1)

            def norm_conv():
                for hf in range(HALVES):
                    cr = crms[:, HN * hf:HN * (hf + 1)]
                    dve.wait_ge(c_rt, hf + 1)
                    did(dve.reciprocal(cr, cr))
                    settle()
                    for c in range(CT):
                        ct = convT[:, c, HN * hf:HN * (hf + 1)]
                        dve.scalar_tensor_tensor(ct, ct, gconv[:, c:c + 1], cr, ALU.mult, ALU.mult)\
                            .then_inc(c_done, 1)

            for n in range(2):
                dve.wait_ge(kc_out[n], 64 * HALVES)
                if n == 0:
                    for k in range(2):
                        dve.wait_ge(q_out[k], 64 * HALVES * QT // 2)
                if n:
                    dve.wait_ge(b_hi, n)
                    dve.wait_ge(b_lo, n)
                for g in range(NKV):
                    src = kcs[:, n, g, 0:CMP_STRIDE * (NC - 1) + CMP_BLOCK]\
                        .rearrange("p (b l) -> p l b", l=CMP_STRIDE)
                    for part in range(2):
                        lh = LP // 2
                        o = blk[:, lh * part:lh * (part + 1), NC * g:NC * (g + 1)]
                        i0 = src[:, 0:CMP_STRIDE:2, part:part + NC]
                        i1 = pos[:, n, lh * part:lh * (part + 1)].unsqueeze(2).broadcast_to([P, lh, NC])
                        ins = dve.tensor_tensor(o, i0, i1, ALU.add)
                        if g == NKV - 1 and part == 1:
                            ins.then_inc(b_raw, 1)
                        else:
                            did(ins)
                settle()
                dve.wait_ge(b_hi, n + 1)
                if n:
                    dve.wait_ge(w_used, W_CMP + CMP_PC)
                dve.tensor_tensor(blo[:, :, :], blk[:, :, :], raw(bhi[:, :, :]), ALU.subtract).then_inc(b_lo, 1)
                dve.wait_ge(h0, n + 1)
                h = hid[0:NB]
                did(dve.tensor_tensor(h[:, 1, :], h[:, 0, :], h[:, 0, :], ALU.mult))
                settle()
                did(dve.tensor_scalar(h[:, 1, :], h[:, 1, :], 0.044715, 1.0, ALU.mult, ALU.add))
                settle()
                dve.tensor_tensor(h[:, 1, :], h[:, 1, :], h[:, 0, :], ALU.mult).then_inc(h1, 1)
                dve.wait_ge(h2, n + 1)
                dve.scalar_tensor_tensor(h[:, 3, :], h[:, 2, :], 1.0, h[:, 0, :], ALU.add, ALU.mult).then_inc(h3, 1)
                dve.wait_ge(cc_hi, n + 1)
                if n == 0:
                    dve.tensor_tensor(kcc[:, 1, :, 0:NC], psum[:, 3, 0:NB].rearrange("p (g m) -> p g m", g=NKV),
                                      raw(kcc[:, 0, :, 0:NC]), ALU.subtract)\
                        .then_inc(cc_lo, 1)
                    norm_conv()
                else:
                    dve.tensor_tensor(vcc[0:NC, :, HD:2 * HD],
                                      psum[0:NC, 3, 0:P].rearrange("p (g d) -> p g d", g=NKV),
                                      raw(vcc[0:NC, :, 0:HD]), ALU.subtract).then_inc(cc_lo, 1)

            def masked(m):
                n, wc = divmod(m, 2)
                u, j = divmod(n, GQA)
                i, g = divmod(u, NKV)
                s = n % SLOTS
                slope = 2.0 ** -(GQA * g + j + 1)
                n_sel, n_win = P * (i + 1), P * min(i + 1, WIN_T + 1)
                flat = psum[:, :, :].rearrange("p b m -> p (b m)")

                def one(br, col, cols, src, dist):
                    return dve.tensor_tensor_reduce(
                        out=probs[:, s, col:col + cols], in0=src, in1=dist, scale=-slope, scalar=-FLOOR,
                        op0=ALU.add, op1=ALU.min, accum_out=nmax[:, s, br:br + 1])

                if u >= 2 and m % ITEMS == 0:
                    dve.wait_ge(pt, KT_BASE[u - 1])
                if wc:
                    dve.wait_ge(qk_wc, n + 1)
                    one(WIN, n_sel, n_win, flat[:, 1024:1024 + n_win], dwin[:, WINDOW + P - n_win:WINDOW + P])
                    one(CMP, n_sel + n_win, NC, psum[:, 3, P:P + NC], dcmp[:, i, :]).then_inc(wc_read, 1)
                else:
                    dve.wait_ge(qk_sel, n + 1)
                    one(SEL, 0, n_sel, flat[:, 0:n_sel], dsel[:, SEQ - n_sel:SEQ]).then_inc(sel_read, 1)

            def weigh(u):
                i, g = divmod(u, NKV)
                s = slice(GQA * u % SLOTS, GQA * u % SLOTS + GQA)
                dve.wait_ge(exped, ITEMS * (u + 1))
                did(dve.tensor_scalar(rsafe[:, s, :], rsum[:, s, :], 1e-30, None, ALU.max))
                settle()
                did(dve.reciprocal(rinv[:, s, :], rsafe[:, s, :]))
                settle()
                did(dve.tensor_tensor(wgt[:, s, :], rinv[:, s, :],
                                      gates[:, i, NBR * GQA * g:NBR * GQA * (g + 1)]
                                      .rearrange("p (h b) -> p h b", b=NBR), ALU.mult))
                settle()

            def weighed(gr):
                u, br = divmod(gr, NBR)
                s0 = GQA * u % SLOTS
                w = wgt[:, s0:s0 + GQA, (SEL, WIN, CMP)[br]].unsqueeze(2).broadcast_to([P, GQA, HD])
                dve.wait_ge(o_tok, gr + 1)
                if u >= 2:
                    dve.wait_ge(o_done, u - 1)
                dve.tensor_tensor(parts[:, u % 2, br, :].rearrange("p (h d) -> p h d", d=HD),
                                  psum[:, 6 + gr % 2, 0:GQA * HD].rearrange("p (h d) -> p h d", d=HD), w,
                                  ALU.mult).then_inc(o_part, 1)

            def lo_tile(kt):
                rows = rows_of(kt)
                dve.wait_ge(pt_hi, kt + 1)
                dve.tensor_tensor(ptlo[0:rows, kt % 2, :], psum[0:rows, 4 + kt % 2, :],
                                  raw(pthi[0:rows, kt % 2, :]), ALU.subtract).then_inc(pt_lo, 1)
                for gr in groups_ending(kt - 2):
                    weighed(gr)

            dve.wait_ge(consts, CONSTS_ALL)
            for m in range(ITEMS):
                masked(m)
            for u in range(UNITS):
                for b in range(BEATS):
                    if b < ITEMS and u + 1 < UNITS:
                        masked(ITEMS * (u + 1) + b)
                    if b == 0:
                        weigh(u)
                    for kt in beat_tiles(u, b):
                        lo_tile(kt)
            for kt in range(N_KT - 2, N_KT):
                for gr in groups_ending(kt):
                    weighed(gr)

            def half_inv(n, width):
                dve.wait_ge(s_sq, (HT + 1) * n + HT)
                dve.tensor_scalar(ssq[:, 0:HT], ssq[:, 0:HT], 1.0 / width, EPS, ALU.mult, ALU.add).then_inc(s_ms, 1)
                dve.wait_ge(s_sq, (HT + 1) * (n + 1))
                dve.reciprocal(inv[:, 0:HT], rms[:, 0:HT]).then_inc(s_ms, 1)
                dve.wait_ge(s_ms, 2 * n + 2)

            for hf in range(HALVES):
                def lo_of(n, dst, hi, bank):
                    dve.wait_ge(tr_hi, n + 1)
                    dve.tensor_tensor(dst, psum[:, bank, :].rearrange("p (k m) -> p k m", m=P), raw(hi),
                                      ALU.subtract).then_inc(tr_lo, 1)

                half_inv(3 * hf, NH * HD)
                dve.wait_ge(gv_in, 16 * (3 * hf + 1))
                for t in range(HT):
                    n = TR_BASE(hf) + t
                    if t >= 2:
                        dve.wait_ge(tr, n - 1)
                    ins = dve.scalar_tensor_tensor(nrm[:, t % 2, 0:NH * HD], nsa[:, HT * hf + t, :], inv[:, t:t + 1],
                                                   gvec[:, 0:NH * HD], ALU.mult, ALU.mult)
                    ins.then_inc(s_n, 1)
                    if t:
                        sl = (slice(None), slice(CT, KD), slice(P * (t - 1), P * t))
                        lo_of(n - 1, mlo[sl], mhi[sl], (t - 1) % 2)
                sl = (slice(None), slice(CT, KD), slice(P * (HT - 1), P * HT))
                lo_of(TR_BASE(hf) + HT - 1, mlo[sl], mhi[sl], (HT - 1) % 2)

                def add_y(n, par, dst):
                    dve.wait_ge(y_tr, n + 1)
                    dve.tensor_tensor(dst, dst, psum[:, 6 + par, :].rearrange("p (t m) -> p t m", t=HT), ALU.add)\
                        .then_inc(y_add, 1)

                dve.wait_ge(res_in, 16 * (hf + 1))
                y0 = 2 * KD * hf
                with dve.Fori(0, KD // 2) as mm:
                    for d in range(2):
                        add_y(mm * 2 + (y0 + d), d, res[:, :, ds(mm * (2 * P) + P * d, P)])

                half_inv(3 * hf + 1, DM)
                dve.wait_ge(gv_in, 16 * (3 * hf + 2))
                for t in range(HT):
                    n = TR_BASE(hf) + HT + 2 * t
                    if t >= 2:
                        dve.wait_ge(tr, n - 2)
                    dve.scalar_tensor_tensor(nrm[:, t % 2, :], res[:, t, :], inv[:, t:t + 1], gvec[:, :],
                                             ALU.mult, ALU.mult).then_inc(s_n, 1)
                    for tt in ([t - 1] if t else []) + ([t] if t == HT - 1 else []):
                        for b in range(2):
                            sl = (slice(None), slice(4 * b, 4 * b + 4), slice(P * tt, P * (tt + 1)))
                            lo_of(TR_BASE(hf) + HT + 2 * tt + b, vlo[sl], vhi[sl], 2 * (tt % 2) + b)

                f0, w0 = FT * hf, w_of(hf, "glu")

                def up_of(f, par):
                    dve.wait_ge(sil, f + (f0 + 1))
                    dve.wait_ge(w_used, f * 2 + (w0 + 2))
                    dve.tensor_tensor(silu[:, par, :], silu[:, par, :], psum[:, 2 * par + 1, :], ALU.mult)\
                        .then_inc(glu, 1)
                    dve.wait_ge(g_hi, f + (f0 + 1))

                with dve.Fori(0, FT // 2) as ff:
                    for e in range(2):
                        f = ff * 2 + e
                        up_of(f, e)
                        dve.tensor_tensor(hlo[:, ds(f, 1), :], silu[:, e:e + 1, :], raw(hhi[:, ds(f, 1), :]),
                                          ALU.subtract).then_inc(g_lo, 1)

                y0 = KD * (2 * hf + 1)
                with dve.Fori(0, KD // 2) as mm:
                    for d in range(2):
                        add_y(mm * 2 + (y0 + d), d, res[:, :, ds(mm * (2 * P) + P * d, P)])
                half_inv(3 * hf + 2, DM)
                dve.wait_ge(gv_in, 16 * (3 * hf + 3))
                for t in range(HT):
                    dve.scalar_tensor_tensor(res[:, t, :], res[:, t, :], inv[:, t:t + 1], gvec[:, :],
                                             ALU.mult, ALU.mult).then_inc(fin, 1)


CONSTS_FIRST = 2 + CT + 2
CONSTS_ALL = CONSTS_FIRST + 3
VECS = 16 * (1 + 1 + 3 + 2 * 3)


def TR_BASE(hf):
    return 2 * NT + 3 * HT * hf


_INS = ["x", "norm1_g", "w_in", "conv_w", "k_cmp_pos", "k_cmp_w1", "k_cmp_w2", "v_cmp_pos", "v_cmp_w1",
        "v_cmp_w2", "gn_conv_g", "gn_nsa_g", "w_out", "norm2_g", "w_gate", "w_up", "w_down", "norm_f_g"]


def kernel(**inputs):
    import numpy as np
    import concourse.bacc as bacc
    from concourse.bass_utils import run_bass_kernel_spmd

    nc = bacc.Bacc("TRN2", target_bir_lowering=False, num_devices=1)
    arrays, args = {}, []
    for name in _INS:
        a = np.ascontiguousarray(inputs[name])
        arrays[f"in_{name}"] = a
        args.append(nc.dram_tensor(f"in_{name}", a.shape, mybir.dt.from_np(a.dtype), kind="ExternalInput").ap())
    args.append(nc.dram_tensor("out_h", (1, SEQ, DM), mybir.dt.float32, kind="ExternalOutput").ap())
    hymba_block(nc, *args)
    r = run_bass_kernel_spmd(nc, [arrays], core_ids=[0])
    return r.results[0]["out_h"]
```

```python
from contextlib import ExitStack

import concourse.bass as bass
from concourse import mybir

P = 128
SEQ, DM = 1024, 1024
NT = SEQ // P
KD = DM // P
HALVES, HT = 2, NT // 2
HN = HT * P
CONV = 512
CT = CONV // P
NH, HD, NKV, GQA = 8, 64, 2, 4
CMP_BLOCK, CMP_STRIDE, CMP_HID = 32, 16, 256
NC = (SEQ - CMP_BLOCK) // CMP_STRIDE + 1
NB = NKV * NC
LP = CMP_BLOCK // 2
SEL_BLOCK, SEL_TOP = 64, 16
assert SEQ // SEL_BLOCK <= SEL_TOP
WIN_T = 4
WINDOW = WIN_T * P
DFF = 2816
FT = DFF // P
EPS = 1e-6
NBR = 3
NGATE = NH * NBR

D_IN = 3 * CONV + NH * HD + 6 * NKV * HD + NGATE
Q0 = 3 * CONV
KC0, VC0, KS0, VS0, KW0, VW0 = (Q0 + NH * HD + P * n for n in range(6))
QT = NH * HD // P
FIRST_COLS = [Q0 + P * t for t in range(QT)] + [KS0, KW0, VS0, VW0, KC0, VC0]
N_FIRST = len(FIRST_COLS)
N_IN = N_FIRST + 3 * CT + 1
GATE0 = P - NGATE
ACT_EV = N_FIRST + CT + 1
DVE_EV = N_FIRST + 2 * CT
PIECES = [(0, 8), (8, 8), (16, FT - 16)]
NPC = len(PIECES)
CMP_PC = 4

W_CMP = HALVES * N_IN
W_BACK = W_CMP + 2 * CMP_PC
N_OUT = HALVES * KD
N_FFN = 2 * FT + NPC * KD
W_END = W_BACK + N_OUT + HALVES * N_FFN

MASKED = -1.0e38
CMP, SEL, WIN = range(NBR)
FLOOR = -1.0e30
SLOTS = 8
UNITS = NT * NKV
CMP_AT = SEQ + WINDOW + P

KiB = 1024


def key_tiles(i):
    j0 = max(0, i - WIN_T)
    sel = [(0, j, P * j) for j in range(i + 1)]
    win = [(1, j, P * (i + 1) + P * (j - j0)) for j in range(j0, i + 1)]
    return sel + win + [(2, 0, P * (i + 1) + P * (i + 1 - j0))]


KTS = [key_tiles(u // NKV) for u in range(UNITS)]
KT_BASE = [sum(len(k) for k in KTS[:u]) for u in range(UNITS + 1)]


ITEMS = 2 * GQA
N_ITEMS = ITEMS * UNITS
BEATS = ITEMS + 1
N_KT = KT_BASE[UNITS]
LAG = 2
GROUP_END = [KT_BASE[u] + max(q for q, (b, _, _) in enumerate(KTS[u]) if b == br)
             for u in range(UNITS) for br in range(NBR)]
GROUP_START = [0] + [e + 1 for e in GROUP_END[:-1]]


def slot_of(n):
    return (n + GQA) % SLOTS


def beat_tiles(u, b):
    n = len(KTS[u])
    return range(KT_BASE[u] + n * b // BEATS, KT_BASE[u] + n * (b + 1) // BEATS)


def unit_of(kt):
    return max(u for u in range(UNITS) if KT_BASE[u] <= kt)


def rows_of(kt):
    u = unit_of(kt)
    return NC if KTS[u][kt - KT_BASE[u]][0] == 2 else P


def groups_ending(kt):
    return [g for g in range(NBR * UNITS) if GROUP_END[g] == kt]


def hymba_block(nc, x, norm1_g, w_in, conv_w, k_cmp_pos, k_cmp_w1, k_cmp_w2, v_cmp_pos, v_cmp_w1,
                v_cmp_w2, gn_conv_g, gn_nsa_g, w_out, norm2_g, w_gate, w_up, w_down, norm_f_g, out):
    f32, f32r = mybir.dt.float32, mybir.dt.float32r
    ALU = mybir.AluOpType
    ACT = mybir.ActivationFunctionType
    ds = bass.ds

    x, out = x[0], out[0]
    w_in, w_out, w_gate, w_up, w_down = w_in[0], w_out[0], w_gate[0], w_up[0], w_down[0]
    x_t = x.rearrange("(t p) d -> p t d", p=P)
    out_t = out.rearrange("(t p) d -> p t d", p=P)
    w_in_k = w_in.rearrange("(k p) m -> p k m", p=P)
    w_out_k = w_out.rearrange("(k p) m -> p k m", p=P)
    w_gate_k = w_gate.rearrange("(k p) m -> p k m", p=P)
    w_up_k = w_up.rearrange("(k p) m -> p k m", p=P)
    w_down_k = w_down.rearrange("(k p) m -> p k m", p=P)
    w1_k = [w[0].rearrange("(c p) m -> p c m", p=P) for w in (k_cmp_w1, v_cmp_w1)]
    w2_k = [w[0].rearrange("(c p) m -> p c m", p=P) for w in (k_cmp_w2, v_cmp_w2)]
    pos_k = [w[0].rearrange("(c l) d -> (l d) c", l=2) for w in (k_cmp_pos, v_cmp_pos)]

    ctx = ExitStack()
    with ctx:
        origin = (nc.sbuf_base + 31) // 32 * 32
        limit = nc.sbuf_usable_end

        def at(name, offset, shape, dt=f32):
            size = 4
            for n in shape[1:]:
                size *= n
            assert origin + offset + size <= limit, (name, origin + offset + size - limit)
            return nc.alloc_sbuf_tensor_at(name, shape, dt, offset=origin + int(offset))

        def sem(name):
            return ctx.enter_context(nc.semaphore(name))

        place = [0]

        def small(name, shape, dt=f32):
            size = 4
            for n in shape[1:]:
                size *= n
            t = at(name, place[0], shape, dt)
            place[0] += (size + 31) // 32 * 32
            assert place[0] <= 8 * KiB, place[0]
            return t

        ident = small("ident", [P, P])
        fold = small("fold", [P, HD])
        ones = small("ones", [P, P])
        ssq = small("ssq", [P, NT])
        rms = small("rms", [P, NT])
        inv = small("inv", [P, NT])
        gconv = small("gconv", [P, CT])
        taps = small("taps", [P, 3, CT])
        gates = small("gates", [P, NT, NGATE])
        pos = small("pos", [P, 2, LP])
        w2d = small("w2d", [P, 2, 2, 2 * HD])
        qscale = small("qscale", [P, QT])
        kcc = small("kcc", [P, 2, NKV, NC + 1], f32r)
        vcc = small("vcc", [P, NKV, 2 * HD], f32r)
        nmax = small("nmax", [P, SLOTS, NBR])
        rsum = small("rsum", [P, SLOTS, NBR])
        rsafe = small("rsafe", [P, SLOTS, NBR])
        rinv = small("rinv", [P, SLOTS, NBR])
        wgt = small("wgt", [P, SLOTS, NBR])

        convT = at("convT", 8 * KiB, [P, CT, SEQ])
        wraw = at("wraw", 104 * KiB, [P, 2, 1024])
        whi = at("whi", 112 * KiB, [P, 2, 1024], f32r)
        wlo = at("wlo", 120 * KiB, [P, 2, 1024], f32r)
        qs = at("qs", 24 * KiB, [P, NH, SEQ], f32r)
        vs = at("vs", 56 * KiB, [P, 2, NT, NKV, 2 * HD], f32r)
        kT = at("kT", 72 * KiB, [P, 2, 2, SEQ], f32r)
        kcs = at("kcs", 88 * KiB, [P, 2, NKV, SEQ])
        uhi = at("uhi", 128 * KiB, [P, KD, HN], f32r)
        ulo = at("ulo", 144 * KiB, [P, KD, HN], f32r)
        xin = at("xin", 160 * KiB, [P, 2, DM])
        g1b = at("g1b", 168 * KiB, [P, DM])
        qstage = at("qstage", 172 * KiB, [P, 2, 2, HN], f32r)
        vraw = at("vraw", 180 * KiB, [P, 2, HN])
        kcraw = at("kcraw", 184 * KiB, [P, 2, HN])
        graw = at("graw", 188 * KiB, [P, HN])
        ccs = at("ccs", 190 * KiB, [P, HN])
        cacc = at("cacc", 192 * KiB, [P, HN])
        useq = at("useq", 194 * KiB, [P, CT, HN + 2])
        junk1 = at("junk1", 203 * KiB, [P, DM])
        csq = at("csq", 198 * KiB, [P, 2, HN])
        crms = at("crms", 202 * KiB, [P, SEQ])
        ks = at("ks", 128 * KiB, [P, 2, 2, NKV, SEQ], f32r)
        blk = at("blk", 160 * KiB, [P, LP, NB])
        bhi = at("bhi", 168 * KiB, [P, LP, NB], f32r)
        blo = at("blo", 176 * KiB, [P, LP, NB], f32r)
        hid = at("hid", 184 * KiB, [P, 4, CMP_HID])
        hidT = at("hidT", 206.5 * KiB, [P, 2, NB])
        dsel = at("dsel", 188 * KiB, [P, SEQ])
        dwin = at("dwin", 192 * KiB, [P, WINDOW + P])
        dcmp = at("dcmp", 194.5 * KiB, [P, NT, NC])
        probs = at("probs", 72 * KiB, [P, SLOTS, CMP_AT + HD])
        pthi = [at(f"pthi{n}", k * KiB, [P, GQA * P], f32r) for n, k in enumerate((160, 162, 204.5))]
        ptlo = [at(f"ptlo{n}", k * KiB, [P, GQA * P], f32r) for n, k in enumerate((164, 166, 202.5))]
        osb = at("osb", 168 * KiB, [P, 2, GQA * P])
        parts = at("parts", 196.5 * KiB, [P, 2, NBR, GQA * HD])
        nsa = at("nsa", 172 * KiB, [P, NT, NH * HD])
        gnsa = at("gnsa", 148 * KiB, [P, NH * HD])
        junk2 = at("junk2", 126 * KiB, [P, NH * HD])
        mhi = at("mhi", 24 * KiB, [P, HALVES, KD, HN], f32r)
        mlo = at("mlo", 128 * KiB, [P, HALVES, KD, HN], f32r)
        nnsa = [at("nnsa0", 144 * KiB, [P, 2, NH * HD]),
                at("nnsa1", 56 * KiB, [P, 2, NH * HD])]
        junk3 = at("junk3", 60 * KiB, [P, NH * HD])
        res = [at("res0", 188 * KiB, [P, HT, DM]),
               at("res1", 172 * KiB, [P, HT, DM])]
        yT = at("yT", 100 * KiB, [P, 2, HN])
        g2 = at("g2", 8 * KiB, [P, DM])
        gf = at("gf", 12 * KiB, [P, DM])
        nrm = at("nrm", 16 * KiB, [P, 2, DM])
        hhi = at("hhi", 24 * KiB, [P, FT, HN], f32r)
        hlo = at("hlo", 128 * KiB, [P, FT, HN], f32r)
        vhi = at("vhi", 68 * KiB, [P, KD, HN], f32r)
        vlo = at("vlo", 84 * KiB, [P, KD, HN], f32r)
        silu = yT
        psum = ctx.enter_context(nc.psum_tensor("psum", [P, 8, 512], f32))

        w_in_sem = [sem("w_arrived0"), sem("w_arrived1")]
        w_hi = sem("w_hi")
        w_lo = sem("w_lo")
        w_used = sem("w_used")
        consts = sem("consts")
        vecs = sem("vecs")
        x_in = [sem("x_in0"), sem("x_in1")]
        x_sq = sem("x_sq")
        x_ms = sem("x_ms")
        x_n = sem("x_n")
        tr = sem("tr")
        tr_hi = sem("tr_hi")
        tr_lo = sem("tr_lo")
        act_ev = sem("act_ev")
        dve_ev = sem("dve_ev")
        q_out = [sem("q_out0"), sem("q_out1")]
        kc_out = [sem("kc_out0"), sem("kc_out1")]
        ks_out = sem("ks_out")
        vt = sem("vt")
        vt_hi = sem("vt_hi")
        vt_lo = sem("vt_lo")
        gexp = sem("gexp")
        own = sem("own")
        pool_own = sem("pool_own")
        c_sq = sem("c_sq")
        c_ss = sem("c_ss")
        c_ms = sem("c_ms")
        c_rt = sem("c_rt")
        c_done = sem("c_done")
        b_raw = sem("b_raw")
        b_hi = sem("b_hi")
        b_lo = sem("b_lo")
        h0 = sem("h0")
        h1 = sem("h1")
        h2 = sem("h2")
        h3 = sem("h3")
        h4 = sem("h4")
        h5 = sem("h5")
        m2 = sem("m2")
        cc_hi = sem("cc_hi")
        cc_lo = sem("cc_lo")
        qk_sel = sem("qk_sel")
        qk_wc = sem("qk_wc")
        sel_read = sem("sel_read")
        wc_read = sem("wc_read")
        exped = sem("exped")
        pt = sem("pt")
        pt_hi = sem("pt_hi")
        pt_lo = sem("pt_lo")
        pv = sem("pv")
        o_sb = sem("o_sb")
        o_tok = sem("o_tok")
        o_part = sem("o_part")
        o_done = sem("o_done")
        res_in = [sem("res_in0"), sem("res_in1")]
        gn_in = sem("gn_in")
        g2_in = sem("g2_in")
        s_sq = sem("s_sq")
        s_ms = sem("s_ms")
        s_n = sem("s_n")
        cm_hi = sem("cm_hi")
        cm_lo = sem("cm_lo")
        y_sb = sem("y_sb")
        y_tr = sem("y_tr")
        y_add = sem("y_add")
        sil = sem("sil")
        glu = sem("glu")
        g_hi = sem("g_hi")
        g_lo = sem("g_lo")
        fin = sem("fin")
        stored = sem("stored")

        block = ctx.enter_context(nc.Block())

        def raw(ap):
            return ap.bitcast(f32)

        def slot(w):
            return w % 2

        def w_of(hf, stage):
            return W_BACK + {"out": KD * hf, "glu": N_OUT + N_FFN * hf, "down": N_OUT + N_FFN * hf + 2 * FT}[stage]

        @block.sync
        def _(sp):
            def load_w(w, par, src, cols=1024):
                sp.wait_ge(w_lo, w - 1)
                sp.dma_start(wraw[:, par, 0:cols].rearrange("p (k m) -> p k m", m=src.shape[2]), src)\
                    .then_inc(w_in_sem[par], 16)

            def cols_of(k):
                if k < N_FIRST:
                    return FIRST_COLS[k]
                if k == N_IN - 1:
                    return D_IN - P
                c, n = divmod(k - N_FIRST, 3)
                return P * c + (CONV, 2 * CONV, 0)[n]

            def store(hf):
                for t in range(HT):
                    sp.wait_ge(fin, HT * hf + t + 1)
                    sp.dma_start(out_t[:, HT * hf + t, :], res[hf][:, t, :]).then_inc(stored, 16)

            sp.dma_start(xin[:, 0, :], x_t[:, 0, :]).then_inc(x_in[0], 16)
            sp.dma_start(xin[:, 1, :], x_t[:, 1, :]).then_inc(x_in[1], 16)
            sp.dma_start(g1b[:, :], norm1_g[0].partition_broadcast(P)).then_inc(vecs, 16)
            for w in range(2):
                sp.dma_start(wraw[:, w, :].rearrange("p (k m) -> p k m", m=P),
                             w_in_k[:, :, cols_of(w):cols_of(w) + P]).then_inc(w_in_sem[w], 16)
            for t in range(2, HT):
                sp.wait_ge(x_n, t - 1)
                sp.wait_ge(tr, 2 * (t - 1))
                sp.dma_start(xin[:, t % 2, :], x_t[:, t, :]).then_inc(x_in[t % 2], 16)
            with nc.allow_non_contiguous_dma(reason="small parameters, once"):
                sp.dma_start(gconv[:, :], gn_conv_g[0].rearrange("(c p) -> p c", p=P)).then_inc(vecs, 16)
                for n in range(3):
                    sp.dma_start(taps[:, n, :], conv_w[0, n].rearrange("(c p) -> p c", p=P)).then_inc(vecs, 16)
                for n in range(2):
                    sp.dma_start(pos[:, n, :], pos_k[n]).then_inc(vecs, 16)
                    for d in range(2):
                        sp.dma_start(w2d[:, n, :, d * HD:(d + 1) * HD], w2_k[n]).then_inc(vecs, 16)

            def stage_out(hf, k):
                w = N_IN * hf + k
                tok = HN * hf
                if k < QT:
                    sp.wait_ge(act_ev, ACT_EV * hf + k + 1)
                    sp.wait_ge(dve_ev, DVE_EV * hf + k + 1)
                    for r in range(2):
                        for part in range(2):
                            sp.dma_start(raw(qs[HD * part:HD * (part + 1), 2 * k + r, tok:tok + HN]),
                                         raw(qstage[HD * r:HD * (r + 1), k % 2, part, :])).then_inc(q_out[k % 2], 16)
                elif k in (8, 9):
                    n = k - 8
                    sp.wait_ge(act_ev, ACT_EV * hf + k + 1)
                    sp.wait_ge(dve_ev, DVE_EV * hf + k + 1)
                    for g in range(NKV):
                        src = kcraw[HD * g:HD * (g + 1), n, :]
                        sp.dma_start(kcs[0:HD, n, g, tok:tok + HN], src).then_inc(kc_out[n], 16)
                        skip = 1 - hf
                        sp.dma_start(kcs[HD:P, n, g, tok - 1 + skip:tok - 1 + HN], src[:, skip:HN])\
                            .then_inc(kc_out[n], 16)

            for hf in range(HALVES):
                for k in range(N_IN):
                    w = N_IN * hf + k
                    if w >= 2:
                        load_w(w, slot(w), w_in_k[:, :, cols_of(k):cols_of(k) + P])
                    if (hf, k) in ((0, 18), (0, 19), (1, 1), (1, 2)):
                        t = HT + k - 18 if hf == 0 else HT + 1 + k
                        sp.wait_ge(tr, 2 * (t - 1))
                        sp.dma_start(xin[:, t % 2, :], x_t[:, t, :]).then_inc(x_in[t % 2], 16)
                    if k >= 2:
                        stage_out(hf, k - 2)

            sp.wait_ge(w_used, HALVES * N_IN)
            sp.wait_ge(act_ev, ACT_EV * HALVES - 1)
            sp.wait_ge(dve_ev, DVE_EV * HALVES)
            for br in range(2):
                for part in range(2):
                    for g in range(NKV):
                        for d in range(2):
                            sp.dma_start(raw(ks[HD * d:HD * (d + 1), br, part, g, :]),
                                         raw(kT[HD * g:HD * (g + 1), br, part, :])).then_inc(ks_out, 16)

            for n in range(2):
                for pc in range(CMP_PC):
                    w = W_CMP + CMP_PC * n + pc
                    load_w(w, slot(w), w1_k[n][:, 4 * pc:4 * pc + 4, :])

            def out_tile(m):
                w = W_BACK + m
                c = P * (m % KD)
                load_w(w, slot(w), w_out_k[:, :, c:c + P])

            sp.wait_ge(pt, KT_BASE[UNITS - 1])
            for m in range(2):
                out_tile(m)
            sp.wait_ge(sel_read, UNITS * GQA)
            sp.wait_ge(wc_read, UNITS * GQA)
            sp.dma_start(gnsa[:, :], gn_nsa_g[0].partition_broadcast(P)).then_inc(gn_in, 16)
            sp.dma_start(res[0][:, 0:2, :], x_t[:, 0:2, :]).then_inc(res_in[0], 16)
            for m in range(2, 4):
                out_tile(m)
            sp.wait_ge(o_done, UNITS)
            sp.dma_start(res[0][:, 2:HT, :], x_t[:, 2:HT, :]).then_inc(res_in[0], 16)
            for m in range(4, 6):
                out_tile(m)
            sp.wait_ge(s_n, NT)
            sp.dma_start(res[1][:, :, :], x_t[:, HT:NT, :]).then_inc(res_in[1], 16)
            for m in range(6, KD):
                out_tile(m)
            sp.wait_ge(cm_lo, HALVES * CT)
            sp.dma_start(g2[:, :], norm2_g[0].partition_broadcast(P)).then_inc(g2_in, 16)
            sp.dma_start(gf[:, :], norm_f_g.partition_broadcast(P)).then_inc(g2_in, 16)
            w0 = w_of(1, "out")
            with sp.Fori(0, KD // 2) as mm:
                for d in range(2):
                    load_w(mm * 2 + (w0 + d), slot(w0 + d), w_out_k[:, :, ds(mm * (2 * P) + P * d, P)])

            for hf in range(HALVES):
                w0 = w_of(hf, "glu")
                with sp.Fori(0, FT) as f:
                    for d, src in enumerate((w_gate_k, w_up_k)):
                        load_w(f * 2 + (w0 + d), slot(w0 + d), src[:, :, ds(f * P, P)])
                if hf:
                    store(0)
                w0 = w_of(hf, "down")
                with sp.Fori(0, KD // 2) as mm:
                    for e in range(2):
                        for n, (k0, nk) in enumerate(PIECES):
                            d = NPC * e + n
                            load_w(mm * (2 * NPC) + (w0 + d), slot(w0 + d),
                                   w_down_k[:, k0:k0 + nk, ds(mm * (2 * P) + P * e, P)], nk * P)
            store(1)
            sp.wait_ge(stored, 16 * NT)

        @block.gpsimd
        def _(pool):
            def w_lo_of(w, par, cols=1024):
                pool.wait_ge(w_hi, w + 1)
                pool.tensor_tensor(wlo[:, par, 0:cols], wraw[:, par, 0:cols], raw(whi[:, par, 0:cols]),
                                   ALU.subtract).then_inc(w_lo, 1)

            pool.memset(ident[:, :], 0.0).then_inc(pool_own, 1)
            pool.memset(fold[:, :], 0.0).then_inc(pool_own, 1)
            pool.memset(ones[:, :], 1.0).then_inc(consts, 1)
            pool.memset(raw(kcc[:, :, :, :]), 0.0).then_inc(consts, 1)
            for c in range(CT):
                pool.memset(useq[:, c, 0:2], 0.0).then_inc(consts, 1)
            pool.wait_ge(pool_own, 2)
            pool.affine_select(out=ident[:, :], in_=ident[:, :], compare_op=ALU.not_equal, fill=1.0, base=0,
                               pattern=[[-1, P]], channel_multiplier=1).then_inc(consts, 1)
            pool.affine_select(out=fold[:, :], in_=fold[:, :], compare_op=ALU.not_equal, fill=1.0, base=0,
                               pattern=[[-1, HD]], channel_multiplier=1).then_inc(pool_own, 1)
            pool.wait_ge(pool_own, 3)
            pool.affine_select(out=fold[:, :], in_=fold[:, :], compare_op=ALU.not_equal, fill=1.0, base=-HD,
                               pattern=[[-1, HD]], channel_multiplier=1).then_inc(consts, 1)

            assert HALVES * N_IN % 2 == 0
            with pool.Fori(0, HALVES * N_IN, 2) as w:
                for d in range(2):
                    w_lo_of(w + d, d)

            pool.wait_ge(act_ev, ACT_EV * HALVES)
            pool.wait_ge(dve_ev, DVE_EV * HALVES)
            pool.wait_ge(vt, 3 * HALVES)
            pool.wait_ge(kc_out[0], 64 * HALVES)
            pool.wait_ge(kc_out[1], 64 * HALVES)
            pool.iota(dsel[:, :], pattern=[[1, SEQ]], base=P - SEQ, channel_multiplier=-1,
                      allow_small_or_imprecise_dtypes=True).then_inc(pool_own, 1)
            pool.iota(dwin[:, :], pattern=[[1, WINDOW + P]], base=-WINDOW, channel_multiplier=-1,
                      allow_small_or_imprecise_dtypes=True).then_inc(pool_own, 1)
            pool.iota(dcmp[:, :, :], pattern=[[-P, NT], [CMP_STRIDE, NC]], base=CMP_BLOCK - 1,
                      channel_multiplier=-1, allow_small_or_imprecise_dtypes=True).then_inc(pool_own, 1)
            pool.wait_ge(pool_own, 6)
            pool.affine_select(out=dsel[:, :], in_=dsel[:, :], compare_op=ALU.is_ge, fill=MASKED,
                               base=SEQ - P, pattern=[[-1, SEQ]], channel_multiplier=1).then_inc(consts, 1)
            pool.affine_select(out=dwin[:, :], in_=dwin[:, :], compare_op=ALU.is_ge, fill=MASKED,
                               base=WINDOW, pattern=[[-1, WINDOW + P]], channel_multiplier=1).then_inc(pool_own, 1)
            pool.affine_select(out=dcmp[:, :, :], in_=dcmp[:, :, :], compare_op=ALU.is_ge, fill=MASKED,
                               base=1 - CMP_BLOCK, pattern=[[P, NT], [-CMP_STRIDE, NC]],
                               channel_multiplier=1).then_inc(consts, 1)
            pool.wait_ge(pool_own, 7)
            pool.affine_select(out=dwin[:, :], in_=dwin[:, :], compare_op=ALU.is_ge, fill=MASKED,
                               base=-1, pattern=[[1, WINDOW + P]], channel_multiplier=-1).then_inc(consts, 1)

            for w in range(W_CMP, W_BACK):
                w_lo_of(w, slot(w))

            def conv_lo(hf, c):
                pool.wait_ge(cm_hi, CT * hf + c + 1)
                pool.tensor_tensor(mlo[:, hf, c, :], convT[:, c, HN * hf:HN * (hf + 1)], raw(mhi[:, hf, c, :]),
                                   ALU.subtract).then_inc(cm_lo, 1)

            for u in range(UNITS):
                if u == UNITS - 1:
                    for c in range(CT):
                        conv_lo(0, c)
                    for w in range(W_BACK, W_BACK + 2):
                        w_lo_of(w, slot(w))
                i, g = divmod(u, NKV)
                o = nsa[:, i, GQA * HD * g:GQA * HD * (g + 1)]
                pool.wait_ge(o_part, NBR * (u + 1))
                pool.tensor_tensor(o, parts[:, u % 2, 2, :], parts[:, u % 2, 0, :], ALU.add).then_inc(pool_own, 1)
                pool.wait_ge(pool_own, 8 + u)
                pool.tensor_tensor(o, o, parts[:, u % 2, 1, :], ALU.add).then_inc(o_done, 1)

            for m in range(2, KD):
                w_lo_of(W_BACK + m, slot(W_BACK + m))
                if m >= CT:
                    pool.wait_ge(s_n, NT)
                    conv_lo(1, m - CT)
            with pool.Fori(KD, N_OUT, 2) as k:
                for d in range(2):
                    w_lo_of(k + (W_BACK + d), slot(W_BACK + d))
            for hf in range(HALVES):
                w0 = w_of(hf, "glu")
                with pool.Fori(0, 2 * FT, 2) as k:
                    for d in range(2):
                        w_lo_of(k + (w0 + d), slot(w0 + d))
                w0 = w_of(hf, "down")
                with pool.Fori(0, KD // 2) as mm:
                    for e in range(2):
                        for n, (_, nk) in enumerate(PIECES):
                            d = NPC * e + n
                            w_lo_of(mm * (2 * NPC) + (w0 + d), slot(w0 + d), nk * P)

        @block.scalar
        def _(act):
            def w_hi_of(w, par, pairs, cols=1024):
                act.wait_ge(w_in_sem[par], pairs * 16)
                act.activation(whi[:, par, 0:cols], wraw[:, par, 0:cols], ACT.Copy).then_inc(w_hi, 1)

            def next_w(w, pairs, cols=1024, par=None):
                act.wait_ge(w_used, w - 1)
                w_hi_of(w, slot(w) if par is None else par, pairs, cols)

            def norm_tile(hf, t, n):
                act.wait_ge(x_in[n % 2], 16 * (n // 2 + 1))
                act.activation(junk1[:, :], xin[:, n % 2, :], ACT.Square, accum_out=ssq[:, n:n + 1])\
                    .then_inc(x_sq, 1)
                act.wait_ge(x_ms, 2 * n + 1)
                act.activation(rms[:, n:n + 1], ssq[:, n:n + 1], ACT.Sqrt).then_inc(x_sq, 1)

            def norm_hi(t, n):
                for b in range(2):
                    act.wait_ge(tr, 2 * n + b + 1)
                    act.activation(uhi[:, 4 * b:4 * b + 4, P * t:P * (t + 1)],
                                   psum[:, 2 * (n % 2) + b, :].rearrange("p (k m) -> p k m", m=P),
                                   ACT.Copy).then_inc(tr_hi, 1)

            w_hi_of(0, 0, 1)
            act.wait_ge(own, NH)
            for hf in range(HALVES):
                if hf:
                    act.wait_ge(w_used, N_IN * hf)
                for t in range(HT):
                    n = HT * hf + t
                    if n:
                        act.wait_ge(x_sq, 2 * n)
                    norm_tile(hf, t, n)
                    if t:
                        norm_hi(t - 1, n - 1)
                norm_hi(HT - 1, HT * hf + HT - 1)

                w0, e0, tok = N_IN * hf, ACT_EV * hf, HN * hf
                for k in range(QT):
                    w = w0 + k
                    next_w(w + 1, (w + 1) // 2 + 1)
                    act.wait_ge(w_used, w + 1)
                    uses = 2 * hf + k // 2
                    if uses:
                        act.wait_ge(q_out[k % 2], 64 * uses)
                    act.activation(qstage[:, k % 2, 0, :], psum[:, 4 + slot(w), :], ACT.Copy,
                                   scale=qscale[:, k:k + 1]).then_inc(act_ev, 1)
                for k in range(QT, QT + 2):
                    w = w0 + k
                    next_w(w + 1, (w + 1) // 2 + 1)
                    act.wait_ge(w_used, w + 1)
                    act.activation(kT[:, k - QT, 0, tok:tok + HN], psum[:, 4 + slot(w), :],
                                   ACT.Copy).then_inc(act_ev, 1)
                for k in range(QT + 2, N_FIRST):
                    w = w0 + k
                    next_w(w + 1, (w + 1) // 2 + 1)
                    act.wait_ge(w_used, w + 1)
                    dst = vraw if k < QT + 4 else kcraw
                    if hf and k >= QT + 4:
                        act.wait_ge(kc_out[k % 2], 64)
                    act.activation(dst[0:HD, k % 2, :], psum[0:HD, 4 + slot(w), :],
                                   ACT.Copy).then_inc(act_ev, 1)
                for c in range(CT):
                    for n in range(3):
                        w = w0 + N_FIRST + 3 * c + n
                        next_w(w + 1, (w + 1) // 2 + 1)
                        if n == 0:
                            act.wait_ge(w_used, w + 1)
                            act.wait_ge(dve_ev, DVE_EV * hf + N_FIRST + 2 * c)
                            act.activation(ccs[:, :], psum[:, 4 + slot(w), :], ACT.Copy).then_inc(act_ev, 1)
                w = w0 + N_IN - 1
                if w + 1 < W_BACK:
                    next_w(w + 1, (w + 1) // 2 + 1)
                act.wait_ge(w_used, w + 1)
                act.activation(graw[:, :], psum[:, 4 + slot(w), :], ACT.Copy).then_inc(act_ev, 1)

                for br in range(2):
                    act.wait_ge(vt, 3 * hf + br + 1)
                    act.activation(vs[:, br, HT * hf:HT * (hf + 1), :, 0:HD],
                                   psum[:, 6 + br, :].rearrange("p (t g d) -> p t g d", t=HT, g=NKV),
                                   ACT.Copy).then_inc(vt_hi, 1)
                act.wait_ge(vt, 3 * hf + 3)
                act.activation(gates[:, HT * hf:HT * (hf + 1), :],
                               psum[:, 6, :].rearrange("p (t m) -> p t m", m=P)[:, :, GATE0:P],
                               ACT.Exp, scale=-1.0).then_inc(gexp, 1)

            act.wait_ge(dve_ev, DVE_EV * HALVES)
            for n in range(HALVES * CT):
                hf, c = divmod(n, CT)
                if n >= 2:
                    act.wait_ge(c_ss, n - 1)
                act.activation(csq[:, n % 2, :], convT[:, c, HN * hf:HN * (hf + 1)], ACT.Square)\
                    .then_inc(c_sq, 1)
            for hf in range(HALVES):
                act.wait_ge(c_ms, hf + 1)
                act.activation(crms[:, HN * hf:HN * (hf + 1)], crms[:, HN * hf:HN * (hf + 1)], ACT.Sqrt)\
                    .then_inc(c_rt, 1)

            for n in range(2):
                act.wait_ge(b_raw, n + 1)
                if n:
                    act.wait_ge(w_used, W_CMP + CMP_PC)
                act.activation(bhi[:, :, :], blk[:, :, :], ACT.Copy).then_inc(b_hi, 1)
                for pc in range(CMP_PC):
                    w = W_CMP + CMP_PC * n + pc
                    if w + 1 < W_BACK:
                        next_w(w + 1, (w + 1) // 2 + 1)
                act.wait_ge(w_used, W_CMP + CMP_PC * (n + 1))
                act.activation(hid[0:NB, 0, :], psum[0:NB, n, 0:CMP_HID], ACT.Copy).then_inc(h0, 1)
                act.wait_ge(h1, n + 1)
                act.activation(hid[0:NB, 2, :], hid[0:NB, 1, :], ACT.Tanh, scale=(2 / 3.141592653589793) ** 0.5)\
                    .then_inc(h2, 1)
                act.wait_ge(h4, n + 1)
                act.activation(hidT[:, :, :], psum[:, 2, 0:2 * NB].rearrange("p (t m) -> p t m", t=2),
                               ACT.Copy, scale=0.5).then_inc(h5, 1)
                act.wait_ge(m2, n + 1)
                if n == 0:
                    act.activation(kcc[:, 0, :, 0:NC], psum[:, 3, 0:NB].rearrange("p (g m) -> p g m", g=NKV),
                                   ACT.Copy).then_inc(cc_hi, 1)
                else:
                    act.activation(vcc[0:NC, :, 0:HD],
                                   psum[0:NC, 3, 0:P].rearrange("p (g d) -> p g d", g=NKV),
                                   ACT.Copy).then_inc(cc_hi, 1)

            def exp_item(m):
                n, wc = divmod(m, 2)
                i, s = n // GQA // NKV, slot_of(n)
                n_sel, n_win = P * (i + 1), P * min(i + 1, WIN_T + 1)
                act.wait_ge(wc_read if wc else sel_read, n + 1)
                cols = ((WIN, n_sel, n_win), (CMP, n_sel + n_win, NC)) if wc else ((SEL, 0, n_sel),)
                for br, c0, cn in cols:
                    ins = act.activation(probs[:, s, c0:c0 + cn], probs[:, s, c0:c0 + cn], ACT.Exp, scale=-1.0,
                                         bias=nmax[:, s, br:br + 1], accum_out=rsum[:, s, br:br + 1])
                ins.then_inc(exped, 1)

            def outputs(g):
                act.wait_ge(pv, GROUP_END[g] + 1)
                act.activation(osb[:, g % 2, :], psum[:, 6 + g % 2, :], ACT.Copy).then_inc(o_sb, 1)

            def hi_tile(kt):
                rows = rows_of(kt)
                act.wait_ge(pt, kt + 1)
                if kt >= 3:
                    act.wait_ge(pv, kt - 2)
                act.activation(pthi[kt % 3][0:rows, :], psum[0:rows, 4 + kt % 2, :], ACT.Copy)\
                    .then_inc(pt_hi, 1)
                for g in groups_ending(kt - LAG):
                    outputs(g)

            def square(k, src, col, junk):
                if k:
                    act.wait_ge(s_sq, k)
                act.activation(junk, src, ACT.Square, accum_out=ssq[:, col:col + 1]).then_inc(s_sq, 1)

            def root(ms, c0, c1):
                act.wait_ge(s_ms, ms)
                act.activation(rms[:, c0:c1], ssq[:, c0:c1], ACT.Sqrt).then_inc(s_sq, 1)

            def conv_hi(hf, c):
                act.activation(mhi[:, hf, c, :], convT[:, c, HN * hf:HN * (hf + 1)], ACT.Copy).then_inc(cm_hi, 1)

            def nsa_hi(t):
                act.wait_ge(tr, TR_NSA + t + 1)
                c = P * (t % HT)
                act.activation(mhi[:, t // HT, CT:KD, c:c + P], psum[:, t % 2, :].rearrange("p (k m) -> p k m", m=P),
                               ACT.Copy).then_inc(tr_hi, 1)

            def beside_last(b):
                if b == 0:
                    root(1, 0, NT - 1)
                    act.wait_ge(qk_wc, UNITS * GQA)
                if 1 <= b <= CT:
                    conv_hi(0, b - 1)
                if 3 <= b < 3 + HT:
                    nsa_hi(b - 3)
                if b in (7, 8):
                    w = W_BACK + b - 7
                    next_w(w, w // 2 + 1)

            for m in range(ITEMS):
                exp_item(m)
            for u in range(UNITS):
                for b in range(BEATS):
                    for kt in beat_tiles(u, b):
                        hi_tile(kt)
                    if b < ITEMS and u + 1 < UNITS:
                        exp_item(ITEMS * (u + 1) + b)
                    if u == UNITS - 1:
                        beside_last(b)
                if u >= NKV and u % NKV == 0:
                    i = u // NKV - 1
                    act.wait_ge(o_done, u)
                    square(i, nsa[:, i, :], i, junk2[:, :])
            for kt in range(N_KT - LAG, N_KT):
                for g in groups_ending(kt):
                    outputs(g)

            def copy_y(n, par, bank):
                act.wait_ge(y_tr, n - 1)
                act.activation(yT[:, par, :], psum[:, bank, :], ACT.Copy).then_inc(y_sb, 1)

            def h_square(k, src, t):
                square(sq_base(k) + t, src[:, t, :], HT * (k % 2) + t, nrm[:, 1, :])

            def h_root(k):
                c0 = HT * (k % 2)
                root(ms_base(k) + 1, c0, c0 + HT)

            def h_hi(hf, t):
                for b in range(2):
                    act.wait_ge(tr, tr_h(hf) + 2 * t + b + 1)
                    act.activation(vhi[:, 4 * b:4 * b + 4, P * t:P * (t + 1)],
                                   psum[:, 2 * (t % 2) + b, :].rearrange("p (k m) -> p k m", m=P),
                                   ACT.Copy).then_inc(tr_hi, 1)

            for n in range(N_OUT):
                w = W_BACK + n
                if n:
                    next_w(w + 1, (w + 1) // 2 + 1)
                act.wait_ge(w_used, w + 1)
                if n >= 2:
                    copy_y(n, n % 2, 4 + n % 2)
                else:
                    act.activation(yT[:, n, :], psum[:, 4 + n, :], ACT.Copy).then_inc(y_sb, 1)
                if n == 0:
                    act.wait_ge(o_done, UNITS)
                    square(NT, nsa[:, NT - 1, :], NT - 1, junk3[:, :])
                if n == 1:
                    root(3, NT - 1, NT)
                if 2 <= n < 2 + HT:
                    nsa_hi(n + 2)
                if n < CT:
                    conv_hi(1, n)
                if n in (KD + 2, KD + 3):
                    act.wait_ge(y_add, KD)
                    act.wait_ge(cm_lo, HALVES * CT)
                    for t in (0, 1) if n == KD + 2 else (2, 3):
                        h_square(0, res[0], t)
                if n == KD + 4:
                    h_root(0)
                if n >= N_OUT - 2:
                    for t in (0, 1) if n == N_OUT - 2 else (2, 3):
                        h_hi(0, t)

            for hf in range(HALVES):
                w0, f0 = w_of(hf, "glu"), FT * hf

                def silu_of(f, par):
                    act.activation(silu[:, par, :], psum[:, 2 * par, :], ACT.Silu).then_inc(sil, 1)

                def glu_step(f, par, first):
                    a = w0 + 1
                    act.wait_ge(w_used, f * 2 + (a - 1))
                    w_hi_of(f * 2 + a, slot(a), f + (a // 2 + 1))
                    if not first:
                        silu_of(f - 1, 1 - par)
                    b = w0 + 2
                    act.wait_ge(w_used, f * 2 + (b - 1))
                    w_hi_of(f * 2 + b, slot(b), f + (b // 2 + 1))
                    if not first:
                        act.wait_ge(glu, f + f0)
                        act.activation(hhi[:, ds(f - 1, 1), :],
                                       silu[:, 1 - par:2 - par, :], ACT.Copy).then_inc(g_hi, 1)

                glu_step(0, 0, True)
                if hf:
                    act.wait_ge(y_add, N_OUT + KD)
                    for t in range(HT):
                        h_square(2, res[0], t)
                    h_root(2)
                glu_step(1, 1, False)
                with act.Fori(2, FT, 2) as f:
                    for d in range(2):
                        act.wait_ge(g_lo, f + (f0 + d - 2))
                        glu_step(f + d, d, False)
                act.wait_ge(w_used, w0 + 2 * FT)
                act.wait_ge(g_lo, f0 + FT - 2)
                silu_of(FT - 1, 1)
                act.wait_ge(glu, f0 + FT)
                act.activation(hhi[:, FT - 1, :], silu[:, 1, :], ACT.Copy).then_inc(g_hi, 1)

                w0, y0 = w_of(hf, "down"), N_OUT + KD * hf
                act.wait_ge(g_lo, f0 + FT)
                last_w = w0 + NPC * KD - 1
                with act.Fori(0, KD // 2 - 1) as mm:
                    for e in range(2):
                        for n in range(NPC):
                            d = NPC * e + n + 1
                            nk = PIECES[(n + 1) % NPC][1]
                            act.wait_ge(w_used, mm * (2 * NPC) + (w0 + d - 1))
                            w_hi_of(mm * (2 * NPC) + (w0 + d), slot(w0 + d), mm * NPC + ((w0 + d) // 2 + 1), nk * P)
                        act.wait_ge(w_used, mm * (2 * NPC) + (w0 + NPC * (e + 1)))
                        copy_y(mm * 2 + (y0 + e), e, 4 + e)
                for e in range(2):
                    for n in range(NPC):
                        w = w0 + NPC * (KD - 2 + e) + n + 1
                        if w < W_END:
                            next_w(w, w // 2 + 1, PIECES[(n + 1) % NPC][1] * P if w <= last_w else 1024)
                        if hf == 0 and e == 0:
                            if n < 2:
                                for t in (2 * n, 2 * n + 1):
                                    h_square(1, res[1], t)
                            else:
                                h_root(1)
                    act.wait_ge(w_used, w0 + NPC * (KD - 2 + e + 1))
                    copy_y(y0 + KD - 2 + e, e, 4 + e)
                    if hf == 0:
                        for t in (2 * e, 2 * e + 1):
                            h_hi(1, t)
            act.wait_ge(y_add, N_OUT + 2 * KD)
            for t in range(HT):
                h_square(3, res[1], t)
            h_root(3)

        @block.tensor
        def _(pe):
            def mm3(bank_ap, w_ap_hi, w_ap_lo, x_hi, x_lo, first, last):
                pe.matmul(bank_ap, w_ap_hi, x_hi, start=first, stop=False)
                pe.matmul(bank_ap, w_ap_hi, x_lo, start=False, stop=False)
                return pe.matmul(bank_ap, w_ap_lo, x_hi, start=False, stop=last)

            def dense(par, bank, xh, xl, k0=0, nk=KD, first=True, last=True):
                for k in range(nk):
                    c = slice(P * k, P * (k + 1))
                    ins = mm3(psum[:, bank, :], whi[:, par, c], wlo[:, par, c], xh[:, k0 + k, :], xl[:, k0 + k, :],
                              first and k == 0, last and k == nk - 1)
                return ins

            pe.wait_ge(consts, CONSTS_FIRST)
            for hf in range(HALVES):
                for t in range(HT):
                    n = HT * hf + t
                    pe.wait_ge(x_n, n + 1)
                    for b in range(2):
                        if n >= 2:
                            pe.wait_ge(tr_lo, 2 * (n - 2) + b + 1)
                        for k in range(4):
                            ins = pe.transpose(psum[:, 2 * (n % 2) + b, P * k:P * (k + 1)],
                                               xin[:, n % 2, P * (4 * b + k):P * (4 * b + k + 1)], ident[:, :])
                        ins.then_inc(tr, 1)
                pe.wait_ge(tr_hi, 2 * HT * (hf + 1))
                pe.wait_ge(tr_lo, 2 * HT * (hf + 1))
                w0 = N_IN * hf
                A0, D0 = ACT_EV * hf, DVE_EV * hf
                if hf:
                    pe.wait_ge(act_ev, A0)
                    pe.wait_ge(dve_ev, D0)
                for k in range(2):
                    pe.wait_ge(w_lo, w0 + k + 1)
                    dense(slot(w0 + k), 4 + slot(w0 + k), uhi, ulo).then_inc(w_used, 1)
                with pe.Fori(2, N_FIRST, 2) as k:
                    for d in range(2):
                        pe.wait_ge(w_lo, k + (w0 + d + 1))
                        pe.wait_ge(act_ev, k + (A0 + d - 1))
                        pe.wait_ge(dve_ev, k + (D0 + d - 1))
                        dense(slot(w0 + d), 4 + slot(w0 + d), uhi, ulo).then_inc(w_used, 1)
                pe.wait_ge(act_ev, A0 + N_FIRST)
                with pe.Fori(0, CT, 2) as c:
                    for e in range(2):
                        for n in range(3):
                            d = 3 * e + n
                            wd = w0 + N_FIRST + d
                            pe.wait_ge(w_lo, c * 3 + (wd + 1))
                            if n == 0:
                                pe.wait_ge(dve_ev, c * 2 + (D0 + N_FIRST + 2 * e - 1))
                            elif n == 1:
                                pe.wait_ge(dve_ev, c * 2 + (D0 + N_FIRST + 2 * e))
                            else:
                                pe.wait_ge(act_ev, c + (A0 + N_FIRST + e + 1))
                            dense(slot(wd), 4 + slot(wd), uhi, ulo).then_inc(w_used, 1)
                w = w0 + N_IN - 1
                pe.wait_ge(w_lo, w + 1)
                pe.wait_ge(dve_ev, D0 + DVE_EV - 1)
                dense(slot(w), 4 + slot(w), uhi, ulo).then_inc(w_used, 1)

                pe.wait_ge(dve_ev, D0 + N_FIRST)
                for n in range(3):
                    if n == 0 and hf:
                        pe.wait_ge(gexp, hf)
                    if n == 1 and hf:
                        pe.wait_ge(vt_hi, 2 * hf)
                        pe.wait_ge(vt_lo, 2 * hf)
                    if n == 2:
                        pe.wait_ge(act_ev, A0 + ACT_EV)
                        pe.wait_ge(vt_hi, 2 * hf + 1)
                        pe.wait_ge(vt_lo, 2 * hf + 1)
                    for t in range(HT):
                        src = (vraw[:, 0, :], vraw[:, 1, :], graw[:, :])[n]
                        ins = pe.transpose(psum[:, (6, 7, 6)[n], P * t:P * (t + 1)], src[:, P * t:P * (t + 1)],
                                           ident[:, :])
                    ins.then_inc(vt, 1)

            for n in range(HALVES * CT):
                hf, c = divmod(n, CT)
                pe.wait_ge(c_sq, n + 1)
                pe.matmul(psum[:, hf, :], ones[:, :], csq[:, n % 2, :], start=c == 0, stop=c == CT - 1)\
                    .then_inc(c_ss, 1)

            for n in range(2):
                pe.wait_ge(b_lo, n + 1)
                if n == 0:
                    pe.wait_ge(c_ms, HALVES)
                for pc in range(CMP_PC):
                    w = W_CMP + CMP_PC * n + pc
                    pe.wait_ge(w_lo, w + 1)
                    for q in range(LP // CMP_PC):
                        lp = LP // CMP_PC * pc + q
                        c = slice(CMP_HID * q, CMP_HID * (q + 1))
                        o = psum[0:NB, n, 0:CMP_HID]
                        pe.matmul(o, bhi[:, lp, :], whi[:, slot(w), c], start=lp == 0, stop=False)
                        pe.matmul(o, blo[:, lp, :], whi[:, slot(w), c], start=False, stop=False)
                        ins = pe.matmul(o, bhi[:, lp, :], wlo[:, slot(w), c], start=False, stop=lp == LP - 1)
                    ins.then_inc(w_used, 1)
                pe.wait_ge(h3, n + 1)
                if n:
                    pe.wait_ge(h5, n)
                for t in range(2):
                    ins = pe.transpose(psum[:, 2, NB * t:NB * (t + 1)], hid[0:NB, 3, P * t:P * (t + 1)],
                                       ident[0:NB, 0:NB])
                ins.then_inc(h4, 1)
                pe.wait_ge(h5, n + 1)
                if n:
                    pe.wait_ge(cc_lo, n)
                if n == 0:
                    for t in range(2):
                        ins = pe.matmul(psum[:, 3, 0:NB], w2d[:, 0, t, :], hidT[:, t, :], start=t == 0, stop=t == 1)
                else:
                    for g in range(NKV):
                        for t in range(2):
                            ins = pe.matmul(psum[0:NC, 3, HD * g:HD * (g + 1)], hidT[:, t, NC * g:NC * (g + 1)],
                                            w2d[:, 1, t, 0:HD], start=t == 0, stop=t == 1)
                ins.then_inc(m2, 1)

            def scores(m):
                n, wc = divmod(m, 2)
                u, j = divmod(n, GQA)
                i, g = divmod(u, NKV)
                q = qs[:, GQA * g + j, P * i:P * (i + 1)]
                n_sel, n_win = P * (i + 1), P * min(i + 1, WIN_T + 1)

                def against(br, bank, start_key, keys):
                    for c in range(0, keys, 512):
                        cn = min(512, keys - c)
                        o = psum[:, bank + c // 512, 0:cn]
                        for part in range(2):
                            ins = pe.matmul(o, q, ks[:, br, part, g, start_key + c:start_key + c + cn],
                                            start=part == 0, stop=part == 1)
                    return ins

                if n:
                    pe.wait_ge(wc_read if wc else sel_read, n)
                if wc:
                    against(1, 2, n_sel - n_win, n_win)
                    for part in range(2):
                        ins = pe.matmul(psum[:, 3, P:P + NC + 1], q, kcc[:, part, g, :],
                                        start=part == 0, stop=part == 1)
                    ins.then_inc(qk_wc, 1)
                else:
                    against(0, 0, 0, n_sel).then_inc(qk_sel, 1)

            def transposes(kt):
                u = unit_of(kt)
                col, rows = KTS[u][kt - KT_BASE[u]][2], rows_of(kt)
                if kt == KT_BASE[u]:
                    pe.wait_ge(exped, ITEMS * (u + 1))
                if kt >= 2:
                    pe.wait_ge(pt_lo, kt - 1)
                for j in range(GQA):
                    s = slot_of(GQA * u + j)
                    ins = pe.transpose(psum[0:rows, 4 + kt % 2, P * j:P * (j + 1)], probs[:, s, col:col + rows],
                                       ident[:, :])
                ins.then_inc(pt, 1)

            def values(kt):
                u = unit_of(kt)
                br, t, _ = KTS[u][kt - KT_BASE[u]]
                g, rows, group = u % NKV, rows_of(kt), NBR * u + br
                v = vcc[0:rows, g, :] if br == 2 else vs[:, br, t, g, :]
                pe.wait_ge(pt_lo, kt + 1)
                first, last = kt == GROUP_START[group], kt == GROUP_END[group]
                if first and group >= 2:
                    pe.wait_ge(o_part, group - 1)
                o = psum[:, 6 + group % 2, :]
                pe.matmul(o, v, pthi[kt % 3][0:rows, :], start=first, stop=False)
                pe.matmul(o, v, ptlo[kt % 3][0:rows, :], start=False, stop=last).then_inc(pv, 1)
                for e in groups_ending(kt - 1):
                    folded(e)

            def folded(g):
                pe.wait_ge(o_sb, g + 1)
                for j in range(GQA):
                    ins = pe.matmul(psum[:, 6 + g % 2, HD * j:HD * (j + 1)], osb[:, g % 2, P * j:P * (j + 1)],
                                    fold[:, :], start=True, stop=True)
                ins.then_inc(o_tok, 1)

            pe.wait_ge(consts, CONSTS_ALL)
            pe.wait_ge(ks_out, 16 * 16)
            for k in range(2):
                pe.wait_ge(q_out[k], 64 * HALVES * QT // 2)
            pe.wait_ge(cc_lo, 2)
            pe.wait_ge(vt_lo, 2 * HALVES)
            pe.wait_ge(vt_hi, 2 * HALVES)
            for m in range(ITEMS + 1):
                scores(m)
            def nsa_turn(t):
                pe.wait_ge(s_n, t + 1)
                pe.wait_ge(tr_lo, TR_NSA + t - 1)
                for k in range(CT):
                    ins = pe.transpose(psum[:, t % 2, P * k:P * (k + 1)],
                                       nnsa[t // HT][:, t % 2, P * k:P * (k + 1)], ident[:, :])
                ins.then_inc(tr, 1)

            for u in range(UNITS):
                for b in range(BEATS):
                    m = ITEMS * (u + 1) + b + 1
                    if b < ITEMS and m < N_ITEMS:
                        scores(m)
                    for kt in beat_tiles(u, b):
                        transposes(kt)
                        if kt >= LAG:
                            values(kt - LAG)
                    if u == UNITS - 1 and 2 <= b < 2 + HT:
                        nsa_turn(b - 2)
            for kt in range(N_KT - LAG, N_KT):
                values(kt)

            def turn(n, par):
                pe.wait_ge(y_sb, n + 1)
                for t in range(HT):
                    ins = pe.transpose(psum[:, 6 + par, P * t:P * (t + 1)], yT[:, par, P * t:P * (t + 1)],
                                       ident[:, :])
                ins.then_inc(y_tr, 1)

            def project(n, par, hf):
                pe.wait_ge(w_lo, n + (W_BACK + 1))
                dense(slot(W_BACK + par), 4 + par, mhi[:, hf], mlo[:, hf]).then_inc(w_used, 1)

            def h_turn(hf, t):
                pe.wait_ge(s_n, NT + HT * hf + t + 1)
                for b in range(2):
                    n = tr_h(hf) + 2 * t + b
                    pe.wait_ge(tr_lo, n - 3 if t >= 2 else tr_h(hf))
                    for k in range(4):
                        ins = pe.transpose(psum[:, 2 * (t % 2) + b, P * k:P * (k + 1)],
                                           nrm[:, t % 2, P * (4 * b + k):P * (4 * b + k + 1)], ident[:, :])
                    ins.then_inc(tr, 1)

            pe.wait_ge(tr_lo, TR_NSA + HT)
            pe.wait_ge(tr_hi, TR_NSA + HT)
            pe.wait_ge(cm_lo, CT)
            project(0, 0, 0)
            for g in groups_ending(N_KT - 1):
                folded(g)
            project(1, 1, 0)
            for n in range(2, KD):
                pe.wait_ge(y_sb, n - 1)
                project(n, n % 2, 0)
                if n < 4:
                    pe.wait_ge(o_part, NBR * UNITS)
                else:
                    pe.wait_ge(y_add, n - 3)
                turn(n - 2, n % 2)
                if n < 2 + HT:
                    nsa_turn(n + 2)
            pe.wait_ge(tr_lo, TR_NSA + NT)
            pe.wait_ge(tr_hi, TR_NSA + NT)
            pe.wait_ge(cm_lo, HALVES * CT)

            def out_step(n, par):
                pe.wait_ge(y_sb, n - 1)
                project(n, par, 1)
                pe.wait_ge(y_add, n - 3)
                turn(n - 2, par)

            with pe.Fori(KD, N_OUT - 2, 2) as n:
                for d in range(2):
                    out_step(n + d, d)
            for e in range(2):
                out_step(N_OUT - 2 + e, e)
                for t in (2 * e, 2 * e + 1):
                    h_turn(0, t)
            for e in range(2):
                pe.wait_ge(y_add, N_OUT - 3 + e)
                turn(N_OUT - 2 + e, e)

            for hf in range(HALVES):
                pe.wait_ge(tr_hi, tr_h(hf) + 2 * HT)
                pe.wait_ge(tr_lo, tr_h(hf) + 2 * HT)
                w0, f0 = w_of(hf, "glu"), FT * hf
                for f in range(2):
                    for d in range(2):
                        pe.wait_ge(w_lo, w0 + 2 * f + d + 1)
                        dense(slot(w0 + d), 2 * f + d, vhi, vlo).then_inc(w_used, 1)
                with pe.Fori(2, FT, 2) as f:
                    for e in range(2):
                        pe.wait_ge(glu, f + (f0 + e - 1))
                        for d in range(2):
                            pe.wait_ge(w_lo, f * 2 + (w0 + 2 * e + d + 1))
                            dense(slot(w0 + d), 2 * e + d, vhi, vlo).then_inc(w_used, 1)
                pe.wait_ge(g_lo, f0 + FT)
                pe.wait_ge(g_hi, f0 + FT)

                w0, y0 = w_of(hf, "down"), N_OUT + KD * hf

                def down(m, e):
                    pe.wait_ge(y_sb, m + (y0 + e - 1))
                    for n, (k0, nk) in enumerate(PIECES):
                        d = NPC * e + n
                        pe.wait_ge(w_lo, m * NPC + (w0 + d + 1))
                        dense(slot(w0 + d), 4 + e, hhi, hlo, k0, nk, n == 0, n == NPC - 1).then_inc(w_used, 1)

                def down_step(m, e):
                    down(m, e)
                    pe.wait_ge(y_add, m + (y0 + e - 3))
                    turn(m + (y0 + e - 2), e)

                for e in range(2):
                    down(0, e)
                with pe.Fori(2, KD if hf else KD - 2, 2) as m:
                    for e in range(2):
                        down_step(m, e)
                if hf == 0:
                    for e in range(2):
                        down_step(KD - 2, e)
                        for t in (2 * e, 2 * e + 1):
                            h_turn(1, t)
                for e in range(2):
                    pe.wait_ge(y_add, y0 + KD - 3 + e)
                    turn(y0 + KD - 2 + e, e)

        @block.vector
        def _(dve):
            class Own:
                n = 0

            def did(ins):
                ins.then_inc(own, 1)
                Own.n += 1

            def settle():
                dve.wait_ge(own, Own.n)

            for h in range(NH):
                did(dve.memset(qscale[HD * (h % 2):HD * (h % 2 + 1), h // 2:h // 2 + 1],
                               HD ** -0.5 * 2.0 ** (h + 1)))
            dve.wait_ge(consts, CONSTS_FIRST)
            for hf in range(HALVES):
                def norm_tile(t):
                    n = HT * hf + t
                    dve.wait_ge(x_sq, 2 * n + 1)
                    dve.tensor_scalar(ssq[:, n:n + 1], ssq[:, n:n + 1], 1.0 / DM, EPS, ALU.mult, ALU.add)\
                        .then_inc(x_ms, 1)
                    dve.wait_ge(x_sq, 2 * n + 2)
                    dve.reciprocal(inv[:, n:n + 1], rms[:, n:n + 1]).then_inc(x_ms, 1)
                    dve.wait_ge(x_ms, 2 * n + 2)
                    if n == 0:
                        dve.wait_ge(vecs, 16)
                    dve.scalar_tensor_tensor(xin[:, n % 2, :], xin[:, n % 2, :], inv[:, n:n + 1], g1b[:, :],
                                             ALU.mult, ALU.mult).then_inc(x_n, 1)

                def norm_lo(t):
                    n = HT * hf + t
                    for b in range(2):
                        dve.wait_ge(tr_hi, 2 * n + b + 1)
                        sl = (slice(None), slice(4 * b, 4 * b + 4), slice(P * t, P * (t + 1)))
                        dve.tensor_tensor(ulo[sl], psum[:, 2 * (n % 2) + b, :].rearrange("p (k m) -> p k m", m=P),
                                          raw(uhi[sl]), ALU.subtract).then_inc(tr_lo, 1)

                if hf:
                    dve.wait_ge(w_used, N_IN * hf)
                for t in range(HT):
                    norm_tile(t)
                    if t:
                        norm_lo(t - 1)
                norm_lo(HT - 1)

                w0, tok = N_IN * hf, HN * hf
                for k in range(QT):
                    w = w0 + k
                    dve.wait_ge(act_ev, ACT_EV * hf + k + 1)
                    dve.scalar_tensor_tensor(qstage[:, k % 2, 1, :], psum[:, 4 + slot(w), :], qscale[:, k:k + 1],
                                             raw(qstage[:, k % 2, 0, :]), ALU.mult, ALU.subtract).then_inc(dve_ev, 1)
                for k in range(QT, QT + 2):
                    w = w0 + k
                    dve.wait_ge(act_ev, ACT_EV * hf + k + 1)
                    dve.tensor_tensor(kT[:, k - QT, 1, tok:tok + HN], psum[:, 4 + slot(w), :],
                                      raw(kT[:, k - QT, 0, tok:tok + HN]), ALU.subtract).then_inc(dve_ev, 1)
                for k in range(QT + 2, N_FIRST):
                    w = w0 + k
                    dve.wait_ge(w_used, w + 1)
                    dst = vraw if k < QT + 4 else kcraw
                    if hf and k >= QT + 4:
                        dve.wait_ge(kc_out[k % 2], 64)
                    dve.tensor_copy(dst[HD:P, k % 2, :], psum[HD:P, 4 + slot(w), :]).then_inc(dve_ev, 1)
                if hf == 0:
                    dve.wait_ge(vecs, VECS)
                for c in range(CT):
                    w = w0 + N_FIRST + 3 * c
                    dve.wait_ge(act_ev, ACT_EV * hf + N_FIRST + c + 1)
                    dve.wait_ge(w_used, w + 2)
                    dve.tensor_tensor(useq[:, c, 2:HN + 2], psum[:, 4 + slot(w + 1), :], ccs[:, :], ALU.mult)\
                        .then_inc(dve_ev, 1)
                    dve.wait_ge(dve_ev, DVE_EV * hf + N_FIRST + 2 * c + 1)
                    did(dve.tensor_scalar(cacc[:, :], useq[:, c, 0:HN], taps[:, 0, c:c + 1], None, ALU.mult))
                    for n in (1, 2):
                        settle()
                        did(dve.scalar_tensor_tensor(cacc[:, :], useq[:, c, n:n + HN], taps[:, n, c:c + 1],
                                                     cacc[:, :], ALU.mult, ALU.add))
                    if hf == 0:
                        settle()
                        did(dve.tensor_copy(useq[:, c, 0:2], useq[:, c, HN:HN + 2]))
                    dve.wait_ge(w_used, w + 3)
                    settle()
                    dve.tensor_tensor(convT[:, c, tok:tok + HN], cacc[:, :], psum[:, 4 + slot(w + 2), :],
                                      ALU.mult).then_inc(dve_ev, 1)
                    dve.wait_ge(dve_ev, DVE_EV * hf + N_FIRST + 2 * c + 2)

                for br in range(2):
                    dve.wait_ge(vt_hi, 2 * hf + br + 1)
                    tt = slice(HT * hf, HT * (hf + 1))
                    dve.tensor_tensor(vs[:, br, tt, :, HD:2 * HD],
                                      psum[:, 6 + br, :].rearrange("p (t g d) -> p t g d", t=HT, g=NKV),
                                      raw(vs[:, br, tt, :, 0:HD]), ALU.subtract).then_inc(vt_lo, 1)
                dve.wait_ge(gexp, hf + 1)
                g_ap = gates[:, HT * hf:HT * (hf + 1), :]
                did(dve.tensor_scalar(g_ap, g_ap, 1.0, None, ALU.add))
                settle()
                did(dve.reciprocal(g_ap, g_ap))

            for hf in range(HALVES):
                dve.wait_ge(c_ss, CT * (hf + 1))
                dve.tensor_scalar(crms[:, HN * hf:HN * (hf + 1)], psum[:, hf, :], 1.0 / CONV, EPS,
                                  ALU.mult, ALU.add).then_inc(c_ms, 1)

            def norm_conv():
                for hf in range(HALVES):
                    cr = crms[:, HN * hf:HN * (hf + 1)]
                    dve.wait_ge(c_rt, hf + 1)
                    did(dve.reciprocal(cr, cr))
                    settle()
                    for c in range(CT):
                        ct = convT[:, c, HN * hf:HN * (hf + 1)]
                        dve.scalar_tensor_tensor(ct, ct, gconv[:, c:c + 1], cr, ALU.mult, ALU.mult)\
                            .then_inc(c_done, 1)

            for n in range(2):
                dve.wait_ge(kc_out[n], 64 * HALVES)
                if n == 0:
                    for k in range(2):
                        dve.wait_ge(q_out[k], 64 * HALVES * QT // 2)
                if n:
                    dve.wait_ge(b_hi, n)
                    dve.wait_ge(b_lo, n)
                for g in range(NKV):
                    src = kcs[:, n, g, 0:CMP_STRIDE * (NC - 1) + CMP_BLOCK]\
                        .rearrange("p (b l) -> p l b", l=CMP_STRIDE)
                    for part in range(2):
                        lh = LP // 2
                        o = blk[:, lh * part:lh * (part + 1), NC * g:NC * (g + 1)]
                        i0 = src[:, 0:CMP_STRIDE:2, part:part + NC]
                        i1 = pos[:, n, lh * part:lh * (part + 1)].unsqueeze(2).broadcast_to([P, lh, NC])
                        ins = dve.tensor_tensor(o, i0, i1, ALU.add)
                        if g == NKV - 1 and part == 1:
                            ins.then_inc(b_raw, 1)
                        else:
                            did(ins)
                settle()
                dve.wait_ge(b_hi, n + 1)
                if n:
                    dve.wait_ge(w_used, W_CMP + CMP_PC)
                dve.tensor_tensor(blo[:, :, :], blk[:, :, :], raw(bhi[:, :, :]), ALU.subtract).then_inc(b_lo, 1)
                dve.wait_ge(h0, n + 1)
                h = hid[0:NB]
                did(dve.tensor_tensor(h[:, 1, :], h[:, 0, :], h[:, 0, :], ALU.mult))
                settle()
                did(dve.tensor_scalar(h[:, 1, :], h[:, 1, :], 0.044715, 1.0, ALU.mult, ALU.add))
                settle()
                dve.tensor_tensor(h[:, 1, :], h[:, 1, :], h[:, 0, :], ALU.mult).then_inc(h1, 1)
                dve.wait_ge(h2, n + 1)
                dve.scalar_tensor_tensor(h[:, 3, :], h[:, 2, :], 1.0, h[:, 0, :], ALU.add, ALU.mult).then_inc(h3, 1)
                dve.wait_ge(cc_hi, n + 1)
                if n == 0:
                    dve.tensor_tensor(kcc[:, 1, :, 0:NC], psum[:, 3, 0:NB].rearrange("p (g m) -> p g m", g=NKV),
                                      raw(kcc[:, 0, :, 0:NC]), ALU.subtract)\
                        .then_inc(cc_lo, 1)
                    norm_conv()
                else:
                    dve.tensor_tensor(vcc[0:NC, :, HD:2 * HD],
                                      psum[0:NC, 3, 0:P].rearrange("p (g d) -> p g d", g=NKV),
                                      raw(vcc[0:NC, :, 0:HD]), ALU.subtract).then_inc(cc_lo, 1)

            def masked(m):
                n, wc = divmod(m, 2)
                u, j = divmod(n, GQA)
                i, g = divmod(u, NKV)
                s = slot_of(n)
                slope = 2.0 ** -(GQA * g + j + 1)
                n_sel, n_win = P * (i + 1), P * min(i + 1, WIN_T + 1)
                flat = psum[:, :, :].rearrange("p b m -> p (b m)")

                def one(br, col, cols, src, dist):
                    return dve.tensor_tensor_reduce(
                        out=probs[:, s, col:col + cols], in0=src, in1=dist, scale=-slope, scalar=-FLOOR,
                        op0=ALU.add, op1=ALU.min, accum_out=nmax[:, s, br:br + 1])

                if u >= 2 and m % ITEMS == 0:
                    dve.wait_ge(pt, KT_BASE[u - 1])
                if wc:
                    dve.wait_ge(qk_wc, n + 1)
                    one(WIN, n_sel, n_win, flat[:, 1024:1024 + n_win], dwin[:, WINDOW + P - n_win:WINDOW + P])
                    one(CMP, n_sel + n_win, NC, psum[:, 3, P:P + NC], dcmp[:, i, :]).then_inc(wc_read, 1)
                else:
                    dve.wait_ge(qk_sel, n + 1)
                    one(SEL, 0, n_sel, flat[:, 0:n_sel], dsel[:, SEQ - n_sel:SEQ]).then_inc(sel_read, 1)

            def weigh(u):
                i, g = divmod(u, NKV)
                s = slice(slot_of(GQA * u), slot_of(GQA * u) + GQA)
                dve.wait_ge(exped, ITEMS * (u + 1))
                did(dve.tensor_scalar(rsafe[:, s, :], rsum[:, s, :], 1e-30, None, ALU.max))
                settle()
                did(dve.reciprocal(rinv[:, s, :], rsafe[:, s, :]))
                settle()
                did(dve.tensor_tensor(wgt[:, s, :], rinv[:, s, :],
                                      gates[:, i, NBR * GQA * g:NBR * GQA * (g + 1)]
                                      .rearrange("p (h b) -> p h b", b=NBR), ALU.mult))
                settle()

            def weighed(gr):
                u, br = divmod(gr, NBR)
                s0 = slot_of(GQA * u)
                w = wgt[:, s0:s0 + GQA, (SEL, WIN, CMP)[br]].unsqueeze(2).broadcast_to([P, GQA, HD])
                dve.wait_ge(o_tok, gr + 1)
                if u >= 2:
                    dve.wait_ge(o_done, u - 1)
                dve.tensor_tensor(parts[:, u % 2, br, :].rearrange("p (h d) -> p h d", d=HD),
                                  psum[:, 6 + gr % 2, 0:GQA * HD].rearrange("p (h d) -> p h d", d=HD), w,
                                  ALU.mult).then_inc(o_part, 1)

            def lo_tile(kt):
                rows = rows_of(kt)
                dve.wait_ge(pt_hi, kt + 1)
                dve.tensor_tensor(ptlo[kt % 3][0:rows, :], psum[0:rows, 4 + kt % 2, :],
                                  raw(pthi[kt % 3][0:rows, :]), ALU.subtract).then_inc(pt_lo, 1)
                for gr in groups_ending(kt - LAG - 1):
                    weighed(gr)

            def mean(c0, c1, width, squares):
                dve.wait_ge(s_sq, squares)
                dve.tensor_scalar(ssq[:, c0:c1], ssq[:, c0:c1], 1.0 / width, EPS, ALU.mult, ALU.add)\
                    .then_inc(s_ms, 1)

            def inverse(steps, c0, c1, roots):
                dve.wait_ge(s_sq, roots)
                dve.reciprocal(inv[:, c0:c1], rms[:, c0:c1]).then_inc(s_ms, 1)
                dve.wait_ge(s_ms, steps)

            def nsa_norm(t):
                if t % HT >= 2:
                    dve.wait_ge(tr, TR_NSA + t - 1)
                dve.scalar_tensor_tensor(nnsa[t // HT][:, t % 2, :], nsa[:, t, :], inv[:, t:t + 1], gnsa[:, :],
                                         ALU.mult, ALU.mult).then_inc(s_n, 1)

            def nsa_lo(t):
                dve.wait_ge(tr_hi, TR_NSA + t + 1)
                c = P * (t % HT)
                dve.tensor_tensor(mlo[:, t // HT, CT:KD, c:c + P],
                                  psum[:, t % 2, :].rearrange("p (k m) -> p k m", m=P),
                                  raw(mhi[:, t // HT, CT:KD, c:c + P]), ALU.subtract).then_inc(tr_lo, 1)

            def beside_last(b):
                if b == 0:
                    inverse(2, 0, NT - 1, NT)
                    dve.wait_ge(gn_in, 16)
                    dve.wait_ge(qk_wc, UNITS * GQA)
                if 1 <= b < 1 + HT:
                    nsa_norm(b - 1)
                if 3 <= b < 3 + HT:
                    nsa_lo(b - 3)

            dve.wait_ge(consts, CONSTS_ALL)
            for m in range(ITEMS):
                masked(m)
            for u in range(UNITS):
                if u == UNITS - 1:
                    mean(0, NT - 1, NH * HD, NT - 1)
                for b in range(BEATS):
                    if b < ITEMS and u + 1 < UNITS:
                        masked(ITEMS * (u + 1) + b)
                    if b == 0:
                        weigh(u)
                    for kt in beat_tiles(u, b):
                        lo_tile(kt)
                    if u == UNITS - 1:
                        beside_last(b)
            for kt in range(N_KT - LAG - 1, N_KT):
                for gr in groups_ending(kt):
                    weighed(gr)

            def h_mean(k):
                c0 = HT * (k % 2)
                mean(c0, c0 + HT, DM, sq_base(k) + HT)

            def h_inverse(k):
                c0 = HT * (k % 2)
                inverse(ms_base(k) + 2, c0, c0 + HT, sq_base(k) + HT + 1)

            def h_norm(hf, t):
                if t >= 2:
                    dve.wait_ge(tr, tr_h(hf) + 2 * (t - 1))
                c = HT * hf + t
                dve.scalar_tensor_tensor(nrm[:, t % 2, :], res[hf][:, t, :], inv[:, c:c + 1], g2[:, :],
                                         ALU.mult, ALU.mult).then_inc(s_n, 1)

            def h_lo(hf, t):
                for b in range(2):
                    dve.wait_ge(tr_hi, tr_h(hf) + 2 * t + b + 1)
                    sl = (slice(None), slice(4 * b, 4 * b + 4), slice(P * t, P * (t + 1)))
                    dve.tensor_tensor(vlo[sl], psum[:, 2 * (t % 2) + b, :].rearrange("p (k m) -> p k m", m=P),
                                      raw(vhi[sl]), ALU.subtract).then_inc(tr_lo, 1)

            def add_y(n, par, dst):
                dve.wait_ge(y_tr, n + 1)
                dve.tensor_tensor(dst, dst, psum[:, 6 + par, :].rearrange("p (t m) -> p t m", t=HT), ALU.add)\
                    .then_inc(y_add, 1)

            def add_col(n):
                c = P * (n % KD)
                hf = n // KD % HALVES
                add_y(n, n % 2, res[hf][:, :, c:c + P])

            def final(hf, t):
                c = HT * hf + t
                dve.scalar_tensor_tensor(res[hf][:, t, :], res[hf][:, t, :], inv[:, c:c + 1], gf[:, :],
                                         ALU.mult, ALU.mult).then_inc(fin, 1)

            mean(NT - 1, NT, NH * HD, NT + 1)
            inverse(4, NT - 1, NT, NT + 2)
            for t in range(HT, HT + 2):
                nsa_norm(t)
            dve.wait_ge(res_in[0], 32)
            for n in range(2, N_OUT):
                if n == KD + 2:
                    dve.wait_ge(res_in[1], 16)
                add_col(n - 2)
                if n < 2 + HT:
                    nsa_lo(n + 2)
                    if n + 4 < NT:
                        nsa_norm(n + 4)
                if n == KD + 3:
                    h_mean(0)
                if n == KD + 4:
                    h_inverse(0)
                    dve.wait_ge(g2_in, 32)
                    for t in range(2):
                        h_norm(0, t)
                if n == N_OUT - 2:
                    for t in range(2):
                        h_lo(0, t)
                        h_norm(0, 2 + t)
            for t in range(2, HT):
                h_lo(0, t)
            for n in range(N_OUT - 2, N_OUT):
                add_col(n)

            for hf in range(HALVES):
                f0, w0 = FT * hf, w_of(hf, "glu")

                def glu_of(f, par):
                    dve.wait_ge(sil, f + (f0 + 1))
                    dve.wait_ge(w_used, f * 2 + (w0 + 2))
                    dve.tensor_tensor(silu[:, par, :], silu[:, par, :], psum[:, 2 * par + 1, :], ALU.mult)\
                        .then_inc(glu, 1)
                    dve.wait_ge(g_hi, f + (f0 + 1))
                    dve.tensor_tensor(hlo[:, ds(f, 1), :], silu[:, par:par + 1, :], raw(hhi[:, ds(f, 1), :]),
                                      ALU.subtract).then_inc(g_lo, 1)

                if hf:
                    h_mean(2)
                    glu_of(0, 0)
                    h_inverse(2)
                    for t in range(HT):
                        final(0, t)
                    glu_of(1, 1)
                with dve.Fori(hf, FT // 2) as ff:
                    for e in range(2):
                        glu_of(ff * 2 + e, e)

                y0 = N_OUT + KD * hf
                with dve.Fori(0, KD // 2 if hf else KD // 2 - 2) as mm:
                    for d in range(2):
                        add_y(mm * 2 + (y0 + d), d, res[hf][:, :, ds(mm * (2 * P) + P * d, P)])
                if hf == 0:
                    h_mean(1)
                    h_inverse(1)
                    for t in range(2):
                        h_norm(1, t)
                    for e in range(2):
                        add_col(y0 + KD - 4 + e)
                        for t in (2 * e, 2 * e + 1):
                            h_lo(1, t)
                        if e == 0:
                            for t in range(2, HT):
                                h_norm(1, t)
                    for n in range(y0 + KD - 2, y0 + KD):
                        add_col(n)
            h_mean(3)
            h_inverse(3)
            for t in range(HT):
                final(1, t)


CONSTS_FIRST = 2 + CT + 2
CONSTS_ALL = CONSTS_FIRST + 3
VECS = 16 * (1 + 1 + 3 + 2 * 3)


TR_NSA = 2 * NT


def sq_base(k):
    return NT + 2 + (HT + 1) * k


def ms_base(k):
    return 4 + 2 * k


def tr_h(hf):
    return TR_NSA + NT + 2 * HT * hf


_INS = ["x", "norm1_g", "w_in", "conv_w", "k_cmp_pos", "k_cmp_w1", "k_cmp_w2", "v_cmp_pos", "v_cmp_w1",
        "v_cmp_w2", "gn_conv_g", "gn_nsa_g", "w_out", "norm2_g", "w_gate", "w_up", "w_down", "norm_f_g"]


def kernel(**inputs):
    import numpy as np
    import concourse.bacc as bacc
    from concourse.bass_utils import run_bass_kernel_spmd

    nc = bacc.Bacc("TRN2", target_bir_lowering=False, num_devices=1)
    arrays, args = {}, []
    for name in _INS:
        a = np.ascontiguousarray(inputs[name])
        arrays[f"in_{name}"] = a
        args.append(nc.dram_tensor(f"in_{name}", a.shape, mybir.dt.from_np(a.dtype), kind="ExternalInput").ap())
    args.append(nc.dram_tensor("out_h", (1, SEQ, DM), mybir.dt.float32, kind="ExternalOutput").ap())
    hymba_block(nc, *args)
    r = run_bass_kernel_spmd(nc, [arrays], core_ids=[0])
    return r.results[0]["out_h"]
```

```python
from contextlib import ExitStack

import concourse.bass as bass
from concourse import mybir

P = 128
SEQ, DM = 1024, 1024
NT = SEQ // P
KD = DM // P
HALVES, HT = 2, NT // 2
HN = HT * P
CONV = 512
CT = CONV // P
NH, HD, NKV, GQA = 8, 64, 2, 4
CMP_BLOCK, CMP_STRIDE, CMP_HID = 32, 16, 256
NC = (SEQ - CMP_BLOCK) // CMP_STRIDE + 1
NB = NKV * NC
LP = CMP_BLOCK // 2
SEL_BLOCK, SEL_TOP = 64, 16
assert SEQ // SEL_BLOCK <= SEL_TOP
WIN_T = 4
WINDOW = WIN_T * P
DFF = 2816
FT = DFF // P
EPS = 1e-6
NBR = 3
NGATE = NH * NBR

D_IN = 3 * CONV + NH * HD + 6 * NKV * HD + NGATE
Q0 = 3 * CONV
KC0, VC0, KS0, VS0, KW0, VW0 = (Q0 + NH * HD + P * n for n in range(6))
QT = NH * HD // P
FIRST_COLS = [Q0 + P * t for t in range(QT)] + [KS0, KW0, VS0, VW0, KC0, VC0]
N_FIRST = len(FIRST_COLS)
N_IN = N_FIRST + 3 * CT + 1
GATE0 = P - NGATE
ACT_EV = N_FIRST + CT + 1
DVE_EV = N_FIRST + 2 * CT
PIECES = [(0, 8), (8, 8), (16, FT - 16)]
NPC = len(PIECES)
CMP_PC = 4

CMP_PE = {(0, 0): N_FIRST + 3, (0, 1): N_FIRST + 4, (0, 2): N_FIRST + 7, (0, 3): N_FIRST + 8,
          (1, 0): N_IN - 3, (1, 1): N_IN - 2, (1, 2): N_IN - 1, (1, 3): N_IN - 1}
CMP_SP = {N_FIRST: [0], N_FIRST + 1: [1], N_FIRST + 6: [2], N_FIRST + 7: [3], N_FIRST + 10: [4],
          N_FIRST + 11: [5], N_IN - 1: [6, 7]}
W_BACK = HALVES * N_IN
N_OUT = HALVES * KD
N_FFN = 2 * FT + NPC * KD
W_END = W_BACK + N_OUT + HALVES * N_FFN

MASKED = -1.0e38
CMP, SEL, WIN = range(NBR)
FLOOR = -1.0e30
SLOTS = 8
UNITS = NT * NKV
SLOT_COLS = SEQ + WINDOW + P + HD

KiB = 1024


def key_tiles(i):
    j0 = max(0, i - WIN_T)
    sel = [(0, j, P * j) for j in range(i + 1)]
    win = [(1, j, P * (i + 1) + P * (j - j0)) for j in range(j0, i + 1)]
    return sel + win + [(2, 0, P * (i + 1) + P * (i + 1 - j0))]


KTS = [key_tiles(u // NKV) for u in range(UNITS)]
KT_BASE = [sum(len(k) for k in KTS[:u]) for u in range(UNITS + 1)]


ITEMS = 2 * GQA
N_ITEMS = ITEMS * UNITS
BEATS = ITEMS + 1
N_KT = KT_BASE[UNITS]
LAG = 2
GROUP_END = [KT_BASE[u] + max(q for q, (b, _, _) in enumerate(KTS[u]) if b == br)
             for u in range(UNITS) for br in range(NBR)]
GROUP_START = [0] + [e + 1 for e in GROUP_END[:-1]]


def score_banks(n):
    i = n // (GQA * NKV)
    n_win = P * min(i + 1, WIN_T + 1)
    if two_heads(n):
        return n % 2, 2 + n % 2, (2 + n % 2, n_win)
    return 0, 2, (3, P)


def two_heads(n):
    return P * (n // (GQA * NKV) + 1) + NC + 1 <= 512


def ahead(m):
    return 2 if two_heads(m // 2) else 1


def slot_of(n):
    return (n + GQA) % SLOTS


def beat_tiles(u, b):
    first, last = ((len(KTS[u]) * n + BEATS // 2) // BEATS for n in (b, b + 1))
    return range(KT_BASE[u] + first, KT_BASE[u] + last)


FEW = 5


def lo_beat(kt):
    u = unit_of(kt)
    b = next(b for b in range(BEATS) if kt in beat_tiles(u, b))
    return BEATS * u + b + (len(KTS[u]) <= FEW)


def unit_of(kt):
    return max(u for u in range(UNITS) if KT_BASE[u] <= kt)


def rows_of(kt):
    u = unit_of(kt)
    return NC if KTS[u][kt - KT_BASE[u]][0] == 2 else P


def groups_ending(kt):
    return [g for g in range(NBR * UNITS) if GROUP_END[g] == kt]


def hymba_block(nc, x, norm1_g, w_in, conv_w, k_cmp_pos, k_cmp_w1, k_cmp_w2, v_cmp_pos, v_cmp_w1,
                v_cmp_w2, gn_conv_g, gn_nsa_g, w_out, norm2_g, w_gate, w_up, w_down, norm_f_g, out):
    f32, f32r = mybir.dt.float32, mybir.dt.float32r
    ALU = mybir.AluOpType
    ACT = mybir.ActivationFunctionType
    ds = bass.ds

    x, out = x[0], out[0]
    w_in, w_out, w_gate, w_up, w_down = w_in[0], w_out[0], w_gate[0], w_up[0], w_down[0]
    x_t = x.rearrange("(t p) d -> p t d", p=P)
    out_t = out.rearrange("(t p) d -> p t d", p=P)
    w_in_k = w_in.rearrange("(k p) m -> p k m", p=P)
    w_out_k = w_out.rearrange("(k p) m -> p k m", p=P)
    w_gate_k = w_gate.rearrange("(k p) m -> p k m", p=P)
    w_up_k = w_up.rearrange("(k p) m -> p k m", p=P)
    w_down_k = w_down.rearrange("(k p) m -> p k m", p=P)
    w1_k = [w[0].rearrange("(c p) m -> p c m", p=P) for w in (k_cmp_w1, v_cmp_w1)]
    w2_k = [w[0].rearrange("(c p) m -> p c m", p=P) for w in (k_cmp_w2, v_cmp_w2)]
    pos_k = [w[0].rearrange("(c l) d -> (l d) c", l=2) for w in (k_cmp_pos, v_cmp_pos)]

    ctx = ExitStack()
    with ctx:
        origin = (nc.sbuf_base + 31) // 32 * 32
        limit = nc.sbuf_usable_end

        def at(name, offset, shape, dt=f32):
            size = 4
            for n in shape[1:]:
                size *= n
            assert origin + offset + size <= limit, (name, origin + offset + size - limit)
            return nc.alloc_sbuf_tensor_at(name, shape, dt, offset=origin + int(offset))

        def sem(name):
            return ctx.enter_context(nc.semaphore(name))

        place = [0]

        def small(name, shape, dt=f32):
            size = 4
            for n in shape[1:]:
                size *= n
            t = at(name, place[0], shape, dt)
            place[0] += (size + 31) // 32 * 32
            assert place[0] <= 8 * KiB, place[0]
            return t

        ident = small("ident", [P, P])
        fold = small("fold", [P, HD])
        ones = small("ones", [P, P])
        ssq = small("ssq", [P, NT])
        rms = small("rms", [P, NT])
        inv = small("inv", [P, NT])
        gconv = small("gconv", [P, CT])
        taps = small("taps", [P, 3, CT])
        gates = small("gates", [P, NT, NGATE])
        spare = small("spare", [P, 1])
        carry = small("carry", [P, CT, 2])
        pos = small("pos", [P, 2, LP])
        w2d = small("w2d", [P, 2, 2, 2 * HD])
        qscale = small("qscale", [P, QT])
        kcc = small("kcc", [P, 2, NKV, NC + 1], f32r)
        vcc = small("vcc", [P, NKV, 2 * HD], f32r)
        nmax = small("nmax", [P, SLOTS, NBR])
        rsum = small("rsum", [P, SLOTS, NBR])
        rsafe = small("rsafe", [P, SLOTS, NBR])
        rinv = small("rinv", [P, SLOTS, NBR])
        wgt = small("wgt", [P, SLOTS, NBR])

        convT = at("convT", 8 * KiB, [P, CT, SEQ])
        wraw = at("wraw", 104 * KiB, [P, 2, 1024])
        whi = at("whi", 112 * KiB, [P, 2, 1024], f32r)
        wlo = at("wlo", 120 * KiB, [P, 2, 1024], f32r)
        qs = at("qs", 24 * KiB, [P, HALVES, NH, HN], f32r)
        vs = at("vs", 56 * KiB, [P, 2, NT, NKV, 2 * HD], f32r)
        kT = at("kT", 72 * KiB, [P, 2, 2, SEQ], f32r)
        kcs = at("kcs", 88 * KiB, [P, 2, NKV, SEQ])
        uhi = at("uhi", 128 * KiB, [P, KD, HN], f32r)
        ulo = at("ulo", 144 * KiB, [P, KD, HN], f32r)
        xin = [at("xin0", 88 * KiB, [P, HT, DM]),
               at("xin1", 40 * KiB, [P, HT, DM])]
        g1b = at("g1b", 168 * KiB, [P, DM])
        csq = [at("csq0", 172 * KiB, [P, 2, HN]),
               at("csq1", 62 * KiB, [P, 2, HN])]
        crms = [at("crms0", 204.5 * KiB, [P, HN]),
                at("crms1", 66 * KiB, [P, HN])]
        ccs = at("ccs", 176 * KiB, [P, HN])
        cacc = at("cacc", 178 * KiB, [P, HN])
        useq = at("useq", 180 * KiB, [P, HN + 2])
        junk1 = at("junk1", 184 * KiB, [P, DM])
        qstage = at("qstage", 188 * KiB, [P, 2, 2, HN], f32r)
        kcraw = at("kcraw", 196 * KiB, [P, 2, HN])
        vraw = at("vraw", 200 * KiB, [P, 2, HN])
        graw = at("graw", 204.5 * KiB, [P, HN])
        blk = at("blk", 160 * KiB, [P, LP, NB])
        w1 = at("w1", 168 * KiB, [P, 2, 1024])
        hid = at("hid", 184 * KiB, [P, 4, CMP_HID])
        hidT = at("hidT", 206.5 * KiB, [P, 2, NB])
        dsel = at("dsel", 188 * KiB, [P, SEQ])
        dwin = at("dwin", 192 * KiB, [P, WINDOW + P])
        dcmp = at("dcmp", 194.5 * KiB, [P, NT, NC])
        ks = at("ks", 128 * KiB, [P, 2, 2, NKV, SEQ], f32r)
        probs = at("probs", 72 * KiB, [P, SLOTS, SLOT_COLS])
        pthi = [at(f"pthi{n}", k * KiB, [P, GQA * P], f32r) for n, k in enumerate((160, 162, 204.5))]
        ptlo = [at(f"ptlo{n}", k * KiB, [P, GQA * P], f32r) for n, k in enumerate((164, 166, 202.5))]
        osb = at("osb", 168 * KiB, [P, 2, GQA * P])
        parts = at("parts", 196.5 * KiB, [P, 2, NBR, GQA * HD])
        nsa = at("nsa", 172 * KiB, [P, NT, NH * HD])
        gnsa = at("gnsa", 148 * KiB, [P, NH * HD])
        junk2 = at("junk2", 126 * KiB, [P, NH * HD])
        mhi = at("mhi", 24 * KiB, [P, HALVES, KD, HN], f32r)
        mlo = at("mlo", 128 * KiB, [P, HALVES, KD, HN], f32r)
        nnsa = [at("nnsa0", 144 * KiB, [P, 2, NH * HD]),
                at("nnsa1", 56 * KiB, [P, 2, NH * HD])]
        junk3 = at("junk3", 60 * KiB, [P, NH * HD])
        res = [at("res0", 188 * KiB, [P, HT, DM]),
               at("res1", 172 * KiB, [P, HT, DM])]
        yT = at("yT", 100 * KiB, [P, 2, HN])
        g2 = at("g2", 8 * KiB, [P, DM])
        gf = at("gf", 12 * KiB, [P, DM])
        nrm = at("nrm", 16 * KiB, [P, 2, DM])
        hhi = at("hhi", 24 * KiB, [P, FT, HN], f32r)
        hlo = at("hlo", 128 * KiB, [P, FT, HN], f32r)
        vhi = at("vhi", 68 * KiB, [P, KD, HN], f32r)
        vlo = at("vlo", 84 * KiB, [P, KD, HN], f32r)
        silu = yT
        psum = ctx.enter_context(nc.psum_tensor("psum", [P, 8, 512], f32))

        w_in_sem = [sem("w_arrived0"), sem("w_arrived1")]
        w_hi = sem("w_hi")
        w_lo = sem("w_lo")
        w_used = sem("w_used")
        consts = sem("consts")
        g1_in = sem("g1_in")
        vecs = sem("vecs")
        x_in = [sem(f"x_in{t}") for t in range(HT + 1)]
        x2_sq = sem("x2_sq")
        x2_ms = sem("x2_ms")
        x_sq = sem("x_sq")
        x_ms = sem("x_ms")
        x_n = sem("x_n")
        tr = sem("tr")
        tr_hi = sem("tr_hi")
        tr_lo = sem("tr_lo")
        act_ev = sem("act_ev")
        dve_ev = sem("dve_ev")
        q_out = [sem("q_out0"), sem("q_out1")]
        kc_out = [sem("kc_out0"), sem("kc_out1")]
        ks_out = [sem("ks_out0"), sem("ks_out1")]
        vt = sem("vt")
        vt_hi = sem("vt_hi")
        vt_lo = sem("vt_lo")
        gexp = sem("gexp")
        own = sem("own")
        pool_own = sem("pool_own")
        c_sq = sem("c_sq")
        c_ss = sem("c_ss")
        c_ms = sem("c_ms")
        c_rt = sem("c_rt")
        c_done = sem("c_done")
        w1_in = [sem("w1_in0"), sem("w1_in1")]
        w1_used = sem("w1_used")
        b_raw = sem("b_raw")
        hid_sb = sem("hid_sb")
        tanh_arg = sem("tanh_arg")
        tanh_out = sem("tanh_out")
        gelu_out = sem("gelu_out")
        hid_tr = sem("hid_tr")
        hid_tr_sb = sem("hid_tr_sb")
        cmp_mm = sem("cmp_mm")
        cc_hi = sem("cc_hi")
        cc_lo = sem("cc_lo")
        qk_sel = sem("qk_sel")
        qk_wc = sem("qk_wc")
        sel_read = sem("sel_read")
        wc_read = sem("wc_read")
        exped = sem("exped")
        pt = sem("pt")
        pt_hi = sem("pt_hi")
        pt_lo = sem("pt_lo")
        pv = sem("pv")
        o_sb = sem("o_sb")
        o_tok = sem("o_tok")
        o_part = sem("o_part")
        o_done = sem("o_done")
        res_in = [sem("res_in0"), sem("res_in1")]
        gn_in = sem("gn_in")
        g2_in = sem("g2_in")
        s_sq = sem("s_sq")
        s_ms = sem("s_ms")
        s_n = sem("s_n")
        cm_hi = sem("cm_hi")
        cm_lo = sem("cm_lo")
        y_sb = sem("y_sb")
        y_tr = sem("y_tr")
        y_add = sem("y_add")
        sil = sem("sil")
        glu = sem("glu")
        g_hi = sem("g_hi")
        g_lo = sem("g_lo")
        fin = sem("fin")
        scaled = sem("scaled")
        fin_last = sem("fin_last")
        stored = sem("stored")

        block = ctx.enter_context(nc.Block())

        def raw(ap):
            return ap.bitcast(f32)

        def slot(w):
            return w % 2

        def w_of(hf, stage):
            return W_BACK + {"out": KD * hf, "glu": N_OUT + N_FFN * hf, "down": N_OUT + N_FFN * hf + 2 * FT}[stage]

        @block.sync
        def _(sp):
            def load_w(w, par, src, cols=1024):
                sp.wait_ge(w_lo, w - 1)
                sp.dma_start(wraw[:, par, 0:cols].rearrange("p (k m) -> p k m", m=src.shape[2]), src)\
                    .then_inc(w_in_sem[par], 16)

            def cols_of(k):
                if k < N_FIRST:
                    return FIRST_COLS[k]
                if k == N_IN - 1:
                    return D_IN - P
                c, n = divmod(k - N_FIRST, 3)
                return P * c + (CONV, 2 * CONV, 0)[n]

            def store(hf):
                for t in range(HT):
                    if HT * hf + t == NT - 1:
                        sp.wait_ge(fin_last, 1)
                    else:
                        sp.wait_ge(fin, HT * hf + t + 1)
                    sp.dma_start(out_t[:, HT * hf + t, :], res[hf][:, t, :]).then_inc(stored, 16)

            for t in range(HT):
                sp.dma_start(xin[0][:, t, :], x_t[:, t, :]).then_inc(x_in[t], 16)
                if t == 0:
                    sp.dma_start(g1b[:, :], norm1_g[0].partition_broadcast(P)).then_inc(g1_in, 16)
            for w in range(2):
                sp.dma_start(wraw[:, w, :].rearrange("p (k m) -> p k m", m=P),
                             w_in_k[:, :, cols_of(w):cols_of(w) + P]).then_inc(w_in_sem[w], 16)
            sp.dma_start(xin[1][:, :, :], x_t[:, HT:NT, :]).then_inc(x_in[HT], 16)
            with nc.allow_non_contiguous_dma(reason="small parameters, once"):
                sp.dma_start(gconv[:, :], gn_conv_g[0].rearrange("(c p) -> p c", p=P)).then_inc(vecs, 16)
                for n in range(3):
                    sp.dma_start(taps[:, n, :], conv_w[0, n].rearrange("(c p) -> p c", p=P)).then_inc(vecs, 16)
                for n in range(2):
                    sp.dma_start(pos[:, n, :], pos_k[n]).then_inc(vecs, 16)
                    for d in range(2):
                        sp.dma_start(w2d[:, n, :, d * HD:(d + 1) * HD], w2_k[n]).then_inc(vecs, 16)

            def stage_out(hf, k):
                tok = HN * hf
                if k < QT:
                    sp.wait_ge(act_ev, ACT_EV * hf + k + 1)
                    sp.wait_ge(dve_ev, DVE_EV * hf + k + 1)
                    for r in range(2):
                        for part in range(2):
                            sp.dma_start(raw(qs[HD * part:HD * (part + 1), hf, 2 * k + r, :]),
                                         raw(qstage[HD * r:HD * (r + 1), k % 2, part, :])).then_inc(q_out[k % 2], 16)
                elif k in (8, 9):
                    n = k - 8
                    sp.wait_ge(act_ev, ACT_EV * hf + k + 1)
                    sp.wait_ge(dve_ev, DVE_EV * hf + k + 1)
                    for g in range(NKV):
                        src = kcraw[HD * g:HD * (g + 1), n, :]
                        sp.dma_start(kcs[0:HD, n, g, tok:tok + HN], src).then_inc(kc_out[n], 16)
                        skip = 1 - hf
                        sp.dma_start(kcs[HD:P, n, g, tok - 1 + skip:tok - 1 + HN], src[:, skip:HN])\
                            .then_inc(kc_out[n], 16)

            def stack_k(hf, brs):
                cols = slice(HN * hf, HN * (hf + 1))
                for br in brs:
                    for g in range(NKV):
                        for d in range(2):
                            sp.dma_start(raw(ks[HD * d:HD * (d + 1), br, :, g, cols]),
                                         raw(kT[HD * g:HD * (g + 1), br, :, cols])).then_inc(ks_out[hf], 16)

            def load_w1(j):
                n, pc = divmod(j, CMP_PC)
                if j >= 2:
                    sp.wait_ge(w1_used, j - 1)
                sp.dma_start(w1[:, j % 2, :].rearrange("p (k m) -> p k m", m=CMP_HID),
                             w1_k[n][:, 4 * pc:4 * pc + 4, :]).then_inc(w1_in[j % 2], 16)

            for hf in range(HALVES):
                for k in range(N_IN):
                    w = N_IN * hf + k
                    if w >= 2:
                        load_w(w, slot(w), w_in_k[:, :, cols_of(k):cols_of(k) + P])
                    if k >= 2:
                        stage_out(hf, k - 2)
                    if hf and k in CMP_SP:
                        if k == N_FIRST:
                            sp.wait_ge(x_n, NT)
                            sp.wait_ge(c_ss, CT)
                        for j in CMP_SP[k]:
                            load_w1(j)
            sp.wait_ge(w_used, W_BACK)
            stack_k(0, (0, 1))
            stack_k(1, (0, 1))

            def out_tile(m):
                w = W_BACK + m
                c = P * (m % KD)
                load_w(w, slot(w), w_out_k[:, :, c:c + P])

            sp.wait_ge(pt, KT_BASE[UNITS - 1])
            for m in range(2):
                out_tile(m)
            sp.wait_ge(sel_read, UNITS * GQA)
            sp.wait_ge(wc_read, UNITS * GQA)
            sp.dma_start(gnsa[:, :], gn_nsa_g[0].partition_broadcast(P)).then_inc(gn_in, 16)
            sp.dma_start(res[0][:, 0:2, :], x_t[:, 0:2, :]).then_inc(res_in[0], 16)
            for m in range(2, 4):
                out_tile(m)
            sp.wait_ge(o_done, UNITS)
            sp.dma_start(res[0][:, 2:HT, :], x_t[:, 2:HT, :]).then_inc(res_in[0], 16)
            for m in range(4, 4 + HT):
                out_tile(m)
            sp.wait_ge(s_n, NT)
            for t in range(HT):
                out_tile(4 + HT + t)
                sp.dma_start(res[1][:, t, :], x_t[:, HT + t, :]).then_inc(res_in[1], 16)
            sp.wait_ge(cm_lo, HALVES * CT)
            sp.dma_start(g2[:, :], norm2_g[0].partition_broadcast(P)).then_inc(g2_in, 16)
            sp.dma_start(gf[:, :], norm_f_g.partition_broadcast(P)).then_inc(g2_in, 16)
            for m in range(4 + 2 * HT, N_OUT):
                out_tile(m)

            for hf in range(HALVES):
                w0 = w_of(hf, "glu")
                with sp.Fori(0, FT) as f:
                    for d, src in enumerate((w_gate_k, w_up_k)):
                        load_w(f * 2 + (w0 + d), slot(w0 + d), src[:, :, ds(f * P, P)])
                if hf:
                    store(0)
                w0 = w_of(hf, "down")
                with sp.Fori(0, KD // 2) as mm:
                    for e in range(2):
                        for n, (k0, nk) in enumerate(PIECES):
                            d = NPC * e + n
                            load_w(mm * (2 * NPC) + (w0 + d), slot(w0 + d),
                                   w_down_k[:, k0:k0 + nk, ds(mm * (2 * P) + P * e, P)], nk * P)
            store(1)
            sp.wait_ge(stored, 16 * NT)

        @block.gpsimd
        def _(pool):
            def w_lo_of(w, par, cols=1024):
                pool.wait_ge(w_hi, w + 1)
                pool.tensor_tensor(wlo[:, par, 0:cols], wraw[:, par, 0:cols], raw(whi[:, par, 0:cols]),
                                   ALU.subtract).then_inc(w_lo, 1)

            pool.memset(ident[:, :], 0.0).then_inc(pool_own, 1)
            pool.memset(fold[:, :], 0.0).then_inc(pool_own, 1)
            pool.memset(ones[:, :], 1.0).then_inc(consts, 1)
            pool.memset(raw(kcc[:, :, :, :]), 0.0).then_inc(consts, 1)
            pool.memset(carry[:, :, :], 0.0).then_inc(consts, 1)
            pool.wait_ge(pool_own, 2)
            pool.affine_select(out=ident[:, :], in_=ident[:, :], compare_op=ALU.not_equal, fill=1.0, base=0,
                               pattern=[[-1, P]], channel_multiplier=1).then_inc(consts, 1)
            pool.affine_select(out=fold[:, :], in_=fold[:, :], compare_op=ALU.not_equal, fill=1.0, base=0,
                               pattern=[[-1, HD]], channel_multiplier=1).then_inc(pool_own, 1)
            pool.wait_ge(pool_own, 3)
            pool.affine_select(out=fold[:, :], in_=fold[:, :], compare_op=ALU.not_equal, fill=1.0, base=-HD,
                               pattern=[[-1, HD]], channel_multiplier=1).then_inc(consts, 1)

            def distances(step):
                if step == 0:
                    for k in range(2):
                        pool.wait_ge(q_out[k], 64 * HALVES * QT // 2)
                        pool.wait_ge(kc_out[k], 64 * HALVES)
                    pool.iota(dsel[:, :], pattern=[[1, SEQ]], base=P - SEQ, channel_multiplier=-1,
                              allow_small_or_imprecise_dtypes=True).then_inc(pool_own, 1)
                elif step == 1:
                    pool.iota(dwin[:, :], pattern=[[1, WINDOW + P]], base=-WINDOW, channel_multiplier=-1,
                              allow_small_or_imprecise_dtypes=True).then_inc(pool_own, 1)
                    pool.iota(dcmp[:, :, :], pattern=[[-P, NT], [CMP_STRIDE, NC]], base=CMP_BLOCK - 1,
                              channel_multiplier=-1, allow_small_or_imprecise_dtypes=True).then_inc(pool_own, 1)
                elif step == 2:
                    pool.wait_ge(pool_own, 6)
                    pool.affine_select(out=dsel[:, :], in_=dsel[:, :], compare_op=ALU.is_ge, fill=MASKED,
                                       base=SEQ - P, pattern=[[-1, SEQ]], channel_multiplier=1).then_inc(consts, 1)
                    pool.affine_select(out=dwin[:, :], in_=dwin[:, :], compare_op=ALU.is_ge, fill=MASKED,
                                       base=WINDOW, pattern=[[-1, WINDOW + P]], channel_multiplier=1)\
                        .then_inc(pool_own, 1)
                else:
                    pool.affine_select(out=dcmp[:, :, :], in_=dcmp[:, :, :], compare_op=ALU.is_ge, fill=MASKED,
                                       base=1 - CMP_BLOCK, pattern=[[P, NT], [-CMP_STRIDE, NC]],
                                       channel_multiplier=1).then_inc(consts, 1)
                    pool.wait_ge(pool_own, 7)
                    pool.affine_select(out=dwin[:, :], in_=dwin[:, :], compare_op=ALU.is_ge, fill=MASKED,
                                       base=-1, pattern=[[1, WINDOW + P]], channel_multiplier=-1)\
                        .then_inc(consts, 1)

            w_dist = (N_IN + N_FIRST + 3) // 2 * 2
            with pool.Fori(0, w_dist, 2) as w:
                for d in range(2):
                    w_lo_of(w + d, d)
            for w in range(w_dist, w_dist + 4):
                w_lo_of(w, slot(w))
                distances(w - w_dist)
            assert (W_BACK - w_dist) % 2 == 0
            with pool.Fori(w_dist + 4, W_BACK, 2) as w:
                for d in range(2):
                    w_lo_of(w + d, d)

            def conv_lo(hf, c):
                pool.wait_ge(cm_hi, CT * hf + c + 1)
                pool.tensor_tensor(mlo[:, hf, c, :], convT[:, c, HN * hf:HN * (hf + 1)], raw(mhi[:, hf, c, :]),
                                   ALU.subtract).then_inc(cm_lo, 1)

            for u in range(UNITS):
                if u == UNITS - 1:
                    for c in range(CT):
                        conv_lo(0, c)
                    for w in range(W_BACK, W_BACK + 2):
                        w_lo_of(w, slot(w))
                i, g = divmod(u, NKV)
                o = nsa[:, i, GQA * HD * g:GQA * HD * (g + 1)]
                pool.wait_ge(o_part, NBR * (u + 1))
                pool.tensor_tensor(o, parts[:, u % 2, 2, :], parts[:, u % 2, 0, :], ALU.add).then_inc(pool_own, 1)
                pool.wait_ge(pool_own, 8 + u)
                pool.tensor_tensor(o, o, parts[:, u % 2, 1, :], ALU.add).then_inc(o_done, 1)

            for m in range(2, KD):
                w_lo_of(W_BACK + m, slot(W_BACK + m))
                if m >= KD - 2:
                    pool.wait_ge(s_n, NT)
                    for c in range(2):
                        conv_lo(1, 2 * (m - KD + 2) + c)
            with pool.Fori(KD, N_OUT, 2) as k:
                for d in range(2):
                    w_lo_of(k + (W_BACK + d), slot(W_BACK + d))
            for hf in range(HALVES):
                w0 = w_of(hf, "glu")
                with pool.Fori(0, 2 * FT, 2) as k:
                    for d in range(2):
                        w_lo_of(k + (w0 + d), slot(w0 + d))
                w0 = w_of(hf, "down")
                with pool.Fori(0, KD // 2) as mm:
                    for e in range(2):
                        for n, (_, nk) in enumerate(PIECES):
                            d = NPC * e + n
                            w_lo_of(mm * (2 * NPC) + (w0 + d), slot(w0 + d), nk * P)
            pool.wait_ge(scaled, 1)
            pool.tensor_tensor(res[1][:, HT - 1, :], res[1][:, HT - 1, :], gf[:, :], ALU.mult).then_inc(fin_last, 1)

        @block.scalar
        def _(act):
            def w_hi_of(w, par, pairs, cols=1024):
                act.wait_ge(w_in_sem[par], pairs * 16)
                act.activation(whi[:, par, 0:cols], wraw[:, par, 0:cols], ACT.Copy).then_inc(w_hi, 1)

            def next_w(w, pairs, cols=1024, par=None):
                act.wait_ge(w_used, w - 1)
                w_hi_of(w, slot(w) if par is None else par, pairs, cols)

            def norm_tile(t):
                act.wait_ge(x_in[t], 16)
                if t:
                    act.wait_ge(x_sq, 2 * t)
                act.activation(junk1[:, :], xin[0][:, t, :], ACT.Square, accum_out=ssq[:, t:t + 1])\
                    .then_inc(x_sq, 1)
                act.wait_ge(x_ms, 2 * t + 1)
                act.activation(rms[:, t:t + 1], ssq[:, t:t + 1], ACT.Sqrt).then_inc(x_sq, 1)

            def norm_hi(n):
                t = n % HT
                for b in range(2):
                    act.wait_ge(tr, 2 * n + b + 1)
                    act.activation(uhi[:, 4 * b:4 * b + 4, P * t:P * (t + 1)],
                                   psum[:, 2 * (n % 2) + b, :].rearrange("p (k m) -> p k m", m=P),
                                   ACT.Copy).then_inc(tr_hi, 1)

            def second_norm(k):
                if k in (1, 2):
                    if k == 1:
                        act.wait_ge(x_in[HT], 16)
                    for t in (2 * k - 2, 2 * k - 1):
                        if t:
                            act.wait_ge(x2_sq, t)
                        act.activation(junk1[:, :], xin[1][:, t, :], ACT.Square,
                                       accum_out=ssq[:, HT + t:HT + t + 1]).then_inc(x2_sq, 1)
                if k == 3:
                    act.wait_ge(x2_ms, 1)
                    act.activation(rms[:, HT:NT], ssq[:, HT:NT], ACT.Sqrt).then_inc(x2_sq, 1)

            def v_hi(hf):
                for br in range(2):
                    act.wait_ge(vt, 3 * hf + br + 1)
                    act.activation(vs[:, br, HT * hf:HT * (hf + 1), :, 0:HD],
                                   psum[:, 6 + br, :].rearrange("p (t g d) -> p t g d", t=HT, g=NKV),
                                   ACT.Copy).then_inc(vt_hi, 1)

            def gate_exp(hf):
                act.wait_ge(vt, 3 * hf + 3)
                act.activation(gates[:, HT * hf:HT * (hf + 1), :],
                               psum[:, 6, :].rearrange("p (t m) -> p t m", m=P)[:, :, GATE0:P],
                               ACT.Exp, scale=-1.0).then_inc(gexp, 1)

            def conv_square(hf, c):
                n = CT * hf + c
                if n >= 2:
                    act.wait_ge(c_ss, n - 1)
                act.activation(csq[hf][:, c % 2, :], convT[:, c, HN * hf:HN * (hf + 1)], ACT.Square)\
                    .then_inc(c_sq, 1)

            def conv_root(hf):
                act.wait_ge(c_ms, hf + 1)
                act.activation(crms[hf][:, :], crms[hf][:, :], ACT.Sqrt).then_inc(c_rt, 1)

            def evacuate(hf, k):
                w, tok, bank = N_IN * hf + k, HN * hf, 4 + k % 2
                if k < QT:
                    act.wait_ge(w_used, w + 1)
                    uses = 2 * hf + k // 2
                    if uses:
                        act.wait_ge(q_out[k % 2], 64 * uses)
                    act.activation(qstage[:, k % 2, 0, :], psum[:, bank, :], ACT.Copy,
                                   scale=qscale[:, k:k + 1]).then_inc(act_ev, 1)
                elif k < QT + 2:
                    act.wait_ge(w_used, w + 1)
                    act.activation(kT[:, k - QT, 0, tok:tok + HN], psum[:, bank, :], ACT.Copy).then_inc(act_ev, 1)
                elif k < N_FIRST:
                    act.wait_ge(w_used, w + 1)
                    dst = vraw if k < QT + 4 else kcraw
                    if hf and k >= QT + 4:
                        act.wait_ge(kc_out[k % 2], 64)
                    act.activation(dst[0:HD, k % 2, :], psum[0:HD, bank, :], ACT.Copy).then_inc(act_ev, 1)
                elif k == N_IN - 1:
                    act.wait_ge(w_used, w + 1)
                    act.activation(graw[:, :], psum[:, bank, :], ACT.Copy).then_inc(act_ev, 1)
                elif (k - N_FIRST) % 3 == 0:
                    c = (k - N_FIRST) // 3
                    act.wait_ge(w_used, w + 1)
                    act.wait_ge(dve_ev, DVE_EV * hf + N_FIRST + 2 * c)
                    act.activation(ccs[:, :], psum[:, bank, :], ACT.Copy).then_inc(act_ev, 1)

            def hidden(n):
                act.wait_ge(w1_used, CMP_PC * (n + 1))
                act.activation(hid[0:NB, 0, :], psum[0:NB, n, 0:CMP_HID], ACT.Copy).then_inc(hid_sb, 1)
                act.wait_ge(tanh_arg, n + 1)
                act.activation(hid[0:NB, 2, :], hid[0:NB, 1, :], ACT.Tanh, scale=(2 / 3.141592653589793) ** 0.5)\
                    .then_inc(tanh_out, 1)

            def hidden_turned(n):
                act.wait_ge(hid_tr, n + 1)
                act.activation(hidT[:, :, :], psum[:, n, CMP_HID:CMP_HID + 2 * NB].rearrange("p (t m) -> p t m", t=2),
                               ACT.Copy, scale=0.5).then_inc(hid_tr_sb, 1)

            def compressed_hi(n):
                act.wait_ge(cmp_mm, n + 1)
                if n == 0:
                    act.activation(kcc[:, 0, :, 0:NC], psum[:, 0, 0:NB].rearrange("p (g m) -> p g m", g=NKV),
                                   ACT.Copy).then_inc(cc_hi, 1)
                else:
                    act.activation(vcc[0:NC, :, 0:HD], psum[0:NC, 1, 0:P].rearrange("p (g d) -> p g d", g=NKV),
                                   ACT.Copy).then_inc(cc_hi, 1)

            act.wait_ge(consts, CONSTS_FIRST)
            act.activation(spare[:, :], ones[:, 0:1], ACT.Sqrt)
            for t in range(HT):
                norm_tile(t)
                if t == 1:
                    act.wait_ge(own, NH)
                if t:
                    norm_hi(t - 1)
                if t == 2:
                    w_hi_of(0, 0, 1)
            norm_hi(HT - 1)
            for hf in range(HALVES):
                for k in range(N_IN):
                    w = N_IN * hf + k
                    if w + 1 < W_BACK:
                        next_w(w + 1, (w + 1) // 2 + 1)
                    evacuate(hf, k)
                    if hf == 0:
                        second_norm(k)
                        if k == N_IN - 1:
                            for n in range(HT, NT):
                                norm_hi(n)
                            v_hi(0)
                            for c in range(2):
                                conv_square(0, c)
                    elif k == 0:
                        for c in range(2, CT):
                            conv_square(0, c)
                    elif k == 2:
                        conv_root(0)
                    elif k == 3:
                        gate_exp(0)
                    elif k == CMP_PE[0, 3] + 1:
                        hidden(0)
                    elif k == CMP_PE[0, 3] + 3:
                        hidden_turned(0)
            compressed_hi(0)
            v_hi(1)
            hidden(1)
            gate_exp(1)
            hidden_turned(1)
            compressed_hi(1)

            def exp_item(m):
                n, wc = divmod(m, 2)
                i, s = n // GQA // NKV, slot_of(n)
                n_sel, n_win = P * (i + 1), P * min(i + 1, WIN_T + 1)
                act.wait_ge(wc_read if wc else sel_read, n + 1)
                cols = ((WIN, n_sel, n_win), (CMP, n_sel + n_win, NC)) if wc else ((SEL, 0, n_sel),)
                for br, c0, cn in cols:
                    ins = act.activation(probs[:, s, c0:c0 + cn], probs[:, s, c0:c0 + cn], ACT.Exp, scale=-1.0,
                                         bias=nmax[:, s, br:br + 1], accum_out=rsum[:, s, br:br + 1])
                ins.then_inc(exped, 1)

            def outputs(g):
                act.wait_ge(pv, GROUP_END[g] + 1)
                act.activation(osb[:, g % 2, :], psum[:, 6 + g % 2, :], ACT.Copy).then_inc(o_sb, 1)

            def hi_tile(kt):
                rows = rows_of(kt)
                act.wait_ge(pt, kt + 1)
                if kt >= 3:
                    act.wait_ge(pv, kt - 2)
                act.activation(pthi[kt % 3][0:rows, :], psum[0:rows, 4 + kt % 2, :], ACT.Copy)\
                    .then_inc(pt_hi, 1)
                for g in groups_ending(kt - LAG):
                    outputs(g)

            def square(k, src, col, junk):
                if k:
                    act.wait_ge(s_sq, k)
                act.activation(junk, src, ACT.Square, accum_out=ssq[:, col:col + 1]).then_inc(s_sq, 1)

            def root(ms, c0, c1):
                act.wait_ge(s_ms, ms)
                act.activation(rms[:, c0:c1], ssq[:, c0:c1], ACT.Sqrt).then_inc(s_sq, 1)

            def conv_hi(hf, c):
                act.wait_ge(c_done, CT * hf + c + 1)
                act.activation(mhi[:, hf, c, :], convT[:, c, HN * hf:HN * (hf + 1)], ACT.Copy).then_inc(cm_hi, 1)

            def nsa_hi(t):
                act.wait_ge(tr, TR_NSA + t + 1)
                c = P * (t % HT)
                act.activation(mhi[:, t // HT, CT:KD, c:c + P], psum[:, t % 2, :].rearrange("p (k m) -> p k m", m=P),
                               ACT.Copy).then_inc(tr_hi, 1)

            def beside_last(b):
                if b == 0:
                    root(1, 0, NT - 1)
                    act.wait_ge(qk_wc, UNITS * GQA)
                if 1 <= b <= CT:
                    conv_hi(0, b - 1)
                if 3 <= b < 3 + HT:
                    nsa_hi(b - 3)
                if b in (7, 8):
                    w = W_BACK + b - 7
                    next_w(w, w // 2 + 1)

            for m in range(ITEMS):
                exp_item(m)
            for u in range(UNITS):
                for b in range(BEATS):
                    for kt in beat_tiles(u, b):
                        hi_tile(kt)
                    if b < ITEMS and u + 1 < UNITS:
                        exp_item(ITEMS * (u + 1) + b)
                    if u == UNITS - 1:
                        beside_last(b)
                if u >= NKV and u % NKV == 0:
                    i = u // NKV - 1
                    act.wait_ge(o_done, u)
                    square(i, nsa[:, i, :], i, junk2[:, :])
            for kt in range(N_KT - LAG, N_KT):
                for g in groups_ending(kt):
                    outputs(g)

            def copy_y(n, par, bank):
                act.wait_ge(y_tr, n - 1)
                act.activation(yT[:, par, :], psum[:, bank, :], ACT.Copy).then_inc(y_sb, 1)

            def h_square(k, src, t):
                square(sq_base(k) + t, src[:, t, :], HT * (k % 2) + t, nrm[:, 1, :])

            def h_root(k):
                c0 = HT * (k % 2)
                root(ms_base(k) + 1, c0, c0 + HT)

            def h_hi(hf, t):
                for b in range(2):
                    act.wait_ge(tr, tr_h(hf) + 2 * t + b + 1)
                    act.activation(vhi[:, 4 * b:4 * b + 4, P * t:P * (t + 1)],
                                   psum[:, 2 * (t % 2) + b, :].rearrange("p (k m) -> p k m", m=P),
                                   ACT.Copy).then_inc(tr_hi, 1)

            for n in range(N_OUT):
                w = W_BACK + n
                if n:
                    next_w(w + 1, (w + 1) // 2 + 1)
                act.wait_ge(w_used, w + 1)
                if n >= 2:
                    copy_y(n, n % 2, 4 + n % 2)
                else:
                    act.activation(yT[:, n, :], psum[:, 4 + n, :], ACT.Copy).then_inc(y_sb, 1)
                if n < 2:
                    for c in (2 * n, 2 * n + 1):
                        conv_square(1, c)
                if n == 0:
                    act.wait_ge(o_done, UNITS)
                    square(NT, nsa[:, NT - 1, :], NT - 1, junk3[:, :])
                if n == 1:
                    root(3, NT - 1, NT)
                if n == 2:
                    conv_root(1)
                if 2 <= n < 2 + HT:
                    nsa_hi(n + 2)
                if n in (4, 5):
                    for c in (2 * n - 8, 2 * n - 7):
                        conv_hi(1, c)
                if n in (KD + 2, KD + 3):
                    act.wait_ge(y_add, KD)
                    act.wait_ge(cm_lo, HALVES * CT)
                    for t in (0, 1) if n == KD + 2 else (2, 3):
                        h_square(0, res[0], t)
                if n == KD + 4:
                    h_root(0)
                if n >= N_OUT - 2:
                    for t in (0, 1) if n == N_OUT - 2 else (2, 3):
                        h_hi(0, t)

            for hf in range(HALVES):
                w0, f0 = w_of(hf, "glu"), FT * hf

                def silu_of(f, par):
                    act.activation(silu[:, par, :], psum[:, 2 * par, :], ACT.Silu).then_inc(sil, 1)

                def glu_step(f, par, first):
                    a = w0 + 1
                    act.wait_ge(w_used, f * 2 + (a - 1))
                    w_hi_of(f * 2 + a, slot(a), f + (a // 2 + 1))
                    if not first:
                        silu_of(f - 1, 1 - par)
                    b = w0 + 2
                    act.wait_ge(w_used, f * 2 + (b - 1))
                    w_hi_of(f * 2 + b, slot(b), f + (b // 2 + 1))
                    if not first:
                        act.wait_ge(glu, f + f0)
                        act.activation(hhi[:, ds(f - 1, 1), :],
                                       silu[:, 1 - par:2 - par, :], ACT.Copy).then_inc(g_hi, 1)

                glu_step(0, 0, True)
                if hf:
                    act.wait_ge(y_add, N_OUT + KD)
                    for t in range(HT):
                        h_square(2, res[0], t)
                    h_root(2)
                glu_step(1, 1, False)
                with act.Fori(2, FT, 2) as f:
                    for d in range(2):
                        act.wait_ge(g_lo, f + (f0 + d - 1))
                        glu_step(f + d, d, False)
                act.wait_ge(w_used, w0 + 2 * FT)
                act.wait_ge(g_lo, f0 + FT - 2)
                silu_of(FT - 1, 1)
                act.wait_ge(glu, f0 + FT)
                act.activation(hhi[:, FT - 1, :], silu[:, 1, :], ACT.Copy).then_inc(g_hi, 1)

                w0, y0 = w_of(hf, "down"), N_OUT + KD * hf
                last_w = w0 + NPC * KD - 1
                with act.Fori(0, KD // 2 - 1) as mm:
                    for e in range(2):
                        for n in range(NPC):
                            d = NPC * e + n + 1
                            nk = PIECES[(n + 1) % NPC][1]
                            act.wait_ge(w_used, mm * (2 * NPC) + (w0 + d - 1))
                            w_hi_of(mm * (2 * NPC) + (w0 + d), slot(w0 + d), mm * NPC + ((w0 + d) // 2 + 1), nk * P)
                        act.wait_ge(w_used, mm * (2 * NPC) + (w0 + NPC * (e + 1)))
                        copy_y(mm * 2 + (y0 + e), e, 4 + e)
                for e in range(2):
                    for n in range(NPC):
                        w = w0 + NPC * (KD - 2 + e) + n + 1
                        if w < W_END:
                            next_w(w, w // 2 + 1, PIECES[(n + 1) % NPC][1] * P if w <= last_w else 1024)
                        if hf and e == 1:
                            if n == 0:
                                act.activation(spare[:, :], ones[:, 0:1], ACT.Sqrt)
                            if n == 1:
                                act.wait_ge(y_add, y0 + KD - 1)
                                for t in range(HT):
                                    square(sq_base(3) + t, res[1][:, t, 0:DM - P], HT + t, nrm[:, 1, 0:DM - P])
                        if hf == 0 and e == 0:
                            if n < 2:
                                for t in (2 * n, 2 * n + 1):
                                    h_square(1, res[1], t)
                            else:
                                h_root(1)
                    act.wait_ge(w_used, w0 + NPC * (KD - 2 + e + 1))
                    copy_y(y0 + KD - 2 + e, e, 4 + e)
                    if hf == 0:
                        for t in (2 * e, 2 * e + 1):
                            h_hi(1, t)
            act.wait_ge(y_add, N_OUT + 2 * KD)
            for t in range(HT):
                act.wait_ge(s_sq, sq_base(3) + HT + t)
                act.activation(nrm[:, 1, 0:P], res[1][:, t, DM - P:DM], ACT.Square,
                               accum_out=rms[:, HT + t:HT + t + 1]).then_inc(s_sq, 1)
            root(ms_base(3) + 1, HT, NT)
            act.wait_ge(s_ms, ms_base(3) + 2)
            act.activation(res[1][:, HT - 1, :], res[1][:, HT - 1, :], ACT.Copy, scale=inv[:, NT - 1:NT])\
                .then_inc(scaled, 1)

        @block.tensor
        def _(pe):
            def mm3(bank_ap, w_ap_hi, w_ap_lo, x_hi, x_lo, first, last):
                pe.matmul(bank_ap, w_ap_hi, x_hi, start=first, stop=False)
                pe.matmul(bank_ap, w_ap_hi, x_lo, start=False, stop=False)
                return pe.matmul(bank_ap, w_ap_lo, x_hi, start=False, stop=last)

            def dense(par, bank, xh, xl, k0=0, nk=KD, first=True, last=True):
                for k in range(nk):
                    c = slice(P * k, P * (k + 1))
                    ins = mm3(psum[:, bank, :], whi[:, par, c], wlo[:, par, c], xh[:, k0 + k, :], xl[:, k0 + k, :],
                              first and k == 0, last and k == nk - 1)
                return ins

            def norm_turn(n):
                pe.wait_ge(x_n, n + 1)
                for b in range(2):
                    if n >= 2:
                        pe.wait_ge(tr_lo, 2 * (n - 2) + b + 1)
                    for k in range(4):
                        ins = pe.transpose(psum[:, 2 * (n % 2) + b, P * k:P * (k + 1)],
                                           xin[n // HT][:, n % HT, P * (4 * b + k):P * (4 * b + k + 1)], ident[:, :])
                    ins.then_inc(tr, 1)

            def first_tile(hf, k):
                w = N_IN * hf + k
                pe.wait_ge(w_lo, w + 1)
                dense(slot(w), 4 + k, uhi, ulo).then_inc(w_used, 1)

            def first_tiles(hf):
                w0, A0, D0 = N_IN * hf, ACT_EV * hf, DVE_EV * hf
                with pe.Fori(2, N_FIRST, 2) as k:
                    for d in range(2):
                        pe.wait_ge(w_lo, k + (w0 + d + 1))
                        pe.wait_ge(act_ev, k + (A0 + d - 1))
                        pe.wait_ge(dve_ev, k + (D0 + d - 1))
                        dense(slot(w0 + d), 4 + d, uhi, ulo).then_inc(w_used, 1)
                pe.wait_ge(act_ev, A0 + N_FIRST)

            def v_turn(hf, n):
                if n < 2:
                    pe.wait_ge(dve_ev, DVE_EV * hf + N_FIRST)
                if n == 0 and hf:
                    pe.wait_ge(gexp, hf)
                if n == 1 and hf:
                    pe.wait_ge(vt_hi, 2 * hf)
                    pe.wait_ge(vt_lo, 2 * hf)
                if n == 2:
                    pe.wait_ge(act_ev, ACT_EV * (hf + 1))
                    pe.wait_ge(vt_hi, 2 * hf + 1)
                    pe.wait_ge(vt_lo, 2 * hf + 1)
                for t in range(HT):
                    src = (vraw[:, 0, :], vraw[:, 1, :], graw[:, :])[n]
                    ins = pe.transpose(psum[:, (6, 7, 6)[n], P * t:P * (t + 1)], src[:, P * t:P * (t + 1)],
                                       ident[:, :])
                ins.then_inc(vt, 1)

            def conv_sum(hf, c):
                pe.wait_ge(c_sq, CT * hf + c + 1)
                pe.matmul(psum[:, 2, :], ones[:, :], csq[hf][:, c % 2, :], start=c == 0, stop=c == CT - 1)\
                    .then_inc(c_ss, 1)

            def compress(n, pc):
                j = CMP_PC * n + pc
                pe.wait_ge(b_raw, n + 1)
                pe.wait_ge(w1_in[j % 2], 16 * (j // 2 + 1))
                for q in range(LP // CMP_PC):
                    lp = LP // CMP_PC * pc + q
                    ins = pe.matmul(psum[0:NB, n, 0:CMP_HID], blk[:, lp, :],
                                    w1[:, j % 2, CMP_HID * q:CMP_HID * (q + 1)], start=lp == 0, stop=lp == LP - 1)
                ins.then_inc(w1_used, 1)

            def hidden_turn(n):
                pe.wait_ge(gelu_out, n + 1)
                for t in range(2):
                    ins = pe.transpose(psum[:, n, CMP_HID + NB * t:CMP_HID + NB * (t + 1)],
                                       hid[0:NB, 3, P * t:P * (t + 1)], ident[0:NB, 0:NB])
                ins.then_inc(hid_tr, 1)

            def second_product(n):
                pe.wait_ge(hid_tr_sb, n + 1)
                if n == 0:
                    for t in range(2):
                        ins = pe.matmul(psum[:, 0, 0:NB], w2d[:, 0, t, :], hidT[:, t, :], start=t == 0, stop=t == 1)
                else:
                    for g in range(NKV):
                        for t in range(2):
                            ins = pe.matmul(psum[0:NC, 1, HD * g:HD * (g + 1)], hidT[:, t, NC * g:NC * (g + 1)],
                                            w2d[:, 1, t, 0:HD], start=t == 0, stop=t == 1)
                ins.then_inc(cmp_mm, 1)

            pe.wait_ge(consts, CONSTS_FIRST)
            for n in range(HT):
                norm_turn(n)
            pe.wait_ge(tr_hi, 2 * HT)
            pe.wait_ge(tr_lo, 2 * HT)
            for k in range(2):
                first_tile(0, k)
            first_tiles(0)
            with pe.Fori(0, CT, 2) as c:
                for e in range(2):
                    for n in range(3):
                        d = 3 * e + n
                        wd = N_FIRST + d
                        pe.wait_ge(w_lo, c * 3 + (wd + 1))
                        if n == 0:
                            pe.wait_ge(dve_ev, c * 2 + (N_FIRST + 2 * e - 1))
                        elif n == 1:
                            pe.wait_ge(dve_ev, c * 2 + (N_FIRST + 2 * e))
                        else:
                            pe.wait_ge(act_ev, c + (N_FIRST + e + 1))
                        dense(slot(wd), 4 + wd % 2, uhi, ulo).then_inc(w_used, 1)
            for n in range(HT, HT + 2):
                norm_turn(n)
            pe.wait_ge(w_lo, N_IN)
            pe.wait_ge(dve_ev, DVE_EV - 1)
            dense(slot(N_IN - 1), 4 + (N_IN - 1) % 2, uhi, ulo).then_inc(w_used, 1)
            for n in range(2):
                v_turn(0, n)
            for n in range(HT + 2, NT):
                norm_turn(n)

            pe.wait_ge(tr_hi, 2 * NT)
            pe.wait_ge(tr_lo, 2 * NT)
            pe.wait_ge(act_ev, ACT_EV)
            pe.wait_ge(dve_ev, DVE_EV)
            for k in range(2):
                first_tile(1, k)
                for c in (2 * k, 2 * k + 1):
                    conv_sum(0, c)
            v_turn(0, 2)
            first_tiles(1)
            for k in range(N_FIRST, N_IN):
                w = N_IN + k
                c, n = divmod(k - N_FIRST, 3)
                pe.wait_ge(w_lo, w + 1)
                if n == 0:
                    pe.wait_ge(dve_ev, DVE_EV + N_FIRST + 2 * c - 1)
                elif n == 1:
                    pe.wait_ge(dve_ev, DVE_EV + N_FIRST + 2 * c)
                else:
                    pe.wait_ge(act_ev, ACT_EV + N_FIRST + c + 1)
                dense(slot(w), 4 + k % 2, uhi, ulo).then_inc(w_used, 1)
                if k == N_IN - 1:
                    for n in range(2):
                        v_turn(1, n)
                for n, pc in CMP_PE:
                    if CMP_PE[n, pc] == k:
                        compress(n, pc)
                if k == CMP_PE[0, 3] + 2:
                    hidden_turn(0)
                if k == CMP_PE[0, 3] + 3:
                    second_product(0)
            v_turn(1, 2)

            def scores(m):
                n, wc = divmod(m, 2)
                u, j = divmod(n, GQA)
                i, g = divmod(u, NKV)
                q = qs[:, i // HT, GQA * g + j, P * (i % HT):P * (i % HT + 1)]
                n_sel, n_win = P * (i + 1), P * min(i + 1, WIN_T + 1)

                def against(br, bank, start_key, keys):
                    for c in range(0, keys, 512):
                        cn = min(512, keys - c)
                        o = psum[:, bank + c // 512, 0:cn]
                        for part in range(2):
                            ins = pe.matmul(o, q, ks[:, br, part, g, start_key + c:start_key + c + cn],
                                            start=part == 0, stop=part == 1)
                    return ins

                if n >= ahead(m):
                    pe.wait_ge(wc_read if wc else sel_read, n + 1 - ahead(m))
                if u == HT * NKV and j == 0:
                    pe.wait_ge(ks_out[1], 16 * 8)
                sel_bank, win_bank, (cmp_bank, cmp_col) = score_banks(n)
                if wc:
                    against(1, win_bank, n_sel - n_win, n_win)
                    for part in range(2):
                        ins = pe.matmul(psum[:, cmp_bank, cmp_col:cmp_col + NC + 1], q, kcc[:, part, g, :],
                                        start=part == 0, stop=part == 1)
                    ins.then_inc(qk_wc, 1)
                else:
                    against(0, sel_bank, 0, n_sel).then_inc(qk_sel, 1)

            def transposes(kt):
                u = unit_of(kt)
                col, rows = KTS[u][kt - KT_BASE[u]][2], rows_of(kt)
                if kt == KT_BASE[u]:
                    pe.wait_ge(exped, ITEMS * (u + 1))
                if kt >= 2:
                    pe.wait_ge(pt_lo, kt - 1)
                for j in range(GQA):
                    s = slot_of(GQA * u + j)
                    ins = pe.transpose(psum[0:rows, 4 + kt % 2, P * j:P * (j + 1)], probs[:, s, col:col + rows],
                                       ident[:, :])
                ins.then_inc(pt, 1)

            def values(kt):
                u = unit_of(kt)
                br, t, _ = KTS[u][kt - KT_BASE[u]]
                g, rows, group = u % NKV, rows_of(kt), NBR * u + br
                v = vcc[0:rows, g, :] if br == 2 else vs[:, br, t, g, :]
                pe.wait_ge(pt_lo, kt + 1)
                first, last = kt == GROUP_START[group], kt == GROUP_END[group]
                if first and group >= 2:
                    pe.wait_ge(o_part, group - 1)
                o = psum[:, 6 + group % 2, :]
                pe.matmul(o, v, pthi[kt % 3][0:rows, :], start=first, stop=False)
                pe.matmul(o, v, ptlo[kt % 3][0:rows, :], start=False, stop=last).then_inc(pv, 1)
                for e in groups_ending(kt - 1):
                    folded(e)

            def folded(g):
                pe.wait_ge(o_sb, g + 1)
                for j in range(GQA):
                    ins = pe.matmul(psum[:, 6 + g % 2, HD * j:HD * (j + 1)], osb[:, g % 2, P * j:P * (j + 1)],
                                    fold[:, :], start=True, stop=True)
                ins.then_inc(o_tok, 1)

            hidden_turn(1)
            second_product(1)
            pe.wait_ge(ks_out[0], 16 * 8)
            for k in range(2):
                pe.wait_ge(q_out[k], 64 * HALVES * QT // 2)
            pe.wait_ge(cc_lo, 1)
            for m in range(ITEMS + ahead(ITEMS)):
                if m == 2:
                    pe.wait_ge(cc_lo, 2)
                scores(m)
            pe.wait_ge(vt_lo, 2 * HALVES)
            pe.wait_ge(vt_hi, 2 * HALVES)

            def nsa_turn(t):
                pe.wait_ge(s_n, t + 1)
                pe.wait_ge(tr_lo, TR_NSA + t - 1)
                for k in range(CT):
                    ins = pe.transpose(psum[:, t % 2, P * k:P * (k + 1)],
                                       nnsa[t // HT][:, t % 2, P * k:P * (k + 1)], ident[:, :])
                ins.then_inc(tr, 1)

            for u in range(UNITS):
                for b in range(BEATS):
                    for kt in beat_tiles(u, b):
                        transposes(kt)
                        if kt >= LAG:
                            values(kt - LAG)
                    read = ITEMS * (u + 1) + b
                    for m in range(read + 1, min(read + 3, N_ITEMS)) if b < ITEMS else ():
                        if m - ahead(m) == read:
                            scores(m)
                    if u == UNITS - 1 and 2 <= b < 2 + HT:
                        nsa_turn(b - 2)
            for kt in range(N_KT - LAG, N_KT):
                values(kt)

            def turn(n, par):
                pe.wait_ge(y_sb, n + 1)
                for t in range(HT):
                    ins = pe.transpose(psum[:, 6 + par, P * t:P * (t + 1)], yT[:, par, P * t:P * (t + 1)],
                                       ident[:, :])
                ins.then_inc(y_tr, 1)

            def project(n, par, hf):
                pe.wait_ge(w_lo, n + (W_BACK + 1))
                dense(slot(W_BACK + par), 4 + par, mhi[:, hf], mlo[:, hf]).then_inc(w_used, 1)

            def h_turn(hf, t):
                pe.wait_ge(s_n, NT + HT * hf + t + 1)
                for b in range(2):
                    n = tr_h(hf) + 2 * t + b
                    pe.wait_ge(tr_lo, n - 3 if t >= 2 else tr_h(hf))
                    for k in range(4):
                        ins = pe.transpose(psum[:, 2 * (t % 2) + b, P * k:P * (k + 1)],
                                           nrm[:, t % 2, P * (4 * b + k):P * (4 * b + k + 1)], ident[:, :])
                    ins.then_inc(tr, 1)

            pe.wait_ge(tr_lo, TR_NSA + HT)
            pe.wait_ge(tr_hi, TR_NSA + HT)
            pe.wait_ge(cm_lo, CT)
            project(0, 0, 0)
            for g in groups_ending(N_KT - 1):
                folded(g)
            project(1, 1, 0)
            for c in range(2):
                conv_sum(1, c)
            for n in range(2, KD):
                pe.wait_ge(y_sb, n - 1)
                project(n, n % 2, 0)
                if n == 2:
                    for c in range(2, CT):
                        conv_sum(1, c)
                if n < 4:
                    pe.wait_ge(o_part, NBR * UNITS)
                else:
                    pe.wait_ge(y_add, n - 3)
                turn(n - 2, n % 2)
                if n < 2 + HT:
                    nsa_turn(n + 2)
            pe.wait_ge(tr_lo, TR_NSA + NT)
            pe.wait_ge(tr_hi, TR_NSA + NT)
            pe.wait_ge(cm_lo, HALVES * CT)

            def out_step(n, par):
                pe.wait_ge(y_sb, n - 1)
                project(n, par, 1)
                pe.wait_ge(y_add, n - 3)
                turn(n - 2, par)

            with pe.Fori(KD, N_OUT - 2, 2) as n:
                for d in range(2):
                    out_step(n + d, d)
            for e in range(2):
                out_step(N_OUT - 2 + e, e)
                for t in (2 * e, 2 * e + 1):
                    h_turn(0, t)
            for e in range(2):
                pe.wait_ge(y_add, N_OUT - 3 + e)
                turn(N_OUT - 2 + e, e)

            for hf in range(HALVES):
                pe.wait_ge(tr_hi, tr_h(hf) + 2 * HT)
                pe.wait_ge(tr_lo, tr_h(hf) + 2 * HT)
                w0, f0 = w_of(hf, "glu"), FT * hf
                for f in range(2):
                    for d in range(2):
                        pe.wait_ge(w_lo, w0 + 2 * f + d + 1)
                        dense(slot(w0 + d), 2 * f + d, vhi, vlo).then_inc(w_used, 1)
                with pe.Fori(2, FT, 2) as f:
                    for e in range(2):
                        pe.wait_ge(glu, f + (f0 + e - 1))
                        for d in range(2):
                            pe.wait_ge(w_lo, f * 2 + (w0 + 2 * e + d + 1))
                            dense(slot(w0 + d), 2 * e + d, vhi, vlo).then_inc(w_used, 1)
                w0, y0 = w_of(hf, "down"), N_OUT + KD * hf

                def down(m, e, first=False, last=False):
                    pe.wait_ge(y_sb, m + (y0 + e - 1))
                    for n, (k0, nk) in enumerate(PIECES):
                        d = NPC * e + n
                        if last and n == 1:
                            for y in range(y0 + KD - 3, y0 + KD - 1):
                                pe.wait_ge(y_add, y - 1)
                                turn(y, y % 2)
                        if first:
                            pe.wait_ge(g_lo, f0 + k0 + nk)
                            pe.wait_ge(g_hi, f0 + k0 + nk)
                        pe.wait_ge(w_lo, m * NPC + (w0 + d + 1))
                        dense(slot(w0 + d), 4 + e, hhi, hlo, k0, nk, n == 0, n == NPC - 1).then_inc(w_used, 1)

                def down_step(m, e):
                    down(m, e)
                    pe.wait_ge(y_add, m + (y0 + e - 3))
                    turn(m + (y0 + e - 2), e)

                for e in range(2):
                    down(0, e, e == 0)
                with pe.Fori(2, KD - 2, 2) as m:
                    for e in range(2):
                        down_step(m, e)
                down_step(KD - 2, 0)
                for t in range(2) if hf == 0 else ():
                    h_turn(1, t)
                down(KD - 2, 1, last=True)
                for t in range(2, HT) if hf == 0 else ():
                    h_turn(1, t)
                pe.wait_ge(y_add, y0 + KD - 2)
                turn(y0 + KD - 1, 1)

        @block.vector
        def _(dve):
            class Own:
                n = 0

            def did(ins):
                ins.then_inc(own, 1)
                Own.n += 1

            def settle():
                dve.wait_ge(own, Own.n)

            for h in range(NH):
                did(dve.memset(qscale[HD * (h % 2):HD * (h % 2 + 1), h // 2:h // 2 + 1],
                               HD ** -0.5 * 2.0 ** (h + 1)))
            def norm_tile(t):
                dve.wait_ge(x_sq, 2 * t + 1)
                dve.tensor_scalar(ssq[:, t:t + 1], ssq[:, t:t + 1], 1.0 / DM, EPS, ALU.mult, ALU.add)\
                    .then_inc(x_ms, 1)
                dve.wait_ge(x_sq, 2 * t + 2)
                dve.reciprocal(inv[:, t:t + 1], rms[:, t:t + 1]).then_inc(x_ms, 1)
                dve.wait_ge(x_ms, 2 * t + 2)
                if t == 0:
                    dve.wait_ge(g1_in, 16)
                norm_x(t)

            def norm_x(n):
                o = xin[n // HT][:, n % HT, :]
                dve.scalar_tensor_tensor(o, o, inv[:, n:n + 1], g1b[:, :], ALU.mult, ALU.mult).then_inc(x_n, 1)

            def norm_lo(n):
                t = n % HT
                for b in range(2):
                    dve.wait_ge(tr_hi, 2 * n + b + 1)
                    sl = (slice(None), slice(4 * b, 4 * b + 4), slice(P * t, P * (t + 1)))
                    dve.tensor_tensor(ulo[sl], psum[:, 2 * (n % 2) + b, :].rearrange("p (k m) -> p k m", m=P),
                                      raw(uhi[sl]), ALU.subtract).then_inc(tr_lo, 1)

            def second_norm(k):
                if k == 2:
                    dve.wait_ge(x2_sq, HT)
                    dve.tensor_scalar(ssq[:, HT:NT], ssq[:, HT:NT], 1.0 / DM, EPS, ALU.mult, ALU.add)\
                        .then_inc(x2_ms, 1)
                if k == 4:
                    dve.wait_ge(x2_sq, HT + 1)
                    dve.reciprocal(inv[:, HT:NT], rms[:, HT:NT]).then_inc(x2_ms, 1)
                    dve.wait_ge(x2_ms, 2)
                if 4 <= k < 4 + HT:
                    norm_x(k - 4 + HT)

            def v_lo(hf):
                for br in range(2):
                    dve.wait_ge(vt_hi, 2 * hf + br + 1)
                    tt = slice(HT * hf, HT * (hf + 1))
                    dve.tensor_tensor(vs[:, br, tt, :, HD:2 * HD],
                                      psum[:, 6 + br, :].rearrange("p (t g d) -> p t g d", t=HT, g=NKV),
                                      raw(vs[:, br, tt, :, 0:HD]), ALU.subtract).then_inc(vt_lo, 1)

            def gate(hf):
                dve.wait_ge(gexp, hf + 1)
                g_ap = gates[:, HT * hf:HT * (hf + 1), :]
                did(dve.tensor_scalar(g_ap, g_ap, 1.0, None, ALU.add))
                settle()
                did(dve.reciprocal(g_ap, g_ap))

            def conv_mean(hf):
                dve.wait_ge(c_ss, CT * (hf + 1))
                dve.tensor_scalar(crms[hf][:, :], psum[:, 2, :], 1.0 / CONV, EPS, ALU.mult, ALU.add)\
                    .then_inc(c_ms, 1)

            def conv_inverse(hf):
                dve.wait_ge(c_rt, hf + 1)
                did(dve.reciprocal(crms[hf][:, :], crms[hf][:, :]))
                settle()

            def conv_norm(hf, c):
                ct = convT[:, c, HN * hf:HN * (hf + 1)]
                dve.scalar_tensor_tensor(ct, ct, gconv[:, c:c + 1], crms[hf][:, :], ALU.mult, ALU.mult)\
                    .then_inc(c_done, 1)

            def block_raw(n):
                dve.wait_ge(kc_out[n], 64 * HALVES)
                if n:
                    dve.wait_ge(w1_used, CMP_PC)
                for g in range(NKV):
                    src = kcs[:, n, g, 0:CMP_STRIDE * (NC - 1) + CMP_BLOCK]\
                        .rearrange("p (b l) -> p l b", l=CMP_STRIDE)
                    for part in range(2):
                        lh = LP // 2
                        o = blk[:, lh * part:lh * (part + 1), NC * g:NC * (g + 1)]
                        i0 = src[:, 0:CMP_STRIDE:2, part:part + NC]
                        i1 = pos[:, n, lh * part:lh * (part + 1)].unsqueeze(2).broadcast_to([P, lh, NC])
                        ins = dve.tensor_tensor(o, i0, i1, ALU.add)
                        if g == NKV - 1 and part == 1:
                            ins.then_inc(b_raw, 1)
                        else:
                            did(ins)

            def gelu(n, step):
                h = hid[0:NB]
                if step == 0:
                    dve.wait_ge(hid_sb, n + 1)
                    did(dve.tensor_tensor(h[:, 1, :], h[:, 0, :], h[:, 0, :], ALU.mult))
                    settle()
                    did(dve.tensor_scalar(h[:, 1, :], h[:, 1, :], 0.044715, 1.0, ALU.mult, ALU.add))
                    settle()
                    dve.tensor_tensor(h[:, 1, :], h[:, 1, :], h[:, 0, :], ALU.mult).then_inc(tanh_arg, 1)
                else:
                    dve.wait_ge(tanh_out, n + 1)
                    dve.scalar_tensor_tensor(h[:, 3, :], h[:, 2, :], 1.0, h[:, 0, :], ALU.add, ALU.mult)\
                        .then_inc(gelu_out, 1)

            def compressed_lo(n):
                dve.wait_ge(cc_hi, n + 1)
                if n == 0:
                    dve.tensor_tensor(kcc[:, 1, :, 0:NC], psum[:, 0, 0:NB].rearrange("p (g m) -> p g m", g=NKV),
                                      raw(kcc[:, 0, :, 0:NC]), ALU.subtract).then_inc(cc_lo, 1)
                else:
                    dve.tensor_tensor(vcc[0:NC, :, HD:2 * HD],
                                      psum[0:NC, 1, 0:P].rearrange("p (g d) -> p g d", g=NKV),
                                      raw(vcc[0:NC, :, 0:HD]), ALU.subtract).then_inc(cc_lo, 1)

            def evacuate(hf, k):
                w, tok, bank = N_IN * hf + k, HN * hf, 4 + k % 2
                if k < QT:
                    dve.wait_ge(act_ev, ACT_EV * hf + k + 1)
                    dve.scalar_tensor_tensor(qstage[:, k % 2, 1, :], psum[:, bank, :], qscale[:, k:k + 1],
                                             raw(qstage[:, k % 2, 0, :]), ALU.mult, ALU.subtract).then_inc(dve_ev, 1)
                elif k < QT + 2:
                    dve.wait_ge(act_ev, ACT_EV * hf + k + 1)
                    dve.tensor_tensor(kT[:, k - QT, 1, tok:tok + HN], psum[:, bank, :],
                                      raw(kT[:, k - QT, 0, tok:tok + HN]), ALU.subtract).then_inc(dve_ev, 1)
                elif k < N_FIRST:
                    dve.wait_ge(w_used, w + 1)
                    dst = vraw if k < QT + 4 else kcraw
                    if hf and k >= QT + 4:
                        dve.wait_ge(kc_out[k % 2], 64)
                    dve.tensor_copy(dst[HD:P, k % 2, :], psum[HD:P, bank, :]).then_inc(dve_ev, 1)
                elif k < N_IN - 1:
                    c, n = divmod(k - N_FIRST, 3)
                    if n == 1:
                        if c == 0 and hf == 0:
                            dve.wait_ge(vecs, VECS)
                        did(dve.tensor_copy(useq[:, 0:2], carry[:, c, :]))
                        dve.wait_ge(act_ev, ACT_EV * hf + N_FIRST + c + 1)
                        dve.wait_ge(w_used, w + 1)
                        dve.tensor_tensor(useq[:, 2:HN + 2], psum[:, bank, :], ccs[:, :], ALU.mult)\
                            .then_inc(dve_ev, 1)
                        dve.wait_ge(dve_ev, DVE_EV * hf + N_FIRST + 2 * c + 1)
                        settle()
                        did(dve.tensor_scalar(cacc[:, :], useq[:, 0:HN], taps[:, 0, c:c + 1], None, ALU.mult))
                        for n in (1, 2):
                            settle()
                            did(dve.scalar_tensor_tensor(cacc[:, :], useq[:, n:n + HN], taps[:, n, c:c + 1],
                                                         cacc[:, :], ALU.mult, ALU.add))
                        if hf == 0:
                            did(dve.tensor_copy(carry[:, c, :], useq[:, HN:HN + 2]))
                    elif n == 2:
                        dve.wait_ge(w_used, w + 1)
                        settle()
                        dve.tensor_tensor(convT[:, c, tok:tok + HN], cacc[:, :], psum[:, bank, :],
                                          ALU.mult).then_inc(dve_ev, 1)
                        dve.wait_ge(dve_ev, DVE_EV * hf + N_FIRST + 2 * c + 2)

            dve.wait_ge(consts, CONSTS_FIRST)
            for t in range(HT):
                norm_tile(t)
                if t:
                    norm_lo(t - 1)
            norm_lo(HT - 1)
            for hf in range(HALVES):
                for k in range(N_IN):
                    evacuate(hf, k)
                    if hf == 0:
                        second_norm(k)
                        if k == N_IN - 1:
                            for n in range(HT, NT):
                                norm_lo(n)
                            v_lo(0)
                    elif k == 2:
                        conv_mean(0)
                    elif k == 3:
                        conv_inverse(0)
                    elif k == 4:
                        for c in range(CT):
                            conv_norm(0, c)
                        gate(0)
                    elif k == N_FIRST + 2:
                        block_raw(0)
                    elif k == CMP_PE[0, 3] + 1:
                        for step in range(2):
                            gelu(0, step)
                        block_raw(1)
            compressed_lo(0)
            v_lo(1)
            for step in range(2):
                gelu(1, step)
            gate(1)
            compressed_lo(1)

            def masked(m):
                n, wc = divmod(m, 2)
                u, j = divmod(n, GQA)
                i, g = divmod(u, NKV)
                s = slot_of(n)
                slope = 2.0 ** -(GQA * g + j + 1)
                n_sel, n_win = P * (i + 1), P * min(i + 1, WIN_T + 1)
                flat = psum[:, :, :].rearrange("p b m -> p (b m)")
                sel_bank, win_bank, (cmp_bank, cmp_col) = score_banks(n)

                def one(br, col, cols, src, dist):
                    return dve.tensor_tensor_reduce(
                        out=probs[:, s, col:col + cols], in0=src, in1=dist, scale=-slope, scalar=-FLOOR,
                        op0=ALU.add, op1=ALU.min, accum_out=nmax[:, s, br:br + 1])

                if m == 0:
                    dve.wait_ge(w_used, W_BACK)
                if m == ITEMS:
                    dve.wait_ge(ks_out[1], 16 * 8)
                if u >= 2 and m % ITEMS == 0:
                    dve.wait_ge(pt, KT_BASE[u - 1])
                if wc:
                    dve.wait_ge(qk_wc, n + 1)
                    one(WIN, n_sel, n_win, flat[:, 512 * win_bank:512 * win_bank + n_win],
                        dwin[:, WINDOW + P - n_win:WINDOW + P])
                    one(CMP, n_sel + n_win, NC, psum[:, cmp_bank, cmp_col:cmp_col + NC], dcmp[:, i, :])\
                        .then_inc(wc_read, 1)
                else:
                    dve.wait_ge(qk_sel, n + 1)
                    one(SEL, 0, n_sel, flat[:, 512 * sel_bank:512 * sel_bank + n_sel], dsel[:, SEQ - n_sel:SEQ])\
                        .then_inc(sel_read, 1)

            def weigh(u, step):
                i, g = divmod(u, NKV)
                s = slice(slot_of(GQA * u), slot_of(GQA * u) + GQA)
                if step == 0:
                    dve.wait_ge(exped, ITEMS * (u + 1))
                    did(dve.tensor_scalar(rsafe[:, s, :], rsum[:, s, :], 1e-30, None, ALU.max))
                elif step == 1:
                    settle()
                    did(dve.reciprocal(rinv[:, s, :], rsafe[:, s, :]))
                else:
                    settle()
                    did(dve.tensor_tensor(wgt[:, s, :], rinv[:, s, :],
                                          gates[:, i, NBR * GQA * g:NBR * GQA * (g + 1)]
                                          .rearrange("p (h b) -> p h b", b=NBR), ALU.mult))

            def weighed(gr):
                u, br = divmod(gr, NBR)
                s0 = slot_of(GQA * u)
                w = wgt[:, s0:s0 + GQA, (SEL, WIN, CMP)[br]].unsqueeze(2).broadcast_to([P, GQA, HD])
                dve.wait_ge(o_tok, gr + 1)
                settle()
                if u >= 2:
                    dve.wait_ge(o_done, u - 1)
                dve.tensor_tensor(parts[:, u % 2, br, :].rearrange("p (h d) -> p h d", d=HD),
                                  psum[:, 6 + gr % 2, 0:GQA * HD].rearrange("p (h d) -> p h d", d=HD), w,
                                  ALU.mult).then_inc(o_part, 1)

            def lo_tile(kt):
                rows = rows_of(kt)
                dve.wait_ge(pt_hi, kt + 1)
                dve.tensor_tensor(ptlo[kt % 3][0:rows, :], psum[0:rows, 4 + kt % 2, :],
                                  raw(pthi[kt % 3][0:rows, :]), ALU.subtract).then_inc(pt_lo, 1)
                for gr in groups_ending(kt - LAG - 1):
                    weighed(gr)

            def mean(c0, c1, width, squares):
                dve.wait_ge(s_sq, squares)
                dve.tensor_scalar(ssq[:, c0:c1], ssq[:, c0:c1], 1.0 / width, EPS, ALU.mult, ALU.add)\
                    .then_inc(s_ms, 1)

            def inverse(steps, c0, c1, roots):
                dve.wait_ge(s_sq, roots)
                dve.reciprocal(inv[:, c0:c1], rms[:, c0:c1]).then_inc(s_ms, 1)
                dve.wait_ge(s_ms, steps)

            def nsa_norm(t):
                if t % HT >= 2:
                    dve.wait_ge(tr, TR_NSA + t - 1)
                dve.scalar_tensor_tensor(nnsa[t // HT][:, t % 2, :], nsa[:, t, :], inv[:, t:t + 1], gnsa[:, :],
                                         ALU.mult, ALU.mult).then_inc(s_n, 1)

            def nsa_lo(t):
                dve.wait_ge(tr_hi, TR_NSA + t + 1)
                c = P * (t % HT)
                dve.tensor_tensor(mlo[:, t // HT, CT:KD, c:c + P],
                                  psum[:, t % 2, :].rearrange("p (k m) -> p k m", m=P),
                                  raw(mhi[:, t // HT, CT:KD, c:c + P]), ALU.subtract).then_inc(tr_lo, 1)

            def beside_last(b):
                if b == 1:
                    inverse(2, 0, NT - 1, NT)
                    dve.wait_ge(gn_in, 16)
                    dve.wait_ge(qk_wc, UNITS * GQA)
                if 1 <= b < 1 + HT:
                    nsa_norm(b - 1)
                if 3 <= b < 3 + HT:
                    nsa_lo(b - 3)

            dve.wait_ge(consts, CONSTS_ALL)
            for m in range(ITEMS):
                masked(m)
            for u in range(UNITS):
                if u == UNITS - 1:
                    mean(0, NT - 1, NH * HD, NT - 1)
                for b in range(BEATS):
                    if b < ITEMS and u + 1 < UNITS:
                        masked(ITEMS * (u + 1) + b)
                    if b < 3:
                        weigh(u, b)
                    for kt in range(N_KT):
                        if lo_beat(kt) == BEATS * u + b:
                            lo_tile(kt)
                    if u == UNITS - 1:
                        beside_last(b)
            for kt in range(N_KT - LAG - 1, N_KT):
                for gr in groups_ending(kt):
                    weighed(gr)

            def h_mean(k):
                c0 = HT * (k % 2)
                mean(c0, c0 + HT, DM, sq_base(k) + HT)

            def h_inverse(k):
                c0 = HT * (k % 2)
                inverse(ms_base(k) + 2, c0, c0 + HT, sq_base(k) + HT + 1)

            def h_norm(hf, t):
                if t >= 2:
                    dve.wait_ge(tr, tr_h(hf) + 2 * (t - 1))
                c = HT * hf + t
                dve.scalar_tensor_tensor(nrm[:, t % 2, :], res[hf][:, t, :], inv[:, c:c + 1], g2[:, :],
                                         ALU.mult, ALU.mult).then_inc(s_n, 1)

            def h_lo(hf, t):
                for b in range(2):
                    dve.wait_ge(tr_hi, tr_h(hf) + 2 * t + b + 1)
                    sl = (slice(None), slice(4 * b, 4 * b + 4), slice(P * t, P * (t + 1)))
                    dve.tensor_tensor(vlo[sl], psum[:, 2 * (t % 2) + b, :].rearrange("p (k m) -> p k m", m=P),
                                      raw(vhi[sl]), ALU.subtract).then_inc(tr_lo, 1)

            def add_y(n, par, dst):
                dve.wait_ge(y_tr, n + 1)
                dve.tensor_tensor(dst, dst, psum[:, 6 + par, :].rearrange("p (t m) -> p t m", t=HT), ALU.add)\
                    .then_inc(y_add, 1)

            def add_col(n):
                c = P * (n % KD)
                hf = n // KD % HALVES
                add_y(n, n % 2, res[hf][:, :, c:c + P])

            def final(hf, t):
                c = HT * hf + t
                dve.scalar_tensor_tensor(res[hf][:, t, :], res[hf][:, t, :], inv[:, c:c + 1], gf[:, :],
                                         ALU.mult, ALU.mult).then_inc(fin, 1)

            mean(NT - 1, NT, NH * HD, NT + 1)
            inverse(4, NT - 1, NT, NT + 2)
            for t in range(HT, HT + 2):
                nsa_norm(t)
            dve.wait_ge(res_in[0], 32)
            for n in range(2, N_OUT):
                if n == KD + 2:
                    dve.wait_ge(res_in[1], 16 * HT)
                add_col(n - 2)
                if n == 2:
                    conv_mean(1)
                if n == 3:
                    conv_inverse(1)
                if n in (3, 4):
                    for c in (2 * n - 6, 2 * n - 5):
                        conv_norm(1, c)
                if n < 2 + HT:
                    nsa_lo(n + 2)
                    if n + 4 < NT:
                        nsa_norm(n + 4)
                if n == KD + 3:
                    h_mean(0)
                if n == KD + 4:
                    h_inverse(0)
                    dve.wait_ge(g2_in, 32)
                    for t in range(2):
                        h_norm(0, t)
                if n == N_OUT - 2:
                    for t in range(2):
                        h_lo(0, t)
                        h_norm(0, 2 + t)
            for t in range(2, HT):
                h_lo(0, t)
            for n in range(N_OUT - 2, N_OUT):
                add_col(n)

            for hf in range(HALVES):
                f0, w0 = FT * hf, w_of(hf, "glu")

                def glu_of(f, par):
                    dve.wait_ge(sil, f + (f0 + 1))
                    dve.wait_ge(w_used, f * 2 + (w0 + 2))
                    dve.tensor_tensor(silu[:, par, :], silu[:, par, :], psum[:, 2 * par + 1, :], ALU.mult)\
                        .then_inc(glu, 1)
                    dve.wait_ge(g_hi, f + (f0 + 1))
                    dve.tensor_tensor(hlo[:, ds(f, 1), :], silu[:, par:par + 1, :], raw(hhi[:, ds(f, 1), :]),
                                      ALU.subtract).then_inc(g_lo, 1)

                if hf:
                    h_mean(2)
                    glu_of(0, 0)
                    h_inverse(2)
                    for t in range(HT):
                        final(0, t)
                    glu_of(1, 1)
                with dve.Fori(hf, FT // 2) as ff:
                    for e in range(2):
                        glu_of(ff * 2 + e, e)

                y0 = N_OUT + KD * hf
                with dve.Fori(0, KD // 2 - 2) as mm:
                    for d in range(2):
                        add_y(mm * 2 + (y0 + d), d, res[hf][:, :, ds(mm * (2 * P) + P * d, P)])
                if hf == 0:
                    h_mean(1)
                    h_inverse(1)
                    for t in range(2):
                        h_norm(1, t)
                    add_col(y0 + KD - 4)
                    for t in range(2):
                        h_lo(1, t)
                        h_norm(1, t + 2)
                    for n in range(y0 + KD - 3, y0 + KD - 1):
                        add_col(n)
                    for t in range(2, HT):
                        h_lo(1, t)
                    add_col(y0 + KD - 1)
                else:
                    for n in range(y0 + KD - 4, y0 + KD):
                        add_col(n)
            dve.wait_ge(s_sq, sq_base(3) + 2 * HT)
            did(dve.tensor_tensor(ssq[:, HT:NT], ssq[:, HT:NT], rms[:, HT:NT], ALU.add))
            settle()
            mean(HT, NT, DM, sq_base(3) + 2 * HT)
            inverse(ms_base(3) + 2, HT, NT, sq_base(3) + 2 * HT + 1)
            for t in range(HT - 1):
                final(1, t)


CONSTS_FIRST = 2 + 1 + 2
CONSTS_ALL = CONSTS_FIRST + 3
VECS = 16 * (1 + 3 + 2 * 3)


TR_NSA = 2 * NT


def sq_base(k):
    return NT + 2 + (HT + 1) * k


def ms_base(k):
    return 4 + 2 * k


def tr_h(hf):
    return TR_NSA + NT + 2 * HT * hf


_INS = ["x", "norm1_g", "w_in", "conv_w", "k_cmp_pos", "k_cmp_w1", "k_cmp_w2", "v_cmp_pos", "v_cmp_w1",
        "v_cmp_w2", "gn_conv_g", "gn_nsa_g", "w_out", "norm2_g", "w_gate", "w_up", "w_down", "norm_f_g"]


def kernel(**inputs):
    import numpy as np
    import concourse.bacc as bacc
    from concourse.bass_utils import run_bass_kernel_spmd

    nc = bacc.Bacc("TRN2", target_bir_lowering=False, num_devices=1)
    arrays, args = {}, []
    for name in _INS:
        a = np.ascontiguousarray(inputs[name])
        arrays[f"in_{name}"] = a
        args.append(nc.dram_tensor(f"in_{name}", a.shape, mybir.dt.from_np(a.dtype), kind="ExternalInput").ap())
    args.append(nc.dram_tensor("out_h", (1, SEQ, DM), mybir.dt.float32, kind="ExternalOutput").ap())
    hymba_block(nc, *args)
    r = run_bass_kernel_spmd(nc, [arrays], core_ids=[0])
    return r.results[0]["out_h"]
```
